# Optimizing a Trainium2 kernel written in Bass

```python
import jax, jax.numpy as jnp
from jax import lax
import numpy as np

D_MODEL = 1024
BATCH = 1
SEQ = 1024
DEPTH = 1

GRID_W = 64
CTX_LEN = 256
HEAD_DIM = 64
N_HEADS_TOTAL = D_MODEL // HEAD_DIM
ATT_HEADS = N_HEADS_TOTAL // 2
ATT_KV_HEADS = ATT_HEADS // 4
WINDOW = 128
BLOCK = 128
ROPE_BASE = 10000.0
GLA_HEADS = N_HEADS_TOTAL - ATT_HEADS
GLA_DV = HEAD_DIM
GLA_DK = HEAD_DIM // 2
GLA_CHUNK = 64
GATE_RANK = 16
GATE_TAU = 16.0
MIX_WIDTH = ATT_HEADS * HEAD_DIM + GLA_HEADS * GLA_DV
FFN_HIDDEN = -(-8 * D_MODEL // (3 * 256)) * 256
SPLIT_SIZES = (ATT_HEADS * HEAD_DIM, ATT_KV_HEADS * HEAD_DIM, ATT_KV_HEADS * HEAD_DIM,
               GLA_HEADS * GLA_DK, GLA_HEADS * GLA_DK, GLA_HEADS * GLA_DV, GLA_HEADS * GLA_DV,
               GATE_RANK, GATE_RANK)
IN_COLS = sum(SPLIT_SIZES)
NEG_INF = -1e30

kernel_name = 'hybrid_window_gqa_gla_dit_block'

def rmsnorm(x, gain, eps=1e-6):
    x32 = x.astype(jnp.float32)
    y = x32 * lax.rsqrt(jnp.mean(x32 * x32, axis=-1, keepdims=True) + eps)
    return y.astype(x.dtype) * gain

def modulate(h, shift, scale):
    return h * (1.0 + scale) + shift

def heads(t, n):
    return t.reshape(t.shape[:-1] + (n, t.shape[-1] // n))

def flip(t):
    return jnp.flip(t, axis=1)

def split_columns(p):
    idx = np.cumsum(SPLIT_SIZES)[:-1].tolist()
    return jnp.split(p, idx, axis=-1)

def axial_rope_tables(n_tokens):
    ROWS = n_tokens // GRID_W
    row = jnp.repeat(jnp.arange(ROWS), GRID_W).astype(jnp.float32)
    col = jnp.tile(jnp.arange(GRID_W), ROWS).astype(jnp.float32)
    half = HEAD_DIM // 2
    inv_freq = ROPE_BASE ** (-jnp.arange(0, half, 2, dtype=jnp.float32) / half)
    ang_r = row[:, None] * inv_freq[None, :]
    ang_c = col[:, None] * inv_freq[None, :]
    ang = jnp.concatenate([ang_r, ang_r, ang_c, ang_c], axis=-1)
    return jnp.cos(ang), jnp.sin(ang)

def apply_rope(x, cos, sin):
    shp = x.shape
    xr = x.reshape(shp[:-1] + (2, 2, HEAD_DIM // 4))
    rot = jnp.concatenate([-xr[..., 1:2, :], xr[..., 0:1, :]], axis=-2).reshape(shp)
    return x * cos[:, None, :].astype(x.dtype) + rot * sin[:, None, :].astype(x.dtype)

def softmax_with_sink(logits, sink):
    sink_col = jnp.broadcast_to(sink, logits.shape[:-1] + (1,))
    p = jax.nn.softmax(jnp.concatenate([logits, sink_col], axis=-1), axis=-1)
    return p[..., :-1]

def window_attention(q, k, v, k_ctx, v_ctx, sink):
    B, S, H, dh = q.shape
    G = H // ATT_KV_HEADS
    nb = S // BLOCK
    scale = dh ** -0.5
    qb = q.reshape(B, nb, BLOCK, ATT_KV_HEADS, G, dh)
    pad = ((0, 0), (BLOCK, BLOCK), (0, 0), (0, 0))
    kp = jnp.pad(k, pad).reshape(B, nb + 2, BLOCK, ATT_KV_HEADS, dh)
    vp = jnp.pad(v, pad).reshape(B, nb + 2, BLOCK, ATT_KV_HEADS, dh)
    kw = jnp.concatenate([kp[:, :-2], kp[:, 1:-1], kp[:, 2:]], axis=2)
    vw = jnp.concatenate([vp[:, :-2], vp[:, 1:-1], vp[:, 2:]], axis=2)
    s_win = jnp.einsum('bnqhgd,bnkhd->bhgnqk', qb, kw).astype(jnp.float32) * scale
    qpos = jnp.arange(nb)[:, None] * BLOCK + jnp.arange(BLOCK)[None, :]
    kpos = (jnp.arange(nb)[:, None] - 1) * BLOCK + jnp.arange(3 * BLOCK)[None, :]
    rel = kpos[:, None, :] - qpos[:, :, None]
    mask = (jnp.abs(rel) <= WINDOW) & (kpos[:, None, :] >= 0) & (kpos[:, None, :] < S)
    s_win = jnp.where(mask, s_win, NEG_INF)
    s_ctx = jnp.einsum('bnqhgd,bchd->bhgnqc', qb, k_ctx).astype(jnp.float32) * scale
    sink_b = sink.astype(jnp.float32).reshape(ATT_KV_HEADS, G)[None, :, :, None, None, None]
    p = softmax_with_sink(jnp.concatenate([s_win, s_ctx], axis=-1), sink_b).astype(v.dtype)
    n_win = 3 * BLOCK
    o = (jnp.einsum('bhgnqk,bnkhd->bnqhgd', p[..., :n_win], vw)
         + jnp.einsum('bhgnqc,bchd->bnqhgd', p[..., n_win:], v_ctx))
    return o.reshape(B, S, H * dh)

def context_attention(q, k, v, sink):
    B, C, H, dh = q.shape
    G = H // ATT_KV_HEADS
    qg = q.reshape(B, C, ATT_KV_HEADS, G, dh)
    s = jnp.einsum('bqhgd,bkhd->bhgqk', qg, k).astype(jnp.float32) * dh ** -0.5
    sink_b = sink.astype(jnp.float32).reshape(ATT_KV_HEADS, G)[None, :, :, None, None]
    p = softmax_with_sink(s, sink_b).astype(v.dtype)
    return jnp.einsum('bhgqk,bkhd->bqhgd', p, v).reshape(B, C, H * dh)

def log_decay(z, w_gate, b_gate):
    logits = (z @ w_gate + b_gate).astype(jnp.float32)
    return heads(jax.nn.log_sigmoid(logits) / GATE_TAU, GLA_HEADS)

def gla_chunked(q, k, v, log_a, s0):
    B, T, H, DK = q.shape
    DV = v.shape[-1]
    n = T // GLA_CHUNK
    f32 = jnp.float32
    qc = q.astype(f32).reshape(B, n, GLA_CHUNK, H, DK)
    kc = k.astype(f32).reshape(B, n, GLA_CHUNK, H, DK)
    vc = v.astype(f32).reshape(B, n, GLA_CHUNK, H, DV)
    b = jnp.cumsum(log_a.astype(f32).reshape(B, n, GLA_CHUNK, H, DK), axis=2)
    b_last = b[:, :, -1:]
    q_dec = qc * jnp.exp(b)
    k_inv = kc * jnp.exp(-b)
    lower = jnp.tril(jnp.ones((GLA_CHUNK, GLA_CHUNK), dtype=bool))
    A = jnp.where(lower, jnp.einsum('bnihk,bnjhk->bnhij', q_dec, k_inv), 0.0)
    intra = jnp.einsum('bnhij,bnjhv->bnihv', A, vc)
    dS = jnp.einsum('bnjhk,bnjhv->bnhkv', kc * jnp.exp(b_last - b), vc)
    decay = jnp.exp(b_last[:, :, 0])

    def step(state, inp):
        d, ds = inp
        return d[..., None] * state + ds, state

    s_final, s_before = lax.scan(step, s0, (jnp.moveaxis(decay, 1, 0), jnp.moveaxis(dS, 1, 0)))
    inter = jnp.einsum('bnihk,nbhkv->bnihv', q_dec, s_before)
    o = (intra + inter).reshape(B, T, H, DV).astype(v.dtype)
    return o, s_final

def gla_final_state(k, v, log_a):
    b = jnp.cumsum(log_a.astype(jnp.float32), axis=1)
    w = jnp.exp(b[:, -1:] - b)
    return jnp.einsum('bthk,bthv->bhkv', k.astype(jnp.float32) * w, v.astype(jnp.float32))

def gla_output(o, gate, g_norm):
    return rmsnorm(o, g_norm).reshape(gate.shape) * jax.nn.silu(gate)

def swiglu(h, w_in, w_out):
    g, u = jnp.split(h @ w_in, 2, axis=-1)
    return (jax.nn.silu(g) * u) @ w_out

def setup_inputs(seed: int = 0) -> dict:
    key = jax.random.key(seed)
    ks = jax.random.split(key, 24)
    L, D = DEPTH, D_MODEL
    nrm = jax.random.normal
    f32 = jnp.float32
    return {
        'x': nrm(ks[0], (BATCH, SEQ, D), f32),
        'c': nrm(ks[1], (BATCH, D), f32),
        'ctx': nrm(ks[2], (BATCH, CTX_LEN, D), f32),
        'c_ctx': nrm(ks[3], (D,), f32),
        'w_ada': nrm(ks[4], (L, D, 6 * D), f32) * (0.5 * D ** -0.5),
        'b_ada': nrm(ks[5], (L, 6 * D), f32) * 0.02,
        'g_pre_mix': 1.0 + 0.05 * nrm(ks[6], (L, D), f32),
        'g_post_mix': 1.0 + 0.05 * nrm(ks[7], (L, D), f32),
        'g_pre_ffn': 1.0 + 0.05 * nrm(ks[8], (L, D), f32),
        'g_post_ffn': 1.0 + 0.05 * nrm(ks[9], (L, D), f32),
        'w_in': nrm(ks[10], (L, D, IN_COLS), f32) * D ** -0.5,
        'attn_sink': 0.5 * nrm(ks[11], (L, ATT_HEADS), f32),
        'w_gate_fwd': nrm(ks[12], (L, GATE_RANK, GLA_HEADS * GLA_DK), f32) * GATE_RANK ** -0.5,
        'b_gate_fwd': 0.5 * nrm(ks[13], (L, GLA_HEADS * GLA_DK), f32),
        'w_gate_bwd': nrm(ks[14], (L, GATE_RANK, GLA_HEADS * GLA_DK), f32) * GATE_RANK ** -0.5,
        'b_gate_bwd': 0.5 * nrm(ks[15], (L, GLA_HEADS * GLA_DK), f32),
        'g_gla_norm': 1.0 + 0.05 * nrm(ks[16], (L, GLA_DV), f32),
        'w_out': nrm(ks[17], (L, MIX_WIDTH, D), f32) * MIX_WIDTH ** -0.5,
        'w_ffn_in': nrm(ks[18], (L, D, 2 * FFN_HIDDEN), f32) * D ** -0.5,
        'w_ffn_out': nrm(ks[19], (L, FFN_HIDDEN, D), f32) * FFN_HIDDEN ** -0.5,
    }

def reference(x, c, ctx, c_ctx, w_ada, b_ada, g_pre_mix, g_post_mix, g_pre_ffn, g_post_ffn,
              w_in, attn_sink, w_gate_fwd, b_gate_fwd, w_gate_bwd, b_gate_bwd, g_gla_norm,
              w_out, w_ffn_in, w_ffn_out):
    B, S, _ = x.shape
    cos, sin = axial_rope_tables(S)
    zero_state = jnp.zeros((B, GLA_HEADS, GLA_DK, GLA_DV), jnp.float32)
    for l in range(DEPTH):
        need_ctx_out = l < DEPTH - 1
        ada = jax.nn.silu(c) @ w_ada[l] + b_ada[l]
        ada_c = jax.nn.silu(c_ctx) @ w_ada[l] + b_ada[l]
        sh1, sc1, gt1, sh2, sc2, gt2 = jnp.split(ada[:, None, :], 6, axis=-1)
        sh1c, sc1c, gt1c, sh2c, sc2c, gt2c = jnp.split(ada_c, 6, axis=-1)

        h = modulate(rmsnorm(x, g_pre_mix[l]), sh1, sc1)
        hc = modulate(rmsnorm(ctx, g_pre_mix[l]), sh1c, sc1c)
        q, k, v, gq, gk, gv, gg, zf, zb = split_columns(h @ w_in[l])
        qc, kc, vc, gqc, gkc, gvc, ggc, zfc, zbc = split_columns(hc @ w_in[l])

        q_h = apply_rope(heads(q, ATT_HEADS), cos, sin)
        k_h = apply_rope(heads(k, ATT_KV_HEADS), cos, sin)
        v_h = heads(v, ATT_KV_HEADS)
        kc_h = heads(kc, ATT_KV_HEADS)
        vc_h = heads(vc, ATT_KV_HEADS)
        attn_lat = window_attention(q_h, k_h, v_h, kc_h, vc_h, attn_sink[l])

        gkc_h = heads(gkc, GLA_HEADS)
        gvc_h = heads(gvc, GLA_HEADS)
        la_fc = log_decay(zfc, w_gate_fwd[l], b_gate_fwd[l])
        la_bc = log_decay(zbc, w_gate_bwd[l], b_gate_bwd[l])
        if need_ctx_out:
            gqc_h = heads(gqc, GLA_HEADS) * GLA_DK ** -0.5
            oc_f, s_f = gla_chunked(gqc_h, gkc_h, gvc_h, la_fc, zero_state)
            oc_b, s_b = gla_chunked(flip(gqc_h), flip(gkc_h), flip(gvc_h), flip(la_bc), zero_state)
            gla_ctx = gla_output(oc_f + flip(oc_b), ggc, g_gla_norm[l])
            attn_ctx = context_attention(heads(qc, ATT_HEADS), kc_h, vc_h, attn_sink[l])
        else:
            s_f = gla_final_state(gkc_h, gvc_h, la_fc)
            s_b = gla_final_state(flip(gkc_h), flip(gvc_h), flip(la_bc))

        gq_h = heads(gq, GLA_HEADS) * GLA_DK ** -0.5
        gk_h = heads(gk, GLA_HEADS)
        gv_h = heads(gv, GLA_HEADS)
        la_f = log_decay(zf, w_gate_fwd[l], b_gate_fwd[l])
        la_b = log_decay(zb, w_gate_bwd[l], b_gate_bwd[l])
        o_f, _ = gla_chunked(gq_h, gk_h, gv_h, la_f, s_f)
        o_b, _ = gla_chunked(flip(gq_h), flip(gk_h), flip(gv_h), flip(la_b), s_b)
        gla_lat = gla_output(o_f + flip(o_b), gg, g_gla_norm[l])

        y = jnp.concatenate([attn_lat, gla_lat], axis=-1) @ w_out[l]
        x = x + gt1 * rmsnorm(y, g_post_mix[l])

        f = swiglu(modulate(rmsnorm(x, g_pre_ffn[l]), sh2, sc2), w_ffn_in[l], w_ffn_out[l])
        x = x + gt2 * rmsnorm(f, g_post_ffn[l])

        if need_ctx_out:
            yc = jnp.concatenate([attn_ctx, gla_ctx], axis=-1) @ w_out[l]
            ctx = ctx + gt1c * rmsnorm(yc, g_post_mix[l])
            fc = swiglu(modulate(rmsnorm(ctx, g_pre_ffn[l]), sh2c, sc2c), w_ffn_in[l], w_ffn_out[l])
            ctx = ctx + gt2c * rmsnorm(fc, g_post_ffn[l])
    return x


_drawn_inputs = setup_inputs


def setup_inputs(seed=0):
    import zlib

    import numpy as np

    out = dict(_drawn_inputs(seed))
    spreads = {}
    factors = {'g_post_mix': 3.731,
     'g_pre_ffn': 2.997,
     'g_post_ffn': 3.777,
     'attn_sink': 31.641,
     'g_gla_norm': 3.282}
    for name, (base, spread) in spreads.items():
        noise = np.random.default_rng([zlib.crc32(name.encode()), seed]).standard_normal(out[name].shape)
        drawn = base * np.exp(spread * noise) if base else spread * noise
        out[name] = __import__('jax').numpy.asarray(drawn.astype(out[name].dtype))
    for name, factor in factors.items():
        out[name] = (out[name] * factor).astype(out[name].dtype)
    return out
```

```python
from contextlib import ExitStack

import numpy as np

import concourse.bass as bass
from concourse import mybir

ALU = mybir.AluOpType
ACT = mybir.ActivationFunctionType
F32 = mybir.dt.float32
F32R = mybir.dt.float32r
BF16 = mybir.dt.bfloat16
AX = mybir.AxisListType

P = 128
D = 1024
KT = D // P
SEQ = 1024
CTX = 256
TOK = SEQ + CTX
LT = SEQ // P
TT = TOK // P
HEAD = 64
AH, KVH = 8, 2
GH, DK = 8, 32
CHUNK = 64
NCH = SEQ // CHUNK
RANK = 16
TAU = 16.0
GRID_W = 64
ROPE_BASE = 10000.0
HID = 2816
HT = HID // P
EPS = 1e-6
NEG = -1e30
SCRATCH = "Internal"

GK, KK, VV, GV, GG2, ZZ, QQ, GQ, GG1 = 0, 256, 384, 512, 1024, 1280, 1312, 1824, 2080
COLS = 2336
W_Q, W_K, W_GQ, W_GK, W_GV, W_GG, W_Z = 0, 512, 768, 1024, 1280, 1792, 2304
CHUNKS = [[W_GK, W_K], [W_GV, W_GV + 256], [COLS - 512, COLS - 256], [W_Q, W_Q + 256], [W_GQ, W_GG]]
NARROW = COLS - (W_GG + 256)

C_ID, C_ONE, C_PREF_F, C_PREF_B, C_SUF_F, C_SUF_B, C_CTX_F, C_CTX_B, C_ALL, C_PREV, C_NEXT, C_IND = [P * n for n in range(12)]
C_HEAD = C_IND + 2
C_COLS = C_HEAD + 4


def constants():
    j, i = np.arange(P)[:, None], np.arange(P)[None, :]
    same = (j // CHUNK) == (i // CHUNK)
    c = np.zeros((P, C_COLS), np.float32)
    inv = 1.0 / TAU
    c[:, C_ID:C_ID + P] = j == i
    c[:, C_ONE:C_ONE + P] = 1.0
    c[:, C_PREF_F:C_PREF_F + P] = ((j <= i) & same) * inv
    c[:, C_PREF_B:C_PREF_B + P] = ((j >= i) & same) * inv
    c[:, C_SUF_F:C_SUF_F + P] = ((j > i) & same) * inv
    c[:, C_SUF_B:C_SUF_B + P] = ((j < i) & same) * inv
    c[:, C_CTX_F:C_CTX_F + P] = (j > i) * inv
    c[:, C_CTX_B:C_CTX_B + P] = (j < i) * inv
    c[:, C_ALL:C_ALL + P] = inv
    c[:, C_PREV:C_PREV + P] = np.where(i >= j, 0.0, NEG)
    c[:, C_NEXT:C_NEXT + P] = np.where(i <= j, 0.0, NEG)
    c[:, C_IND] = (np.arange(P) < CHUNK) * inv
    c[:, C_IND + 1] = (np.arange(P) >= CHUNK) * inv
    c[:, C_HEAD:C_COLS] = (np.arange(P) // DK)[:, None] == np.arange(4)
    tok = np.arange(SEQ)
    half = HEAD // 2
    freq = (np.float32(ROPE_BASE) ** (-np.arange(0, half, 2, dtype=np.float32) / np.float32(half))).astype(np.float32)
    ar = (tok // GRID_W).astype(np.float32)[:, None] * freq
    ac = (tok % GRID_W).astype(np.float32)[:, None] * freq
    cos = np.ones((TOK, HEAD), np.float32)
    sin = np.zeros((TOK, HEAD), np.float32)
    cos[:SEQ] = np.cos(np.concatenate([ar, ar, ac, ac], 1))
    sin[:SEQ] = np.sin(np.concatenate([-ar, ar, -ac, ac], 1))
    tile = lambda a: np.ascontiguousarray(a.reshape(TT, P, HEAD).transpose(1, 0, 2).reshape(P, TT * HEAD))
    return c, tile(cos), tile(sin)


class Event:

    def __init__(self, nc, ctx, name, per=1, dma=False, credit=None):
        self.sem = ctx.enter_context(nc.semaphore(name))
        self.per = per * (16 if dma else 1)
        self.one = 16 if dma else 1
        self.credit = credit if credit is not None else 0 if dma else 2

    def open(self, eng):
        eng.sem_inc(self.sem, self.credit * self.per)

    def at(self, t, k=None):
        return (t + self.credit) * self.per + (self.per if k is None else k * self.one)


def build(nc, xall, c, c_ctx, w_ada, b_ada, g_pre_mix, g_post_mix, g_pre_ffn, g_post_ffn, w_in, attn_sink,
          w_gate_fwd, b_gate_fwd, w_gate_bwd, b_gate_bwd, g_gla, w_out, w_ffn_in, w_ffn_out, consts, cosd, sind, out,
          proj, mixd, x2d):
    top = ExitStack()
    with top:
        persist(nc, top, locals())


def persist(nc, top, A):
    def sb(stack, name, shape, dt=F32):
        return stack.enter_context(nc.sbuf_tensor(name, shape, dt))

    S = dict(A)
    S["sb"] = sb
    S["con"] = sb(top, "con", [P, C_COLS])
    S["pcol"] = sb(top, "pcol", [P, 80])
    S["A1"] = sb(top, "A1", [P, KT, 2])
    S["B1"] = sb(top, "B1", [P, 16, 2])
    S["A2"] = sb(top, "A2", [P, KT])
    S["B2"] = sb(top, "B2", [P, 16])
    S["G1"] = sb(top, "G1", [P, D])
    S["G2"] = sb(top, "G2", [P, D])
    S["epsb"] = sb(top, "epsb", [P, 1])
    S["scol"] = sb(top, "scol", [P, 16])
    with ExitStack() as s:
        S["hTh"] = sb(s, "hTh", [P, KT, TOK], F32R)
        S["hTl"] = sb(s, "hTl", [P, KT, TOK], F32R)
        modulate_block(nc, S)
        project_block(nc, S)
    with ExitStack() as s:
        S["cos"] = sb(s, "cos", [P, TT, HEAD])
        S["sin"] = sb(s, "sin", [P, TT, HEAD])
        S["keyT"] = sb(s, "keyT", [P, 2, KVH, (TT + 1) * P], F32R)
        S["val"] = sb(s, "val", [P, TT + 1, P])
        S["la"] = sb(s, "la", [P, TT, 512])
        S["state"] = sb(s, "state", [P, 4, TOK // CHUNK, HEAD])
        S["fin"] = sb(s, "fin", [P, 4, HEAD])
        keys_block(nc, S)
        mix_block(nc, S)
    with ExitStack() as s:
        S["h2h"] = sb(s, "h2h", [P, KT, SEQ], F32R)
        S["h2l"] = sb(s, "h2l", [P, KT, SEQ], F32R)
        output_block(nc, S)
        ffn_block(nc, S)


def modulate_block(nc, S):
    sb, con, pcol, A1, B1, scol, epsb = (S[n] for n in ("sb", "con", "pcol", "A1", "B1", "scol", "epsb"))
    hTh, hTl = S["hTh"], S["hTl"]
    with ExitStack() as s:
        def sem(name):
            return s.enter_context(nc.semaphore("m_" + name))
        prow = sb(s, "prow", [80, P])
        wada = sb(s, "wada", [P, 3, 2 * D])
        xin = sb(s, "xin", [P, 2, D])
        junk = sb(s, "junk", [P, D])
        ssq = sb(s, "ssq", [P, 2, 1])
        rst = sb(s, "rst", [P, 2, 1])
        xnT = sb(s, "xnT", [P, KT, TOK])
        modrow = sb(s, "modrow", [2, 2 * D])
        psA = s.enter_context(nc.psum_tensor("psA", [P, 4, 512], F32))
        psX = s.enter_context(nc.psum_tensor("psX", [P, 4, 512], F32))
        rows_in, con_in, ada_in = sem("rows_in"), sem("con_in"), [sem(f"ada_in{n}") for n in range(3)]
        rows_turned, cols_ready, silu_ready = sem("rows_turned"), sem("cols_ready"), sem("silu_ready")
        ada_used, mod_sum, mod_row, mod_turned, mod_col = sem("ada_used"), sem("mod_sum"), sem("mod_row"), sem("mod_turned"), sem("mod_col")
        full, hi, lo = sem("full"), sem("hi"), sem("lo")
        x_in = [Event(nc, s, f"m_x_in{u}", dma=True) for u in range(2)]
        squares, root = Event(nc, s, "m_squares"), Event(nc, s, "m_root")
        rstd, normed = Event(nc, s, "m_rstd"), Event(nc, s, "m_normed")
        turned, turned_out = Event(nc, s, "m_turned"), Event(nc, s, "m_turned_out")
        eps_set = sem("eps_set")
        block = s.enter_context(nc.Block())

        @block.sync
        def _(sp):
            rows = [(S["c"], 0, 8), (S["c_ctx"], 8, 8), (S["g_pre_mix"], 16, 8), (S["g_pre_ffn"], 24, 8), (S["b_ada"], 32, 48)]
            for src, r, n in rows:
                sp.dma_start(prow[r:r + n, :], src.rearrange("(r p) -> r p", p=P)).then_inc(rows_in, 16)
            sp.dma_start(con[:, :], S["consts"]).then_inc(con_in, 16)
            for k in range(KT):
                if k >= 3:
                    sp.wait_ge(ada_used, k - 2)
                sp.dma_start(wada[:, k % 3, :], S["w_ada"][k * P:(k + 1) * P, 0:2 * D]).then_inc(ada_in[k % 3], 16)

        @block.gpsimd
        def _(pool):
            with pool.Fori(0, TT // 2) as i:
                for u in range(2):
                    t = i * 2 + u
                    pool.wait_ge(turned.sem, turned.at(t - 2))
                    pool.dma_start(xin[:, u, :], S["xall"][bass.ds(t * P, P), :]).then_inc(x_in[u].sem, 16)

        @block.scalar
        def _(act):
            squares.open(act)
            root.open(act)
            act.wait_ge(eps_set, 1)
            with act.Fori(0, TT // 2) as i:
                for u in range(2):
                    t = i * 2 + u
                    act.wait_ge(x_in[u].sem, x_in[u].at(i))
                    act.wait_ge(squares.sem, squares.at(t - 1))
                    act.wait_ge(root.sem, root.at(t - 2))
                    act.activation(junk[:, :], xin[:, u, :], ACT.Square, accum_out=ssq[:, u, :]).then_inc(squares.sem, 1)
                    act.wait_ge(squares.sem, squares.at(t))
                    act.wait_ge(rstd.sem, rstd.at(t - 2))
                    act.activation(rst[:, u, :], ssq[:, u, :], ACT.Sqrt, scale=1.0 / D, bias=epsb[:, :]).then_inc(root.sem, 1)
            act.wait_ge(cols_ready, 1)
            act.activation(scol[:, :], pcol[:, 0:16], ACT.Silu).then_inc(silu_ready, 1)
            for k in range(KT):
                act.wait_ge(full, k + 1)
                act.activation(hTh[:, k, :], xnT[:, k, :], ACT.Copy).then_inc(hi, 1)

        @block.tensor
        def _(pe):
            turned.open(pe)
            pe.wait_ge(rows_in, 80)
            pe.wait_ge(con_in, 16)
            pe.transpose(psA[:, 0, 0:80], prow[:, :], con[0:80, C_ID:C_ID + 80]).then_inc(rows_turned, 1)
            with pe.Fori(0, TT // 2) as i:
                for u in range(2):
                    t = i * 2 + u
                    pe.wait_ge(normed.sem, normed.at(t))
                    pe.wait_ge(turned_out.sem, turned_out.at(t - 2))
                    for k in range(KT):
                        mm = pe.transpose(psX[:, 2 * u + k // 4, (k % 4) * P:(k % 4 + 1) * P], xin[:, u, k * P:(k + 1) * P],
                                          con[:, C_ID:C_ID + P])
                    mm.then_inc(turned.sem, 1)
            pe.wait_ge(silu_ready, 1)
            lhs = scol[:, :].rearrange("p (w k) -> p k w", w=2)
            for k in range(KT):
                pe.wait_ge(ada_in[k % 3], 16 * (k // 3 + 1))
                for n in range(4):
                    mm = pe.matmul(psA[0:2, n, :], lhs[:, k, :], wada[:, k % 3, n * 512:(n + 1) * 512],
                                   start=(k == 0), stop=(k == KT - 1))
                mm.then_inc(ada_used, 1)
            pe.wait_ge(mod_row, 1)
            for n in range(16):
                mm = pe.transpose(psA[:, 0, 2 * n:2 * n + 2], modrow[:, n * P:(n + 1) * P], con[0:2, C_ID:C_ID + 2])
            mm.then_inc(mod_turned, 1)

        @block.vector
        def _(dve):
            dve.memset(epsb[:, :], EPS).then_inc(eps_set, 1)
            for e in (rstd, normed, turned_out):
                e.open(dve)
            dve.wait_ge(rows_turned, 1)
            dve.tensor_copy(pcol[:, :], psA[:, 0, 0:80]).then_inc(cols_ready, 1)

            with dve.Fori(0, TT // 2) as i:
                for u in range(2):
                    t = i * 2 + u
                    dve.wait_ge(root.sem, root.at(t))
                    dve.reciprocal(rst[:, u, :], rst[:, u, :]).then_inc(rstd.sem, 1)
                    dve.wait_ge(rstd.sem, rstd.at(t))
                    dve.tensor_scalar(xin[:, u, :], xin[:, u, :], rst[:, u, :], None, ALU.mult).then_inc(normed.sem, 1)
                    dve.wait_ge(turned.sem, turned.at(t))
                    dve.tensor_copy(xnT[:, :, bass.ds(t * P, P)],
                                    psX[:, 2 * u:2 * u + 2, :].rearrange("p b (k j) -> p (b k) j", j=P)).then_inc(turned_out.sem, 1)
            dve.wait_ge(ada_used, KT)
            dve.tensor_copy(modrow[:, :], psA[0:2, :, :].rearrange("p b n -> p (b n)")).then_inc(mod_row, 1)
            dve.wait_ge(mod_turned, 1)
            dve.tensor_tensor(B1[:, :, :], psA[:, 0, 0:32].rearrange("p (n w) -> p n w", w=2),
                              pcol[:, 32:48].unsqueeze(2).broadcast_to([P, 16, 2]), ALU.add).then_inc(mod_col, 1)
            dve.wait_ge(mod_col, 1)
            dve.scalar_tensor_tensor(A1[:, :, :], B1[:, 8:16, :], 1.0,
                                     pcol[:, 16:24].unsqueeze(2).broadcast_to([P, 8, 2]), ALU.add, ALU.mult).then_inc(mod_col, 1)
            dve.wait_ge(mod_col, 2)
            dve.wait_ge(turned_out.sem, turned_out.at(TT - 1))

            def low(k):
                dve.wait_ge(hi, k + 1)
                dve.tensor_tensor(hTl[:, k, :], xnT[:, k, :], hTh[:, k, :].bitcast(F32), ALU.subtract).then_inc(lo, 1)
            for k in range(KT):
                dve.tensor_scalar(xnT[:, k, 0:SEQ], xnT[:, k, 0:SEQ], A1[:, k, 0:1], B1[:, k, 0:1], ALU.mult, ALU.add)
                dve.tensor_scalar(xnT[:, k, SEQ:TOK], xnT[:, k, SEQ:TOK], A1[:, k, 1:2], B1[:, k, 1:2], ALU.mult, ALU.add).then_inc(full, 1)
                if k:
                    low(k - 1)
            low(KT - 1)


def project_block(nc, S):
    sb, con, pcol, scol = (S[n] for n in ("sb", "con", "pcol", "scol"))
    hTh, hTl, A2, B2, G1, G2, proj = (S[n] for n in ("hTh", "hTl", "A2", "B2", "G1", "G2", "proj"))
    with ExitStack() as s:
        def sem(name):
            return s.enter_context(nc.semaphore("p_" + name))
        wh = sb(s, "wh", [P, 2, KT, 512], F32R)
        wl = sb(s, "wl", [P, 2, KT, 512], F32R)
        raw = sb(s, "raw", [P, 2, 4, 512])
        acc = sb(s, "acc", [P, 4 * D])
        ada = sb(s, "ada", [P, 2, 2 * D])
        stage = G2[:, :].rearrange("p (s n) -> p s n", s=2)
        psW = s.enter_context(nc.psum_tensor("psW", [P, 2, 512], F32))
        psG = s.enter_context(nc.psum_tensor("psG", [P, 4, 512], F32))
        psC = s.enter_context(nc.psum_tensor("psC", [P, 512], F32))
        raw_in = [sem(f"raw_in{n}") for n in range(2)]
        ada_in = [sem(f"ada_in{n}") for n in range(2)]
        acc_zero, acc_step, rows, gate_sum, cols_done, gates = (sem(n) for n in ("acc_zero", "acc_step", "rows", "gate_sum", "cols_done", "gates"))
        hi, lo = sem("hi"), sem("lo")
        done, copied = Event(nc, s, "p_done"), Event(nc, s, "p_copied")
        stored = [Event(nc, s, f"p_stored{u}", dma=True, credit=1) for u in range(2)]
        block = s.enter_context(nc.Block())
        FIRST = [0, 10, 20, 30, 38]
        END = 46

        def width(ci, t):
            return 512 if not isinstance(ci, int) or ci != 2 else NARROW if t < LT else 2 * RANK

        @block.sync
        def _(sp):
            n_ada = 0

            def ada_piece(n):
                if n >= 2:
                    sp.wait_ge(acc_step, n)
                k, h = n // 2, n % 2
                sp.dma_start(ada[:, n % 2, :], S["w_ada"][k * P:(k + 1) * P, (2 + 2 * h) * D:(4 + 2 * h) * D]).then_inc(ada_in[n % 2], 16)

            for ci, runs in enumerate(CHUNKS):
                for half in range(2):
                    hf = 2 * ci + half
                    if hf >= 2:
                        sp.wait_ge(lo, hf - 1)
                    for n, first in enumerate(runs):
                        sp.dma_start(raw[:, half, :, n * 256:(n + 1) * 256],
                                     S["w_in"].rearrange("(k p) n -> p k n", p=P)[:, 4 * half:4 * half + 4, first:first + 256]
                                     ).then_inc(raw_in[half], 16)
                    if ci >= 1:
                        for _ in range(2):
                            ada_piece(n_ada)
                            n_ada += 1
            assert n_ada == 16
            for n, (col, gain) in enumerate(((2 * D, S["g_post_mix"]), (5 * D, S["g_post_ffn"]))):
                sp.wait_ge(acc_step, 16 + n)
                sp.dma_start(ada[:, n, 0:D], S["b_ada"][col:col + D].partition_broadcast(P)).then_inc(rows, 16)
                sp.dma_start(ada[:, n, D:2 * D], gain.partition_broadcast(P)).then_inc(rows, 16)

        @block.scalar
        def _(act):
            copied.open(act)
            for u in range(2):
                stored[u].open(act)

            def high(ci, half, slot, before):
                act.wait_ge(raw_in[half], ci * 32 + 32)
                act.wait_ge(done.sem, done.at(before - 1))
                act.activation(wh[:, bass.ds(slot, 1), 4 * half:4 * half + 4, :].rearrange("p s k n -> p (s k) n"),
                               raw[:, half, :, :], ACT.Copy).then_inc(hi, 1)

            def chunk(ci, g0, used, tiles, slot, col, nxt=True):
                for t in range(tiles):
                    n = width(ci, t)
                    act.wait_ge(done.sem, done.at(g0 + t))
                    act.wait_ge(stored[t % 2].sem, stored[t % 2].at(used + (t // 2 - 1)))
                    act.activation(stage[:, t % 2, 0:n], psW[:, t % 2, 0:n], ACT.Copy).then_inc(copied.sem, 1)
                    act.wait_ge(copied.sem, copied.at(g0 + t))
                    c0 = ZZ if n == 2 * RANK else col
                    act.dma_start(proj[t * P:(t + 1) * P, bass.ds(c0, n)], stage[:, t % 2, 0:n]).then_inc(stored[t % 2].sem, 16)
                    if nxt and t in (1, 4):
                        high(ci + 1, t // 4, slot, g0)

            high(0, 0, 0, 0)
            high(0, 1, 0, 0)
            with act.Fori(0, 2) as i:
                slot = act.snap(i * -1 + 1)
                chunk(i, i * 10, i * 5, TT, slot, act.snap(i * 512))
            chunk(2, FIRST[2], FIRST[2] // 2, TT, 1, GG2)
            chunk(3, FIRST[3], FIRST[3] // 2, LT, 0, QQ)
            chunk(4, FIRST[4], FIRST[4] // 2, LT, 0, GQ, False)
            for u in range(2):
                act.wait_ge(stored[u].sem, stored[u].at(END // 2 - 1))

        @block.vector
        def _(dve):
            dve.memset(acc[:, :], 0.0).then_inc(acc_step, 1)
            steps = [0]

            def low(ci, half):
                dve.wait_ge(hi, 2 * ci + half + 1)
                dve.tensor_tensor(wl[:, ci % 2, 4 * half:4 * half + 4, :], raw[:, half, :, :],
                                  wh[:, ci % 2, 4 * half:4 * half + 4, :].bitcast(F32), ALU.subtract).then_inc(lo, 1)

            def ada_step():
                n = steps[0]
                k, h = n // 2, n % 2
                dve.wait_ge(ada_in[n % 2], 16 * (n // 2 + 1))
                dve.wait_ge(acc_step, n + 1)
                a = acc[:, h * 2 * D:(h + 1) * 2 * D]
                dve.scalar_tensor_tensor(a, ada[:, n % 2, :], scol[:, k:k + 1], a, ALU.mult, ALU.add).then_inc(acc_step, 1)
                steps[0] += 1

            low(0, 0)
            low(0, 1)
            for ci in range(1, 5):
                for half in range(2):
                    low(ci, half)
                    ada_step()
                    ada_step()
            dve.wait_ge(gate_sum, 1)
            dve.wait_ge(rows, 64)
            for u in range(2):
                dve.wait_ge(stored[u].sem, stored[u].at(END // 2 - 1))
            for n, G in enumerate((G1, G2)):
                dve.tensor_tensor(G[:, :], psG[:, 2 * n:2 * n + 2, :].rearrange("p b n -> p (b n)"), ada[:, n, 0:D], ALU.add).then_inc(gates, 1)
            dve.tensor_tensor(B2[:, :], psC[:, 0:16], pcol[:, 32 + 24:32 + 40], ALU.add).then_inc(gates, 1)
            dve.wait_ge(gates, 3)
            for n, G in enumerate((G1, G2)):
                dve.tensor_tensor(G[:, :], G[:, :], ada[:, n, D:2 * D], ALU.mult)
            dve.scalar_tensor_tensor(A2[:, :], B2[:, 8:16], 1.0, pcol[:, 24:32], ALU.add, ALU.mult)

        @block.tensor
        def _(pe):
            done.open(pe)

            def tile(ci_sem, g, t, w, col, n):
                if t == 0:
                    pe.wait_ge(lo, ci_sem)
                pe.wait_ge(copied.sem, copied.at(g - 2))
                m = 0
                for k in range(KT):
                    for a, b in ((hTh, wh), (hTl, wh), (hTh, wl)):
                        mm = pe.matmul(psW[:, t % 2, 0:n], a[:, k, t * P:(t + 1) * P], b[:, bass.ds(w, 1), k, col:col + n].rearrange("p s n -> p (s n)"),
                                       start=(m == 0), stop=(m == 3 * KT - 1))
                        m += 1
                mm.then_inc(done.sem, 1)

            with pe.Fori(0, 2) as i:
                for t in range(TT):
                    tile(i * 2 + 2, i * 10 + t, t, i, 0, 512)
            for t in range(TT):
                n = NARROW if t < LT else 2 * RANK
                tile(6, FIRST[2] + t, t, 0, 512 - n, n)
            with pe.Fori(0, 2) as i:
                slot = pe.snap(i * -1 + 1)
                for t in range(LT):
                    tile(i * 2 + 8, i * 8 + FIRST[3] + t, t, slot, 0, 512)
            pe.wait_ge(acc_step, 17)
            one = con[:, C_ONE:C_ONE + P]
            for n in range(4):
                col = (0 if n < 2 else 3 * D) + (n % 2) * 512
                pe.matmul(psG[:, n, :], one, acc[:, col:col + 512], start=True, stop=True)
            for n in range(16):
                mm = pe.matmul(psC[:, n:n + 1], acc[:, D + n * P:D + (n + 1) * P], con[:, C_ONE:C_ONE + 1], start=True, stop=True)
            mm.then_inc(gate_sum, 1)


def rope(pool, rotated, t, x, cos, sin, rot, rot2, heads):
    def table(a):
        return a[:, bass.ds(t, 1), :]
    pool.tensor_tensor(rot[:, :, :], x, table(cos).broadcast_to([P, heads, HEAD]), ALU.mult).then_inc(rotated.sem, 1)
    halves = x.rearrange("p h (a b d) -> p h a b d", a=2, b=2)
    out = rot2[:, :, :].rearrange("p h (a b d) -> p h a b d", a=2, b=2)
    signed = table(sin).rearrange("p s (a b d) -> p s a b d", a=2, b=2)
    for b in range(2):
        pool.tensor_tensor(out[:, :, :, b, :], halves[:, :, :, 1 - b, :],
                           signed[:, :, :, b, :].broadcast_to([P, heads, 2, HEAD // 4]), ALU.mult).then_inc(rotated.sem, 1)
    pool.wait_ge(rotated.sem, rotated.at(t, 3))
    pool.tensor_tensor(rot[:, :, :], rot[:, :, :], rot2[:, :, :], ALU.add).then_inc(rotated.sem, 1)


def keys_block(nc, S):
    sb, con, proj = S["sb"], S["con"], S["proj"]
    cos, sin, keyT, val, la, state, fin = (S[n] for n in ("cos", "sin", "keyT", "val", "la", "state", "fin"))
    with ExitStack() as s:
        def sem(name):
            return s.enter_context(nc.semaphore("k_" + name))

        def ev(name, per=1, dma=False):
            return Event(nc, s, "k_" + name, per, dma)
        wg = sb(s, "wg", [33, 512])
        row = sb(s, "krow", [P, 2, D])
        z = sb(s, "z", [P, 2, 2 * RANK])
        zT = sb(s, "zT", [33, 2, P])
        rot = sb(s, "rot", [P, KVH, HEAD])
        rot2 = sb(s, "rot2", [P, KVH, HEAD])
        kdup = sb(s, "kdup", [P, 2, KVH, 2, HEAD], F32R)
        mag = sb(s, "mag", [P, 512])
        lat = sb(s, "lat", [P, 2, 512])
        grow = sb(s, "grow", [P, 2, 512])
        kd = sb(s, "kd", [P, 2, 2, 256])
        dec = sb(s, "dec", [P, 4, TOK // CHUNK])
        prev = sb(s, "prev", [P, 2, 4, HEAD])
        ps = s.enter_context(nc.psum_tensor("kps", [P, 8, 512], F32))
        psZ, psL, psK, psU, psN, psD = (ps[:, n, :] for n in range(6))
        psS = ps[:, 6:8, 0:256]
        consts_in, wg_zero, wg_in, ones_set = sem("consts_in"), sem("wg_zero"), sem("wg_in"), sem("ones_set")
        row_in = [ev(f"row_in{u}", dma=True) for u in range(2)]
        z_in = [ev(f"z_in{u}", dma=True) for u in range(2)]
        rotated, k_split = ev("rotated", 4), ev("k_split", 4)
        k_turned, k_out = ev("k_turned"), ev("k_out")
        z_turned, z_out, logits = ev("z_turned"), ev("z_out"), ev("logits")
        softplus, decays = ev("softplus", 3), ev("decays")
        kept = ev("kept", 2)
        sums, grown, scaled = ev("sums"), ev("grown", 2), ev("scaled")
        added, moved = ev("added"), ev("moved")
        ctx_sum, ctx_exp, ctx_k, ctx_state, ctx_out, scan = (sem(n) for n in ("ctx_sum", "ctx_exp", "ctx_k", "ctx_state", "ctx_out", "scan"))
        block = s.enter_context(nc.Block())

        @block.sync
        def _(sp):
            sp.dma_start(cos[:, :, :], S["cosd"].rearrange("p (t d) -> p t d", d=HEAD)).then_inc(consts_in, 16)
            sp.dma_start(sin[:, :, :], S["sind"].rearrange("p (t d) -> p t d", d=HEAD)).then_inc(consts_in, 16)
            sp.wait_ge(wg_zero, 1)
            for d, (w, b) in enumerate((("w_gate_fwd", "b_gate_fwd"), ("w_gate_bwd", "b_gate_bwd"))):
                sp.dma_start(wg[d * RANK:(d + 1) * RANK, d * 256:(d + 1) * 256], S[w]).then_inc(wg_in, 16)
                sp.dma_start(wg[32:33, d * 256:(d + 1) * 256], S[b].rearrange("(a n) -> a n", a=1)).then_inc(wg_in, 16)
            with sp.Fori(0, TT // 2) as i:
                for u in range(2):
                    t = sp.snap(i * 2 + u)
                    sp.wait_ge(added.sem, added.at(t - 2))
                    sp.wait_ge(kept.sem, kept.at(t - 2))
                    sp.wait_ge(scaled.sem, scaled.at(t - 2))
                    sp.wait_ge(rotated.sem, rotated.at(t - 2))
                    sp.wait_ge(z_turned.sem, z_turned.at(t - 2))
                    sp.dma_start(row[:, u, :], proj[bass.ds(t * P, P), 0:D]).then_inc(row_in[u].sem, 16)
                    sp.dma_start(z[:, u, :], proj[bass.ds(t * P, P), ZZ:ZZ + 2 * RANK]).then_inc(z_in[u].sem, 16)

        @block.gpsimd
        def _(pool):
            rotated.open(pool)
            kept.open(pool)
            pool.wait_ge(consts_in, 32)
            with pool.Fori(0, TT // 2) as i:
                for u in range(2):
                    t = i * 2 + u
                    k = row[:, u, KK:KK + P].rearrange("p (h d) -> p h d", h=KVH)
                    pool.wait_ge(row_in[u].sem, row_in[u].at(i))
                    pool.wait_ge(k_split.sem, k_split.at(t - 1))
                    rope(pool, rotated, t, k, cos, sin, rot, rot2, KVH)
                    pool.tensor_copy(val[:, bass.ds(t + 1, 1), :].rearrange("p s d -> p (s d)"), row[:, u, VV:VV + P]).then_inc(kept.sem, 1)
                    pool.wait_ge(decays.sem, decays.at(t))
                    pool.tensor_copy(la[:, bass.ds(t, 1), :].rearrange("p s d -> p (s d)"), lat[:, u, :]).then_inc(kept.sem, 1)

        @block.scalar
        def _(act):
            for e in (softplus, grown, added):
                e.open(act)
            with act.Fori(0, TT // 2) as i:
                for u in range(2):
                    t = i * 2 + u
                    act.wait_ge(logits.sem, logits.at(t))
                    act.wait_ge(decays.sem, decays.at(t - 1))
                    act.activation(mag[:, :], psL, ACT.Abs).then_inc(softplus.sem, 1)
                    act.wait_ge(softplus.sem, softplus.at(t, 1))
                    act.activation(mag[:, :], mag[:, :], ACT.Exp, scale=-1.0).then_inc(softplus.sem, 1)
                    act.wait_ge(softplus.sem, softplus.at(t, 2))
                    act.activation(mag[:, :], mag[:, :], ACT.Ln, bias=1.0).then_inc(softplus.sem, 1)
                    act.wait_ge(sums.sem, sums.at(t))
                    act.wait_ge(scaled.sem, scaled.at(t - 2))
                    act.activation(grow[:, u, :], psU, ACT.Exp).then_inc(grown.sem, 1)
                    act.wait_ge(moved.sem, moved.at(t))
                    act.activation(dec[:, :, bass.ds(t * 2, 2)], psD[:, 0:8].rearrange("p (q c) -> p q c", q=4), ACT.Exp).then_inc(grown.sem, 1)
                    act.activation(state[:, :, bass.ds(t * 2, 2), :].rearrange("p q c d -> p c q d"),
                                   psS.rearrange("p c (q d) -> p c q d", q=4), ACT.Copy).then_inc(added.sem, 1)
            act.wait_ge(ctx_sum, 1)
            act.wait_ge(scaled.sem, scaled.at(TT - 1))
            act.activation(grow[:, 0, :], psU, ACT.Exp).then_inc(ctx_exp, 1)
            act.activation(grow[:, 1, :], psN, ACT.Exp).then_inc(ctx_exp, 1)
            act.wait_ge(ctx_state, 1)
            act.activation(fin[:, :, :], psS[:, 0, :].rearrange("p (q d) -> p q d", q=4), ACT.Copy).then_inc(ctx_out, 1)

        @block.vector
        def _(dve):
            for e in (k_split, k_out, z_out, decays, scaled):
                e.open(dve)
            dve.memset(wg[:, :], 0.0).then_inc(wg_zero, 1)
            dve.memset(zT[32:33, :, :], 1.0).then_inc(ones_set, 1)
            dve.memset(val[:, 0, :], 0.0).then_inc(ones_set, 1)
            dve.memset(keyT[:, :, :, 0:P].bitcast(F32), 0.0).then_inc(ones_set, 1)
            with dve.Fori(0, TT // 2) as i:
                for u in range(2):
                    t = i * 2 + u
                    dve.wait_ge(z_turned.sem, z_turned.at(t))
                    dve.wait_ge(logits.sem, logits.at(t - 2))
                    dve.tensor_copy(zT[0:32, u, :], psZ[0:32, 0:P]).then_inc(z_out.sem, 1)
                    dve.wait_ge(rotated.sem, rotated.at(t))
                    dve.wait_ge(k_turned.sem, k_turned.at(t - 1))
                    for c in range(2):
                        dve.tensor_copy(kdup[:, 0, :, c, :], rot[:, :, :]).then_inc(k_split.sem, 1)
                    dve.wait_ge(k_split.sem, k_split.at(t, 2))
                    for c in range(2):
                        dve.tensor_tensor(kdup[:, 1, :, c, :], rot[:, :, :], kdup[:, 0, :, c, :].bitcast(F32), ALU.subtract).then_inc(k_split.sem, 1)
                    dve.wait_ge(softplus.sem, softplus.at(t))
                    dve.wait_ge(kept.sem, kept.at(t - 2))
                    dve.wait_ge(moved.sem, moved.at(t - 2))
                    dve.scalar_tensor_tensor(lat[:, u, :], psL, 0.0, mag[:, :], ALU.min, ALU.subtract).then_inc(decays.sem, 1)
                    dve.wait_ge(k_turned.sem, k_turned.at(t))
                    dve.tensor_copy(keyT[:, :, :, bass.ds(t * P + P, P)],
                                    psK.rearrange("p (s h j) -> p s h j", s=2, h=KVH)).then_inc(k_out.sem, 1)
                    dve.wait_ge(grown.sem, grown.at(t, 1))
                    dve.wait_ge(moved.sem, moved.at(t - 2))
                    dve.tensor_tensor(kd[:, u, :, :], grow[:, u, :].rearrange("p (d n) -> p d n", d=2),
                                      row[:, u, GK:GK + 256].unsqueeze(1).broadcast_to([P, 2, 256]), ALU.mult).then_inc(scaled.sem, 1)
            dve.wait_ge(ctx_exp, 2)
            dve.wait_ge(moved.sem, moved.at(TT - 1))
            for u in range(2):
                dve.tensor_tensor(kd[:, u, :, :], grow[:, u, :].rearrange("p (d n) -> p d n", d=2),
                                  row[:, u, GK:GK + 256].unsqueeze(1).broadcast_to([P, 2, 256]), ALU.mult).then_inc(ctx_k, 1)
            dve.wait_ge(ctx_out, 1)
            dve.tensor_copy(prev[:, 0, :, :], fin[:, :, :]).then_inc(scan, 1)
            dve.wait_ge(added.sem, added.at(TT - 1))
            dve.wait_ge(grown.sem, grown.at(TT - 1))
            dve.wait_ge(scan, 1)
            with dve.Fori(0, NCH // 2) as i:
                for u in range(2):
                    n = i * 2 + u
                    for q in range(4):
                        c = n if q < 2 else n * -1 + (NCH - 1)
                        dve.scalar_tensor_tensor(prev[:, 1 - u, q, :], prev[:, u, q, :], dec[:, q, bass.ds(c, 1)],
                                                 state[:, q, bass.ds(c, 1), :].rearrange("p s d -> p (s d)"), ALU.mult, ALU.add)\
                           .then_inc(scan, 1)
                    dve.wait_ge(scan, n * 8 + 5)
                    for q in range(4):
                        c = n if q < 2 else n * -1 + (NCH - 1)
                        dve.tensor_scalar(state[:, q, bass.ds(c, 1), :].rearrange("p s d -> p (s d)"), prev[:, u, q, :], 1.0, None, ALU.mult).then_inc(scan, 1)
                    dve.wait_ge(scan, n * 8 + 9)

        @block.tensor
        def _(pe):
            for e in (k_turned, z_turned, logits, sums, moved):
                e.open(pe)
            ident = con[:, C_ID:C_ID + P]
            pe.wait_ge(wg_in, 64)
            pe.wait_ge(ones_set, 3)
            with pe.Fori(0, TT // 2) as i:
                for u in range(2):
                    t = i * 2 + u
                    pe.wait_ge(z_in[u].sem, z_in[u].at(i))
                    pe.wait_ge(z_out.sem, z_out.at(t - 1))
                    pe.transpose(psZ[0:32, 0:P], z[:, u, :], ident).then_inc(z_turned.sem, 1)
                    pe.wait_ge(z_out.sem, z_out.at(t))
                    pe.wait_ge(decays.sem, decays.at(t - 1))
                    pe.matmul(psL, zT[:, u, :], wg[:, :], start=True, stop=True).then_inc(logits.sem, 1)
                    pe.wait_ge(k_split.sem, k_split.at(t))
                    pe.wait_ge(k_out.sem, k_out.at(t - 1))
                    for m in range(2):
                        for h in range(KVH):
                            mm = pe.transpose(psK[:, (m * KVH + h) * P:(m * KVH + h + 1) * P],
                                              kdup[:, m, h, :, :].rearrange("p c d -> p (c d)").bitcast(F32), ident)
                    mm.then_inc(k_turned.sem, 1)
                    pe.wait_ge(decays.sem, decays.at(t))
                    pe.wait_ge(grown.sem, grown.at(t - 1))
                    pe.matmul(psU[:, 0:256], con[:, C_SUF_F:C_SUF_F + P], lat[:, u, 0:256], start=True, stop=True)
                    mm = pe.matmul(psU[:, 256:512], con[:, C_SUF_B:C_SUF_B + P], lat[:, u, 256:512], start=True, stop=True)
                    mm.then_inc(sums.sem, 1)
                    pe.wait_ge(scaled.sem, scaled.at(t))
                    pe.wait_ge(added.sem, added.at(t - 1))
                    for q in range(4):
                        pe.matmul(psD[:, 2 * q:2 * q + 2], lat[:, u, q * P:(q + 1) * P], con[:, C_IND:C_IND + 2], start=True, stop=True)
                    for d in range(2):
                        for g in range(2):
                            for ch in range(2):
                                for h in range(4):
                                    n = d * 2 + g
                                    rows = slice(ch * CHUNK, (ch + 1) * CHUNK)
                                    mm = pe.matmul(psS[h * DK:(h + 1) * DK, ch, n * HEAD:(n + 1) * HEAD],
                                                   kd[rows, u, d, (g * 4 + h) * DK:(g * 4 + h + 1) * DK],
                                                   row[rows, u, GV + (g * 4 + h) * HEAD:GV + (g * 4 + h + 1) * HEAD],
                                                   start=True, stop=True, tile_position=(ch * CHUNK, h * DK))
                    mm.then_inc(moved.sem, 1)
            pe.wait_ge(grown.sem, grown.at(TT - 1))
            early, late, every = con[:, C_CTX_B:C_CTX_B + P], con[:, C_CTX_F:C_CTX_F + P], con[:, C_ALL:C_ALL + P]
            pe.matmul(psU[:, 0:256], late, lat[:, 0, 0:256], start=True, stop=False)
            pe.matmul(psU[:, 0:256], every, lat[:, 1, 0:256], start=False, stop=True)
            pe.matmul(psU[:, 256:512], early, lat[:, 0, 256:512], start=True, stop=True)
            pe.matmul(psN[:, 0:256], late, lat[:, 1, 0:256], start=True, stop=True)
            pe.matmul(psN[:, 256:512], early, lat[:, 1, 256:512], start=True, stop=False)
            pe.matmul(psN[:, 256:512], every, lat[:, 0, 256:512], start=False, stop=True).then_inc(ctx_sum, 1)
            pe.wait_ge(ctx_k, 2)
            pe.wait_ge(added.sem, added.at(TT - 1))
            for d in range(2):
                for g in range(2):
                    for h in range(4):
                        n = d * 2 + g
                        for u in range(2):
                            mm = pe.matmul(psS[h * DK:(h + 1) * DK, 0, n * HEAD:(n + 1) * HEAD],
                                           kd[:, u, d, (g * 4 + h) * DK:(g * 4 + h + 1) * DK],
                                           row[:, u, GV + (g * 4 + h) * HEAD:GV + (g * 4 + h + 1) * HEAD],
                                           start=(u == 0), stop=(u == 1), tile_position=(0, h * DK))
            mm.then_inc(ctx_state, 1)


def mix_block(nc, S):
    sb, con, proj = S["sb"], S["con"], S["proj"]
    cos, sin, keyT, val, la, state = (S[n] for n in ("cos", "sin", "keyT", "val", "la", "state"))
    mixd = S["mixd"]
    with ExitStack() as s:
        def sem(name):
            return s.enter_context(nc.semaphore("x_" + name))

        def ev(name, per=1, dma=False, credit=None):
            return Event(nc, s, "x_" + name, per, dma, credit)
        KEYS = 3 * P + CTX
        prev_mask = sb(s, "prev_mask", [P, LT, P], BF16)
        next_mask = sb(s, "next_mask", [P, LT, P], BF16)
        identb = sb(s, "identb", [P, P], BF16)
        nsink = sb(s, "nsink", [P, AH])
        gain = sb(s, "gain", [P, HEAD])
        row = sb(s, "xrow", [P, 2, COLS])
        rot = sb(s, "qrot", [P, AH, HEAD])
        rot2 = sb(s, "qrot2", [P, AH, HEAD])
        qs = sb(s, "qs", [P, AH, 2, HEAD], F32R)
        qT = sb(s, "qT", [P, 2, AH * P], F32R)
        prob = sb(s, "prob", [P, 2, KEYS])
        probT = sb(s, "probT", [P, 2, KEYS])
        mx = sb(s, "mx", [P, AH])
        negm = sb(s, "negm", [P, AH])
        den = sb(s, "den", [P, AH])
        snk = sb(s, "snk", [P, AH])
        mix = sb(s, "mix", [P, 2, D])
        expb = sb(s, "expb", [P, 2, 512])
        qd = sb(s, "qd", [P, 512])
        ki = sb(s, "ki", [P, 512])
        qkT = sb(s, "qkT", [P, 8, P])
        amask = sb(s, "amask", [P, 2, P])
        am = sb(s, "am", [P, 4, 4, P])
        st = sb(s, "st", [P, 4, 2, 4, HEAD])
        sg = sb(s, "sg", [P, 512])
        gg = sb(s, "gg", [P, 512])
        sq = sb(s, "sq", [P, 512])
        ssq = sb(s, "gssq", [P, GH])
        rs = sb(s, "grs", [P, GH])
        ps = s.enter_context(nc.psum_tensor("xps", [P, 8, 512], F32))
        flat = ps[:, :, :].rearrange("p b n -> p (b n)")
        psP = flat[:, 4 * 512:6 * 512]
        psO = flat[:, 6 * 512:7 * 512]
        psM = flat[:, 7 * 512:8 * 512]
        setup_in, setup = sem("setup_in"), sem("setup")
        row_in = [ev(f"row_in{u}", dma=True) for u in range(2)]
        rotated, q_hi, q_lo = ev("rotated", 4), ev("q_hi"), ev("q_lo")
        turned, evac = ev("turned", 10), ev("evac", 10)
        scores, shifted, exps, pv = ev("scores", 8), ev("shifted", 16), ev("exps", 8), ev("pv", 8)
        sink_exp, attn = ev("sink_exp"), ev("attn", 4)
        prefix, expd, q_dec, k_inv = ev("prefix"), ev("expd", 2), ev("q_dec"), ev("k_inv")
        inner, masked, gla, states = ev("inner"), ev("masked", 2), ev("gla"), ev("states", 4)
        gate_exp, gate, gained, gated = ev("gate_exp"), ev("gate", 2), ev("gained", 2), ev("gated")
        squares, meansq, rstd, mixed = ev("squares"), ev("meansq"), ev("rstd", 2), ev("mixed", 2)
        stored = [ev(f"stored{u}", dma=True, credit=1) for u in range(2)]
        block = s.enter_context(nc.Block())

        def score_tile(h):
            return flat[:, (h % 2) * 1024 + P:(h % 2) * 1024 + P + KEYS]

        @block.sync
        def _(sp):
            sp.dma_start(nsink[:, :], S["attn_sink"].partition_broadcast(P)).then_inc(setup_in, 16)
            sp.dma_start(gain[:, :], S["g_gla"].partition_broadcast(P)).then_inc(setup_in, 16)
            for u in range(2):
                stored[u].open(sp)

            def load(t, u):
                sp.wait_ge(gla.sem, gla.at(t - 2))
                sp.wait_ge(gated.sem, gated.at(t - 2))
                sp.wait_ge(k_inv.sem, k_inv.at(t - 2))
                sp.wait_ge(rotated.sem, rotated.at(t - 2))
                sp.dma_start(row[:, u, :], proj[bass.ds(t * P, P), :]).then_inc(row_in[u].sem, 16)

            def store(t, u):
                sp.wait_ge(mixed.sem, mixed.at(t))
                sp.wait_ge(attn.sem, attn.at(t))
                sp.dma_start(mixd[bass.ds(t * P, P), :], mix[:, u, :]).then_inc(stored[u].sem, 16)

            load(0, 0)
            with sp.Fori(0, LT // 2 - 1) as i:
                for u in range(2):
                    t = sp.snap(i * 2 + u)
                    load(sp.snap(t + 1), 1 - u)
                    store(t, u)
            load(LT - 1, 1)
            store(LT - 2, 0)
            store(LT - 1, 1)
            for u in range(2):
                sp.wait_ge(stored[u].sem, stored[u].at(LT // 2 - 1))

        @block.gpsimd
        def _(pool):
            for e in (rotated, k_inv, states, gained, gated):
                e.open(pool)
            with pool.Fori(0, LT // 2) as i:
                for u in range(2):
                    t = i * 2 + u
                    pool.wait_ge(row_in[u].sem, row_in[u].at(i))
                    pool.wait_ge(q_hi.sem, q_hi.at(t - 1))
                    pool.wait_ge(q_lo.sem, q_lo.at(t - 1))
                    rope(pool, rotated, t, row[:, u, QQ:QQ + 512].rearrange("p (h d) -> p h d", h=AH), cos, sin, rot, rot2, AH)
                    pool.wait_ge(gla.sem, gla.at(t - 1))
                    for q in range(4):
                        pool.tensor_tensor(st[:, q, :, :, :], state[:, q, bass.ds(t * 2, 2), :].unsqueeze(2).broadcast_to([P, 2, 4, HEAD]),
                                           con[:, C_HEAD:C_COLS].unsqueeze(1).unsqueeze(3).broadcast_to([P, 2, 4, HEAD]),
                                           ALU.mult).then_inc(states.sem, 1)
                    pool.wait_ge(expd.sem, expd.at(t))
                    pool.wait_ge(turned.sem, turned.at(t - 1))
                    pool.tensor_tensor(ki[:, :].rearrange("p (d n) -> p d n", d=2), expb[:, 1, :].rearrange("p (d n) -> p d n", d=2),
                                       row[:, u, GK:GK + 256].unsqueeze(1).broadcast_to([P, 2, 256]), ALU.mult).then_inc(k_inv.sem, 1)
                    for n, col in enumerate((GG1, GG2)):
                        pool.wait_ge(mixed.sem, mixed.at(t - 1))
                        pool.tensor_tensor(gg[:, n * 256:(n + 1) * 256].rearrange("p (h d) -> p h d", d=HEAD),
                                           row[:, u, col:col + 256].rearrange("p (h d) -> p h d", d=HEAD),
                                           gain[:, :].unsqueeze(1).broadcast_to([P, 4, HEAD]), ALU.mult).then_inc(gained.sem, 1)
                    pool.wait_ge(gate.sem, gate.at(t))
                    pool.wait_ge(gained.sem, gained.at(t))
                    pool.tensor_tensor(gg[:, :], gg[:, :], sg[:, :], ALU.mult).then_inc(gated.sem, 1)

        @block.scalar
        def _(act):
            for e in (q_hi, exps, sink_exp, expd, gate_exp, squares, rstd):
                e.open(act)
            with act.Fori(0, LT // 2) as i:
                for u in range(2):
                    t = i * 2 + u
                    act.wait_ge(rotated.sem, rotated.at(t))
                    act.wait_ge(turned.sem, turned.at(t - 1, 1))
                    act.activation(qs[:, :, 0, :], rot[:, :, :], ACT.Copy).then_inc(q_hi.sem, 1)
                    act.wait_ge(prefix.sem, prefix.at(t))
                    act.wait_ge(q_dec.sem, q_dec.at(t - 1))
                    act.wait_ge(k_inv.sem, k_inv.at(t - 1))
                    act.activation(expb[:, 0, :], psM, ACT.Exp).then_inc(expd.sem, 1)
                    act.activation(expb[:, 1, :], psM, ACT.Exp, scale=-1.0).then_inc(expd.sem, 1)
                    act.wait_ge(row_in[u].sem, row_in[u].at(i))
                    act.wait_ge(gated.sem, gated.at(t - 1))
                    for n, col in enumerate((GG1, GG2)):
                        a = act.activation(sg[:, n * 256:(n + 1) * 256], row[:, u, col:col + 256], ACT.Exp, scale=-1.0)
                    a.then_inc(gate_exp.sem, 1)
                    for h in range(AH):
                        act.wait_ge(shifted.sem, shifted.at(t, 2 * h + 2))
                        act.wait_ge(turned.sem, turned.at(t, h) if h >= 2 else turned.at(t - 1, 8 + h))
                        if h == 0:
                            act.wait_ge(attn.sem, attn.at(t - 1))
                        act.activation(prob[:, h % 2, :], score_tile(h), ACT.Exp, scale=0.125, bias=negm[:, h:h + 1],
                                       accum_out=den[:, h:h + 1]).then_inc(exps.sem, 1)
                    act.wait_ge(attn.sem, attn.at(t, 1))
                    act.activation(snk[:, :], snk[:, :], ACT.Exp).then_inc(sink_exp.sem, 1)
                    act.wait_ge(gla.sem, gla.at(t))
                    act.wait_ge(meansq.sem, meansq.at(t - 1))
                    act.activation(sq[:, :], psM, ACT.Square).then_inc(squares.sem, 1)
                    act.wait_ge(meansq.sem, meansq.at(t))
                    act.wait_ge(mixed.sem, mixed.at(t - 1))
                    act.activation(rs[:, :], ssq[:, :], ACT.Ln, scale=1.0 / HEAD, bias=S["epsb"][:, :]).then_inc(rstd.sem, 1)
                    act.wait_ge(rstd.sem, rstd.at(t, 1))
                    act.activation(rs[:, :], rs[:, :], ACT.Exp, scale=-0.5).then_inc(rstd.sem, 1)

        @block.vector
        def _(dve):
            for e in (q_lo, evac, shifted, attn, q_dec, masked, gate, meansq, mixed):
                e.open(dve)
            dve.wait_ge(setup_in, 32)
            dve.tensor_scalar(nsink[:, :], nsink[:, :], -1.0, None, ALU.mult).then_inc(setup, 1)
            dve.memset(prev_mask[:, 0:1, :], NEG).then_inc(setup, 1)
            dve.memset(next_mask[:, LT - 1:LT, :], NEG).then_inc(setup, 1)
            dve.tensor_copy(prev_mask[:, 1:LT, :], con[:, C_PREV:C_PREV + P].unsqueeze(1).broadcast_to([P, LT - 1, P])).then_inc(setup, 1)
            dve.tensor_copy(next_mask[:, 0:LT - 1, :], con[:, C_NEXT:C_NEXT + P].unsqueeze(1).broadcast_to([P, LT - 1, P])).then_inc(setup, 1)
            dve.tensor_copy(identb[:, :], con[:, C_ID:C_ID + P]).then_inc(setup, 1)
            dve.tensor_scalar(amask[:, 0, :], con[:, C_PREF_F:C_PREF_F + P], TAU, None, ALU.mult).then_inc(setup, 1)
            dve.tensor_scalar(amask[:, 1, :], con[:, C_PREF_B:C_PREF_B + P], TAU, None, ALU.mult).then_inc(setup, 1)
            dve.wait_ge(setup, 8)
            with dve.Fori(0, LT // 2) as i:
                for u in range(2):
                    t = i * 2 + u
                    dve.wait_ge(q_hi.sem, q_hi.at(t))
                    dve.tensor_tensor(qs[:, :, 1, :], rot[:, :, :], qs[:, :, 0, :].bitcast(F32), ALU.subtract).then_inc(q_lo.sem, 1)
                    dve.wait_ge(turned.sem, turned.at(t, 1))
                    dve.wait_ge(scores.sem, scores.at(t - 2))
                    dve.tensor_copy(qT[:, u, :], psP).then_inc(evac.sem, 1)
                    dve.wait_ge(expd.sem, expd.at(t))
                    dve.wait_ge(turned.sem, turned.at(t - 1))
                    dve.scalar_tensor_tensor(qd[:, :].rearrange("p (d n) -> p d n", d=2),
                                             row[:, u, GQ:GQ + 256].unsqueeze(1).broadcast_to([P, 2, 256]), DK ** -0.5,
                                             expb[:, 0, :].rearrange("p (d n) -> p d n", d=2), ALU.mult, ALU.mult).then_inc(q_dec.sem, 1)
                    dve.wait_ge(gate_exp.sem, gate_exp.at(t))
                    dve.tensor_scalar(sg[:, :], sg[:, :], 1.0, None, ALU.add).then_inc(gate.sem, 1)
                    dve.wait_ge(gate.sem, gate.at(t, 1))
                    dve.reciprocal(sg[:, :], sg[:, :]).then_inc(gate.sem, 1)

                    def transposed(h):
                        dve.wait_ge(turned.sem, turned.at(t, h + 2))
                        dve.wait_ge(pv.sem, pv.at(t, h - 1) if h >= 2 else pv.at(t - 1, 7 + h))
                        dve.tensor_copy(probT[:, h % 2, :], psP[:, 0:KEYS]).then_inc(evac.sem, 1)

                    for h in range(AH):
                        dve.wait_ge(scores.sem, scores.at(t, h + 1))
                        if h == 0:
                            dve.wait_ge(exps.sem, exps.at(t - 1))
                        dve.reduce_max(mx[:, h:h + 1], score_tile(h), AX.X).then_inc(shifted.sem, 1)
                        dve.wait_ge(shifted.sem, shifted.at(t, 2 * h + 1))
                        dve.tensor_scalar(negm[:, h:h + 1], mx[:, h:h + 1], -0.125, nsink[:, h:h + 1], ALU.mult, ALU.min).then_inc(shifted.sem, 1)
                        if h:
                            transposed(h - 1)
                    transposed(AH - 1)
                    dve.wait_ge(shifted.sem, shifted.at(t))
                    dve.tensor_tensor(snk[:, :], negm[:, :], nsink[:, :], ALU.subtract).then_inc(attn.sem, 1)
                    dve.wait_ge(sink_exp.sem, sink_exp.at(t))
                    dve.tensor_tensor(den[:, :], den[:, :], snk[:, :], ALU.add).then_inc(attn.sem, 1)
                    dve.wait_ge(attn.sem, attn.at(t, 2))
                    dve.reciprocal(den[:, :], den[:, :]).then_inc(attn.sem, 1)
                    dve.wait_ge(attn.sem, attn.at(t, 3))
                    dve.wait_ge(pv.sem, pv.at(t))
                    dve.wait_ge(stored[u].sem, stored[u].at(i - 1))
                    dve.tensor_tensor(mix[:, u, 0:512].rearrange("p (h d) -> p h d", d=HEAD), psO.rearrange("p (h d) -> p h d", d=HEAD),
                                      den[:, :].unsqueeze(2).broadcast_to([P, AH, HEAD]), ALU.mult).then_inc(attn.sem, 1)
                    dve.wait_ge(turned.sem, turned.at(t, 10))
                    dve.tensor_copy(qkT[:, :, :], psP.rearrange("p (b j) -> p b j", j=P)).then_inc(evac.sem, 1)
                    dve.wait_ge(inner.sem, inner.at(t))
                    for d in range(2):
                        dve.tensor_tensor(am[:, 2 * d:2 * d + 2, :, :].rearrange("p g h j -> p h g j"),
                                          ps[:, 0:4, 2 * d * P:2 * (d + 1) * P].rearrange("p h (g j) -> p h g j", g=2),
                                          amask[:, d, :].unsqueeze(1).unsqueeze(1).broadcast_to([P, 4, 2, P]), ALU.mult).then_inc(masked.sem, 1)
                    dve.wait_ge(squares.sem, squares.at(t))
                    dve.wait_ge(rstd.sem, rstd.at(t - 1))
                    dve.reduce_sum(ssq[:, :], sq[:, :].rearrange("p (h d) -> p h d", d=HEAD), AX.X).then_inc(meansq.sem, 1)
                    dve.wait_ge(rstd.sem, rstd.at(t))
                    o = mix[:, u, 512:1024]
                    dve.tensor_tensor(o.rearrange("p (h d) -> p h d", d=HEAD), psM.rearrange("p (h d) -> p h d", d=HEAD),
                                      rs[:, :].unsqueeze(2).broadcast_to([P, GH, HEAD]), ALU.mult).then_inc(mixed.sem, 1)
                    dve.wait_ge(mixed.sem, mixed.at(t, 1))
                    dve.wait_ge(gated.sem, gated.at(t))
                    dve.tensor_tensor(o, o, gg[:, :], ALU.mult).then_inc(mixed.sem, 1)

        @block.tensor
        def _(pe):
            for e in (turned, scores, pv, prefix, inner, gla):
                e.open(pe)
            ident = con[:, C_ID:C_ID + P]
            pe.wait_ge(setup, 8)
            with pe.Fori(0, LT // 2) as i:
                for u in range(2):
                    t = i * 2 + u
                    pe.wait_ge(mixed.sem, mixed.at(t - 1, 1))
                    for d, m in enumerate((C_PREF_F, C_PREF_B)):
                        mm = pe.matmul(psM[:, d * 256:(d + 1) * 256], con[:, m:m + P],
                                       la[:, bass.ds(t, 1), d * 256:(d + 1) * 256].rearrange("p s n -> p (s n)"), start=True, stop=True)
                    mm.then_inc(prefix.sem, 1)
                    pe.wait_ge(q_lo.sem, q_lo.at(t))
                    pe.wait_ge(evac.sem, evac.at(t - 1))
                    for h in range(AH):
                        mm = pe.transpose(psP[:, h * P:(h + 1) * P], qs[:, h, :, :].rearrange("p m d -> p (m d)").bitcast(F32), ident)
                    mm.then_inc(turned.sem, 1)

                    def score(h):
                        if h == 0:
                            pe.wait_ge(evac.sem, evac.at(t, 1))
                            pe.wait_ge(masked.sem, masked.at(t - 1))
                        if h >= 2:
                            pe.wait_ge(exps.sem, exps.at(t, h - 1))
                        sc, q, kv = score_tile(h), qT[:, u, h * P:(h + 1) * P], h // 4
                        pe.matmul(sc[:, 0:3 * P], q, keyT[:, 0, kv, bass.ds(t * P, 3 * P)], start=True, stop=False)
                        pe.matmul(sc[:, 0:P], identb[:, :], prev_mask[:, bass.ds(t, 1), :].rearrange("p s j -> p (s j)"), start=False, stop=False)
                        pe.matmul(sc[:, 2 * P:3 * P], identb[:, :], next_mask[:, bass.ds(t, 1), :].rearrange("p s j -> p (s j)"), start=False, stop=False)
                        pe.matmul(sc[:, 0:3 * P], q, keyT[:, 1, kv, bass.ds(t * P, 3 * P)], start=False, stop=True)
                        for m in range(2):
                            mm = pe.matmul(sc[:, 3 * P:KEYS], q, keyT[:, m, kv, (LT + 1) * P:(TT + 1) * P], start=(m == 0), stop=(m == 1))
                        mm.then_inc(scores.sem, 1)

                    def turn(h):
                        pe.wait_ge(exps.sem, exps.at(t, h + 1))
                        pe.wait_ge(evac.sem, evac.at(t, h + 1))
                        for b in range(KEYS // P):
                            mm = pe.transpose(psP[:, b * P:(b + 1) * P], prob[:, h % 2, b * P:(b + 1) * P], ident)
                        mm.then_inc(turned.sem, 1)

                    def weigh(h):
                        pe.wait_ge(evac.sem, evac.at(t, h + 2))
                        if h == 0:
                            pe.wait_ge(attn.sem, attn.at(t - 1))
                        kv = (h // 4) * HEAD
                        for b in range(KEYS // P):
                            v = val[:, bass.ds(t + b, 1), kv:kv + HEAD].rearrange("p s d -> p (s d)") if b < 3 else val[:, LT + 1 + b - 3, kv:kv + HEAD]
                            mm = pe.matmul(psO[:, h * HEAD:(h + 1) * HEAD], probT[:, h % 2, b * P:(b + 1) * P], v,
                                           start=(b == 0), stop=(b == KEYS // P - 1))
                        mm.then_inc(pv.sem, 1)

                    for h in range(AH + 2):
                        if h < AH:
                            score(h)
                        if 1 <= h <= AH:
                            turn(h - 1)
                        if h >= 2:
                            weigh(h - 2)
                    pe.wait_ge(q_dec.sem, q_dec.at(t))
                    pe.wait_ge(k_inv.sem, k_inv.at(t))
                    pe.wait_ge(evac.sem, evac.at(t, 9))
                    for b in range(8):
                        mm = pe.transpose(psP[:, b * P:(b + 1) * P], (qd if b < 4 else ki)[:, (b % 4) * P:(b % 4 + 1) * P], ident)
                    mm.then_inc(turned.sem, 1)
                    pe.wait_ge(evac.sem, evac.at(t, 10))
                    pe.wait_ge(exps.sem, exps.at(t))
                    for q in range(4):
                        for h in range(4):
                            r = slice(h * DK, (h + 1) * DK)
                            mm = pe.matmul(ps[:, h, q * P:(q + 1) * P], qkT[r, 4 + q, :], qkT[r, q, :], start=True, stop=True)
                    mm.then_inc(inner.sem, 1)
                    pe.wait_ge(masked.sem, masked.at(t))
                    pe.wait_ge(states.sem, states.at(t))
                    pe.wait_ge(expd.sem, expd.at(t))
                    for g in range(2):
                        for d in range(2):
                            for ch in range(2):
                                j = slice(ch * CHUNK, (ch + 1) * CHUNK)
                                pe.matmul(psM[j, g * 256:(g + 1) * 256], qkT[:, d * 2 + g, j],
                                          st[:, d * 2 + g, ch, :, :].rearrange("p h d -> p (h d)"),
                                          start=(g == 0 and d == 0), stop=False, skip_group_check=True)
                    for h in range(GH):
                        for d in range(2):
                            mm = pe.matmul(psM[:, h * HEAD:(h + 1) * HEAD], am[:, 2 * d + h // 4, h % 4, :],
                                           row[:, u, GV + h * HEAD:GV + (h + 1) * HEAD], start=False, stop=(h == GH - 1 and d == 1),
                                           skip_group_check=True)
                    mm.then_inc(gla.sem, 1)


def output_block(nc, S):
    sb, con, A2, B2, G1, epsb = (S[n] for n in ("sb", "con", "A2", "B2", "G1", "epsb"))
    h2h, h2l, mixd, x2d = (S[n] for n in ("h2h", "h2l", "mixd", "x2d"))
    with ExitStack() as s:
        def sem(name):
            return s.enter_context(nc.semaphore("o_" + name))

        def ev(name, per=1, dma=False, credit=None):
            return Event(nc, s, "o_" + name, per, dma, credit)
        woh = sb(s, "woh", [P, KT, D], F32R)
        wol = sb(s, "wol", [P, KT, D], F32R)
        raw = sb(s, "oraw", [P, 2, D])
        mix = sb(s, "omix", [P, D])
        x = sb(s, "ox", [P, 2, D])
        mh = sb(s, "omh", [P, 2, KT, P], F32R)
        ml = sb(s, "oml", [P, 2, KT, P], F32R)
        junk = sb(s, "ojunk", [P, D])
        work = sb(s, "owork", [P, 2, D])
        stats = sb(s, "ostats", [P, 2, 4])
        h2 = sb(s, "oh2", [P, KT, P])
        ps = s.enter_context(nc.psum_tensor("ops", [P, 8, 512], F32))
        flat = ps[:, :, :].rearrange("p b n -> p (b n)")
        psT, psY, psH = flat[:, 0:1024], [flat[:, 1024:2048], flat[:, 2048:3072]], flat[:, 3072:4096]
        raw_in, hi, lo = [sem(f"raw_in{n}") for n in range(2)], sem("hi"), sem("lo")
        mix_in, x_in = ev("mix_in", dma=True), [ev(f"x_in{u}", dma=True) for u in range(2)]
        mix_turned, mix_hi, mix_lo, product = ev("mix_turned"), ev("mix_hi"), ev("mix_lo"), ev("product")
        squares, roots, inverse = ev("squares", 2), ev("roots", 2), ev("inverse", 2)
        branch, residual, normed = ev("branch"), ev("residual"), ev("normed")
        turned, modulated, h_hi, h_lo = ev("turned"), ev("modulated"), ev("h_hi"), ev("h_lo")
        stored = [ev(f"stored{u}", dma=True, credit=1) for u in range(2)]
        block = s.enter_context(nc.Block())

        def pipelined(eng, ahead, now, behind):
            ahead(0, 0, 0)
            ahead(1, 1, 0)
            now(0, 0, 0)
            with eng.Fori(0, LT // 2 - 1) as i:
                for u in range(2):
                    t = i * 2 + (u + 1)
                    ahead(t + 1, u, i + 1)
                    now(t, 1 - u, i + u)
                    behind(t - 1, u, i)
            now(LT - 1, 1, LT // 2 - 1)
            behind(LT - 2, 0, LT // 2 - 1)
            behind(LT - 1, 1, LT // 2 - 1)

        def nothing(t, u, n):
            pass

        @block.sync
        def _(sp):
            for k in range(KT):
                if k >= 2:
                    sp.wait_ge(lo, k - 1)
                sp.dma_start(raw[:, k % 2, :], S["w_out"][k * P:(k + 1) * P, :]).then_inc(raw_in[k % 2], 16)

            def load(t, u, i):
                sp.wait_ge(mix_turned.sem, mix_turned.at(t - 1))
                sp.dma_start(mix[:, :], mixd[bass.ds(t * P, P), :]).then_inc(mix_in.sem, 16)
                sp.wait_ge(turned.sem, turned.at(t - 2))
                sp.wait_ge(stored[u].sem, stored[u].at(i - 1))
                sp.dma_start(x[:, u, :], S["xall"][bass.ds(t * P, P), :]).then_inc(x_in[u].sem, 16)
            with sp.Fori(0, LT // 2) as i:
                for u in range(2):
                    load(sp.snap(i * 2 + u), u, i)

        @block.gpsimd
        def _(pool):
            residual.open(pool)
            h_lo.open(pool)

            def add(t, u, n):
                pool.wait_ge(branch.sem, branch.at(t))
                pool.wait_ge(x_in[u].sem, x_in[u].at(n))
                pool.tensor_tensor(x[:, u, :], x[:, u, :], work[:, u, :], ALU.add).then_inc(residual.sem, 1)

            def low(t, u, n):
                pool.wait_ge(h_hi.sem, h_hi.at(t))
                pool.tensor_tensor(h2l[:, :, bass.ds(t * P, P)], h2[:, :, :], h2h[:, :, bass.ds(t * P, P)].bitcast(F32),
                                   ALU.subtract).then_inc(h_lo.sem, 1)
            pipelined(pool, nothing, add, low)

        @block.scalar
        def _(act):
            for e in (mix_hi, squares, roots, modulated, h_hi, *stored):
                e.open(act)
            for k in range(KT):
                act.wait_ge(raw_in[k % 2], 16 * (k // 2 + 1))
                act.activation(woh[:, k, :], raw[:, k % 2, :], ACT.Copy).then_inc(hi, 1)

            def stat(n, t, u, src):
                act.activation(junk[:, :], src, ACT.Square, accum_out=stats[:, u, 2 * n:2 * n + 1]).then_inc(squares.sem, 1)
                act.wait_ge(squares.sem, squares.at(t, n + 1))
                act.activation(stats[:, u, 2 * n + 1:2 * n + 2], stats[:, u, 2 * n:2 * n + 1], ACT.Sqrt, scale=1.0 / D,
                               bias=epsb[:, :]).then_inc(roots.sem, 1)

            def high(t, u, n):
                act.wait_ge(mix_turned.sem, mix_turned.at(t))
                act.wait_ge(product.sem, product.at(t - 2))
                act.activation(mh[:, u, :, :], psT.rearrange("p (k j) -> p k j", j=P), ACT.Copy).then_inc(mix_hi.sem, 1)

            def sums(t, u, n):
                act.wait_ge(product.sem, product.at(t))
                act.wait_ge(squares.sem, squares.at(t - 1))
                act.wait_ge(branch.sem, branch.at(t - 2))
                stat(0, t, u, psY[u])
                act.wait_ge(residual.sem, residual.at(t))
                act.dma_start(x2d[bass.ds(t * P, P), :], x[:, u, :]).then_inc(stored[u].sem, 16)
                act.wait_ge(squares.sem, squares.at(t, 1))
                stat(1, t, u, x[:, u, :])

            def modulate(t, u, n):
                act.wait_ge(turned.sem, turned.at(t))
                act.wait_ge(h_lo.sem, h_lo.at(t - 1))
                for k in range(KT):
                    a = act.activation(h2[:, k, :], psH[:, k * P:(k + 1) * P], ACT.Identity, scale=A2[:, k:k + 1], bias=B2[:, k:k + 1])
                a.then_inc(modulated.sem, 1)
                act.wait_ge(modulated.sem, modulated.at(t))
                act.activation(h2h[:, :, bass.ds(t * P, P)], h2[:, :, :], ACT.Copy).then_inc(h_hi.sem, 1)
            pipelined(act, high, sums, modulate)
            for u in range(2):
                act.wait_ge(stored[u].sem, stored[u].at(LT // 2 - 1))

        @block.vector
        def _(dve):
            for e in (mix_lo, inverse, branch, normed):
                e.open(dve)
            for k in range(KT):
                dve.wait_ge(hi, k + 1)
                dve.tensor_tensor(wol[:, k, :], raw[:, k % 2, :], woh[:, k, :].bitcast(F32), ALU.subtract).then_inc(lo, 1)

            def low(t, u, n):
                dve.wait_ge(mix_hi.sem, mix_hi.at(t))
                dve.tensor_tensor(ml[:, u, :, :], psT.rearrange("p (k j) -> p k j", j=P), mh[:, u, :, :].bitcast(F32), ALU.subtract).then_inc(mix_lo.sem, 1)

            def norm(t, u, n):
                dve.wait_ge(roots.sem, roots.at(t, 1))
                dve.reciprocal(stats[:, u, 1:2], stats[:, u, 1:2]).then_inc(inverse.sem, 1)
                dve.wait_ge(inverse.sem, inverse.at(t, 1))
                dve.wait_ge(turned.sem, turned.at(t - 2))
                dve.scalar_tensor_tensor(work[:, u, :], psY[u], stats[:, u, 1:2], G1[:, :], ALU.mult, ALU.mult).then_inc(branch.sem, 1)
                dve.wait_ge(roots.sem, roots.at(t, 2))
                dve.reciprocal(stats[:, u, 3:4], stats[:, u, 3:4]).then_inc(inverse.sem, 1)
                dve.wait_ge(inverse.sem, inverse.at(t, 2))
                dve.wait_ge(branch.sem, branch.at(t))
                dve.tensor_scalar(work[:, u, :], x[:, u, :], stats[:, u, 3:4], None, ALU.mult).then_inc(normed.sem, 1)
            pipelined(dve, low, norm, nothing)

        @block.tensor
        def _(pe):
            for e in (mix_turned, product, turned):
                e.open(pe)
            ident = con[:, C_ID:C_ID + P]

            def turn_mix(t, u, n):
                pe.wait_ge(mix_in.sem, mix_in.at(t))
                pe.wait_ge(mix_lo.sem, mix_lo.at(t - 1))
                for k in range(KT):
                    mm = pe.transpose(psT[:, k * P:(k + 1) * P], mix[:, k * P:(k + 1) * P], ident)
                mm.then_inc(mix_turned.sem, 1)

            def project(t, u, n):
                pe.wait_ge(mix_lo.sem, mix_lo.at(t))
                pe.wait_ge(branch.sem, branch.at(t - 2))
                for n in range(2):
                    m = 0
                    for k in range(KT):
                        for a, b in ((mh, woh), (ml, woh), (mh, wol)):
                            mm = pe.matmul(psY[u][:, n * 512:(n + 1) * 512], a[:, u, k, :], b[:, k, n * 512:(n + 1) * 512],
                                           start=(m == 0), stop=(m == 3 * KT - 1))
                            m += 1
                mm.then_inc(product.sem, 1)

            def turn_h(t, u, n):
                pe.wait_ge(normed.sem, normed.at(t))
                pe.wait_ge(modulated.sem, modulated.at(t - 1))
                for k in range(KT):
                    mm = pe.transpose(psH[:, k * P:(k + 1) * P], work[:, u, k * P:(k + 1) * P], ident)
                mm.then_inc(turned.sem, 1)

            pe.wait_ge(lo, KT)
            pipelined(pe, turn_mix, project, turn_h)


def ffn_block(nc, S):
    sb, G2, epsb, h2h, h2l, x2d = (S[n] for n in ("sb", "G2", "epsb", "h2h", "h2l", "x2d"))
    with ExitStack() as s:
        def sem(name):
            return s.enter_context(nc.semaphore("f_" + name))

        def ev(name, per=1, dma=False):
            return Event(nc, s, "f_" + name, per, dma)
        HALF = SEQ // 2
        wih = sb(s, "wih", [P, 2, KT, 2, P], F32R)
        wil = sb(s, "wil", [P, 2, KT, 2, P], F32R)
        raw = sb(s, "fraw", [P, KT, 2, 2 * P])
        wdh = sb(s, "wdh", [P, 2, D], F32R)
        wdl = sb(s, "wdl", [P, 2, D], F32R)
        draw = sb(s, "fdraw", [P, D])
        ah = sb(s, "ah", [P, 2, SEQ], F32R)
        al = sb(s, "al", [P, 2, SEQ], F32R)
        x_back = raw[:, :, :, :].rearrange("p k m n -> p (k m n)").rearrange("p (t n) -> p t n", n=D)
        act_t = sb(s, "act_t", [P, SEQ])
        down = sb(s, "down", [P, LT, D])
        stats = sb(s, "fstats", [P, LT])
        ps = s.enter_context(nc.psum_tensor("fps", [P, 8, 512], F32))
        flat = ps[:, :, :].rearrange("p b n -> p (b n)")
        psG, psU = flat[:, 0:1024], flat[:, 1024:2048]
        psD = [flat[:, 2048:3072], flat[:, 3072:4096]]
        raw_in, draw_in = ev("raw_in", 2, dma=True), ev("draw_in", dma=True)
        in_hi, in_lo, down_hi, down_lo = ev("in_hi"), ev("in_lo"), ev("down_hi"), ev("down_lo")
        product, silu, act_full, act_hi, act_lo = ev("product"), ev("silu"), ev("act_full"), ev("act_hi"), ev("act_lo")
        share, summed = ev("share", LT), ev("summed", LT)
        x_in = [sem(f"x_in{n}") for n in range(4)]
        zeroed, f_sq, f_root, f_inv, f_res, f_out = (sem(n) for n in (
            "zeroed", "f_sq", "f_root", "f_inv", "f_res", "f_out"))
        block = s.enter_context(nc.Block())
        w_in = S["w_ffn_in"].rearrange("(k p) (two n) -> p k two n", p=P, two=2)

        @block.sync
        def _(sp):
            with sp.Fori(0, HT // 2) as i:
                sp.wait_ge(in_lo.sem, in_lo.at(i * 2 - 1))
                for m in range(2):
                    sp.dma_start(raw[:, :, m, :], w_in[:, :, m, bass.ds(i * 2 * P, 2 * P)]).then_inc(raw_in.sem, 16)
                for u in range(2):
                    j = i * 2 + u
                    sp.wait_ge(down_lo.sem, down_lo.at(j - 1))
                    sp.dma_start(draw[:, :], S["w_ffn_out"][bass.ds(j * P, P), :]).then_inc(draw_in.sem, 16)
            sp.wait_ge(in_lo.sem, in_lo.at(HT - 1))
            for t in range(LT):
                if t >= 4:
                    sp.wait_ge(f_res, t - 3)
                sp.dma_start(x_back[:, t % 4, :], x2d[t * P:(t + 1) * P, :]).then_inc(x_in[t % 4], 16)
            for t in range(LT):
                sp.wait_ge(f_res, t + 1)
                sp.dma_start(S["out"][t * P:(t + 1) * P, :], down[:, t, :]).then_inc(f_out, 16)
            sp.wait_ge(f_out, 16 * LT)

        @block.gpsimd
        def _(pool):
            pool.memset(down[:, :, :], 0.0).then_inc(zeroed, 1)

        def steps(body):
            def run(eng):
                body(0, 0, 0)
                with eng.Fori(0, HT // 2 - 1) as i:
                    for u in range(2):
                        body(i * 2 + (u + 1), 1 - u, i + 1)
                body(HT - 1, 1, None)
            return run

        @block.scalar
        def _(act):
            for e in (in_hi, down_hi, silu, act_hi):
                e.open(act)

            def split_in(j, slot, pair):
                act.wait_ge(raw_in.sem, raw_in.at(pair))
                act.wait_ge(product.sem, product.at(j - 2))
                act.activation(wih[:, slot, :, :, :], raw[:, :, :, slot * P:(slot + 1) * P], ACT.Copy).then_inc(in_hi.sem, 1)

            def body(j, slot, pair):
                if pair is not None:
                    split_in(j + 1, 1 - slot, pair)
                act.wait_ge(draw_in.sem, draw_in.at(j))
                act.wait_ge(share.sem, share.at(j - 2))
                act.activation(wdh[:, slot, :], draw[:, :], ACT.Copy).then_inc(down_hi.sem, 1)
                act.wait_ge(product.sem, product.at(j))
                act.wait_ge(act_lo.sem, act_lo.at(j - 1))
                act.activation(act_t[:, :], psG, ACT.Silu).then_inc(silu.sem, 1)
                act.wait_ge(act_full.sem, act_full.at(j))
                act.activation(ah[:, slot, :], act_t[:, :], ACT.Copy).then_inc(act_hi.sem, 1)

            split_in(0, 0, 0)
            steps(body)(act)
            act.wait_ge(act_lo.sem, act_lo.at(HT - 1))
            for t in range(LT):
                act.wait_ge(summed.sem, summed.at(HT - 1, t + 1))
                if t:
                    act.wait_ge(f_sq, t)
                act.activation(act_t[:, :], down[:, t, :], ACT.Square, accum_out=stats[:, t:t + 1]).then_inc(f_sq, 1)
                act.wait_ge(f_sq, t + 1)
                act.activation(stats[:, t:t + 1], stats[:, t:t + 1], ACT.Sqrt, scale=1.0 / D, bias=epsb[:, :]).then_inc(f_root, 1)

        @block.vector
        def _(dve):
            for e in (in_lo, down_lo, act_full, act_lo, summed):
                e.open(dve)

            def split_in(j, slot):
                dve.wait_ge(in_hi.sem, in_hi.at(j))
                dve.tensor_tensor(wil[:, slot, :, :, :], raw[:, :, :, slot * P:(slot + 1) * P], wih[:, slot, :, :, :].bitcast(F32),
                                  ALU.subtract).then_inc(in_lo.sem, 1)

            def add(j, t):
                dve.wait_ge(share.sem, share.at(j, t + 1))
                dve.wait_ge(summed.sem, summed.at(j - 1, t + 1))
                dve.tensor_tensor(down[:, t, :], down[:, t, :], psD[t % 2], ALU.add).then_inc(summed.sem, 1)

            def body(j, slot, pair, adds=True):
                if pair is not None:
                    split_in(j + 1, 1 - slot)
                dve.wait_ge(down_hi.sem, down_hi.at(j))
                dve.tensor_tensor(wdl[:, slot, :], draw[:, :], wdh[:, slot, :].bitcast(F32), ALU.subtract).then_inc(down_lo.sem, 1)
                dve.wait_ge(silu.sem, silu.at(j))
                dve.tensor_tensor(act_t[:, :], act_t[:, :], psU, ALU.mult).then_inc(act_full.sem, 1)
                if adds:
                    for t in range(4):
                        add(j - 1, t)
                dve.wait_ge(act_hi.sem, act_hi.at(j))
                dve.tensor_tensor(al[:, slot, :], act_t[:, :], ah[:, slot, :].bitcast(F32), ALU.subtract).then_inc(act_lo.sem, 1)
                if adds:
                    for t in range(4, LT):
                        add(j - 1, t)

            def finish(t):
                dve.wait_ge(f_root, t + 1)
                dve.reciprocal(stats[:, t:t + 1], stats[:, t:t + 1]).then_inc(f_inv, 1)
                dve.wait_ge(f_inv, 2 * t + 1)
                dve.scalar_tensor_tensor(down[:, t, :], down[:, t, :], stats[:, t:t + 1], G2[:, :], ALU.mult, ALU.mult).then_inc(f_inv, 1)
                dve.wait_ge(f_inv, 2 * t + 2)
                dve.wait_ge(x_in[t % 4], 16 * (t // 4 + 1))
                dve.tensor_tensor(down[:, t, :], down[:, t, :], x_back[:, t % 4, :], ALU.add).then_inc(f_res, 1)

            dve.wait_ge(zeroed, 1)
            split_in(0, 0)
            body(0, 0, 0, adds=False)
            with dve.Fori(0, HT // 2 - 1) as i:
                for u in range(2):
                    body(i * 2 + (u + 1), 1 - u, i + 1)
            body(HT - 1, 1, None)
            for t in range(LT):
                add(HT - 1, t)
                if t:
                    finish(t - 1)
            finish(LT - 1)

        @block.tensor
        def _(pe):
            product.open(pe)
            share.open(pe)

            def gate_up(j, slot):
                pe.wait_ge(in_lo.sem, in_lo.at(j))
                pe.wait_ge(act_full.sem, act_full.at(j - 1))
                for m, bank in enumerate((psG, psU)):
                    for n in range(2):
                        c = 0
                        for k in range(KT):
                            for w, h in ((wih, h2h), (wih, h2l), (wil, h2h)):
                                mm = pe.matmul(bank[:, n * HALF:(n + 1) * HALF], w[:, slot, k, m, :], h[:, k, n * HALF:(n + 1) * HALF],
                                               start=(c == 0), stop=(c == 3 * KT - 1))
                                c += 1
                mm.then_inc(product.sem, 1)

            def down_share(j, slot):
                pe.wait_ge(act_lo.sem, act_lo.at(j))
                pe.wait_ge(down_lo.sem, down_lo.at(j))
                for t in range(LT):
                    pe.wait_ge(summed.sem, summed.at(j, t - 1) if t >= 2 else summed.at(j - 1, LT - 1 + t))
                    for n in range(2):
                        for c, (a, w) in enumerate(((ah, wdh), (al, wdh), (ah, wdl))):
                            mm = pe.matmul(psD[t % 2][:, n * 512:(n + 1) * 512], a[:, slot, t * P:(t + 1) * P],
                                           w[:, slot, n * 512:(n + 1) * 512], start=(c == 0), stop=(c == 2))
                    mm.then_inc(share.sem, 1)

            gate_up(0, 0)
            with pe.Fori(0, HT // 2 - 1) as i:
                for u in range(2):
                    j = i * 2 + (u + 1)
                    gate_up(j, 1 - u)
                    down_share(j - 1, u)
            gate_up(HT - 1, 1)
            down_share(HT - 2, 0)
            down_share(HT - 1, 1)


def kernel(**inputs):
    import concourse.bacc as bacc
    from concourse.bass_utils import run_bass_kernel_spmd

    a = {n: np.ascontiguousarray(v) for n, v in inputs.items()}
    consts, cosd, sind = constants()
    arrays = {
        "xall": np.concatenate([a["x"][0], a["ctx"][0]], axis=0), "c": a["c"][0], "c_ctx": a["c_ctx"],
        "w_ada": a["w_ada"][0], "b_ada": a["b_ada"][0], "g_pre_mix": a["g_pre_mix"][0], "g_post_mix": a["g_post_mix"][0],
        "g_pre_ffn": a["g_pre_ffn"][0], "g_post_ffn": a["g_post_ffn"][0], "w_in": a["w_in"][0], "attn_sink": a["attn_sink"][0],
        "w_gate_fwd": a["w_gate_fwd"][0], "b_gate_fwd": a["b_gate_fwd"][0], "w_gate_bwd": a["w_gate_bwd"][0],
        "b_gate_bwd": a["b_gate_bwd"][0], "g_gla": a["g_gla_norm"][0], "w_out": a["w_out"][0],
        "w_ffn_in": a["w_ffn_in"][0], "w_ffn_out": a["w_ffn_out"][0], "consts": consts, "cosd": cosd, "sind": sind,
    }
    nc = bacc.Bacc("TRN2", target_bir_lowering=False, num_devices=1)
    args = {n: nc.dram_tensor(f"in_{n}", v.shape, F32, kind="ExternalInput").ap() for n, v in arrays.items()}
    args["out"] = nc.dram_tensor("out_0", (SEQ, D), F32, kind="ExternalOutput").ap()
    for n, shape in (("proj", (TOK, COLS)), ("mixd", (SEQ, D)), ("x2d", (SEQ, D))):
        args[n] = nc.dram_tensor(f"scratch_{n}", shape, F32, kind=SCRATCH).ap()
    build(nc, **args)
    r = run_bass_kernel_spmd(nc, [{f"in_{n}": v for n, v in arrays.items()}], core_ids=[0])
    return r.results[0]["out_0"].reshape(1, SEQ, D)
```

```python
from contextlib import ExitStack

import numpy as np

import concourse.bass as bass
from concourse import mybir

ALU = mybir.AluOpType
ACT = mybir.ActivationFunctionType
F32 = mybir.dt.float32
F32R = mybir.dt.float32r
BF16 = mybir.dt.bfloat16
AX = mybir.AxisListType

P = 128
D = 1024
KT = D // P
SEQ = 1024
CTX = 256
TOK = SEQ + CTX
LT = SEQ // P
TT = TOK // P
HEAD = 64
AH, KVH = 8, 2
GH, DK = 8, 32
CHUNK = 64
NCH = SEQ // CHUNK
RANK = 16
TAU = 16.0
GRID_W = 64
ROPE_BASE = 10000.0
HID = 2816
HT = HID // P
EPS = 1e-6
NEG = -1e30
SCRATCH = "Internal"

GK, KK, VV, GV, GG2, ZZ, QQ, GQ, GG1 = 0, 256, 384, 512, 1024, 1280, 1312, 1824, 2080
COLS = 2336
W_Q, W_K, W_GQ, W_GK, W_GV, W_GG, W_Z = 0, 512, 768, 1024, 1280, 1792, 2304
CHUNKS = [[W_GK, W_K], [W_GV, W_GV + 256], [COLS - 512, COLS - 256], [W_Q, W_Q + 256], [W_GQ, W_GG]]
NARROW = COLS - (W_GG + 256)

C_ID, C_ONE, C_PREF_F, C_PREF_B, C_SUF_F, C_SUF_B, C_CTX_F, C_CTX_B, C_ALL, C_PREV, C_NEXT, C_IND = [P * n for n in range(12)]
C_HEAD = C_IND + 2
C_COLS = C_HEAD + 4


def constants():
    j, i = np.arange(P)[:, None], np.arange(P)[None, :]
    same = (j // CHUNK) == (i // CHUNK)
    c = np.zeros((P, C_COLS), np.float32)
    inv = 1.0 / TAU
    c[:, C_ID:C_ID + P] = j == i
    c[:, C_ONE:C_ONE + P] = 1.0
    c[:, C_PREF_F:C_PREF_F + P] = ((j <= i) & same) * inv
    c[:, C_PREF_B:C_PREF_B + P] = ((j >= i) & same) * inv
    c[:, C_SUF_F:C_SUF_F + P] = ((j > i) & same) * inv
    c[:, C_SUF_B:C_SUF_B + P] = ((j < i) & same) * inv
    c[:, C_CTX_F:C_CTX_F + P] = (j > i) * inv
    c[:, C_CTX_B:C_CTX_B + P] = (j < i) * inv
    c[:, C_ALL:C_ALL + P] = inv
    c[:, C_PREV:C_PREV + P] = np.where(i >= j, 0.0, NEG)
    c[:, C_NEXT:C_NEXT + P] = np.where(i <= j, 0.0, NEG)
    c[:, C_IND] = (np.arange(P) < CHUNK) * inv
    c[:, C_IND + 1] = (np.arange(P) >= CHUNK) * inv
    c[:, C_HEAD:C_COLS] = (np.arange(P) // DK)[:, None] == np.arange(4)
    tok = np.arange(SEQ)
    half = HEAD // 2
    freq = (np.float32(ROPE_BASE) ** (-np.arange(0, half, 2, dtype=np.float32) / np.float32(half))).astype(np.float32)
    ar = (tok // GRID_W).astype(np.float32)[:, None] * freq
    ac = (tok % GRID_W).astype(np.float32)[:, None] * freq
    cos = np.ones((TOK, HEAD), np.float32)
    sin = np.zeros((TOK, HEAD), np.float32)
    cos[:SEQ] = np.cos(np.concatenate([ar, ar, ac, ac], 1))
    sin[:SEQ] = np.sin(np.concatenate([-ar, ar, -ac, ac], 1))
    tile = lambda a: np.ascontiguousarray(a.reshape(TT, P, HEAD).transpose(1, 0, 2).reshape(P, TT * HEAD))
    return c, tile(cos), tile(sin)


class Event:

    def __init__(self, nc, ctx, name, per=1, dma=False, credit=None):
        self.sem = ctx.enter_context(nc.semaphore(name))
        self.per = per * (16 if dma else 1)
        self.one = 16 if dma else 1
        self.credit = credit if credit is not None else 0 if dma else 2

    def open(self, eng):
        eng.sem_inc(self.sem, self.credit * self.per)

    def at(self, t, k=None):
        return (t + self.credit) * self.per + (self.per if k is None else k * self.one)


def build(nc, xall, c, c_ctx, w_ada, b_ada, g_pre_mix, g_post_mix, g_pre_ffn, g_post_ffn, w_in, attn_sink,
          w_gate_fwd, b_gate_fwd, w_gate_bwd, b_gate_bwd, g_gla, w_out, w_ffn_in, w_ffn_out, consts, cosd, sind, out,
          proj, mixd, x2d):
    top = ExitStack()
    with top:
        persist(nc, top, locals())


def persist(nc, top, A):
    def sb(stack, name, shape, dt=F32):
        return stack.enter_context(nc.sbuf_tensor(name, shape, dt))

    S = dict(A)
    S["sb"] = sb
    S["con"] = sb(top, "con", [P, C_COLS])
    S["pcol"] = sb(top, "pcol", [P, 80])
    S["A1"] = sb(top, "A1", [P, KT, 2])
    S["B1"] = sb(top, "B1", [P, 16, 2])
    S["A2"] = sb(top, "A2", [P, KT])
    S["B2"] = sb(top, "B2", [P, 16])
    S["G1"] = sb(top, "G1", [P, D])
    S["G2"] = sb(top, "G2", [P, D])
    S["epsb"] = sb(top, "epsb", [P, 1])
    S["scol"] = sb(top, "scol", [P, 16])
    with ExitStack() as s:
        S["hTh"] = sb(s, "hTh", [P, KT, TOK], F32R)
        S["hTl"] = sb(s, "hTl", [P, KT, TOK], F32R)
        S["raw"] = sb(s, "raw", [P, 2, 4, 512])
        S["raw_in"] = [s.enter_context(nc.semaphore(f"p_raw_in{n}")) for n in range(2)]
        modulate_block(nc, S)
        project_block(nc, S)
    with ExitStack() as s:
        S["cos"] = sb(s, "cos", [P, TT, HEAD])
        S["sin"] = sb(s, "sin", [P, TT, HEAD])
        S["keyT"] = sb(s, "keyT", [P, 2, KVH, (TT + 1) * P], F32R)
        S["val"] = sb(s, "val", [P, TT + 1, P])
        S["la"] = sb(s, "la", [P, TT, 512])
        S["state"] = sb(s, "state", [P, 4, TOK // CHUNK, HEAD])
        S["fin"] = sb(s, "fin", [P, 4, HEAD])
        keys_block(nc, S)
        mix_block(nc, S)
    with ExitStack() as s:
        S["h2h"] = sb(s, "h2h", [P, KT, SEQ], F32R)
        S["h2l"] = sb(s, "h2l", [P, KT, SEQ], F32R)
        output_block(nc, S)
        ffn_block(nc, S)


def modulate_block(nc, S):
    sb, con, pcol, A1, B1, scol, epsb = (S[n] for n in ("sb", "con", "pcol", "A1", "B1", "scol", "epsb"))
    hTh, hTl, raw = S["hTh"], S["hTl"], S["raw"]
    with ExitStack() as s:
        def sem(name):
            return s.enter_context(nc.semaphore("m_" + name))
        WS, XS = 3, 4
        prow = sb(s, "prow", [80, P])
        wada = sb(s, "wada", [P, WS, 2 * D])
        xin = sb(s, "xin", [P, XS, D])
        junk = sb(s, "junk", [P, D])
        ssq = sb(s, "ssq", [P, TT])
        rst = sb(s, "rst", [P, TT])
        xnT = sb(s, "xnT", [P, KT, TOK])
        modrow = sb(s, "modrow", [2, 2 * D])
        psA = s.enter_context(nc.psum_tensor("psA", [P, 4, 512], F32))
        psX = s.enter_context(nc.psum_tensor("psX", [P, 4, 512], F32))
        rows_in, con_in, eps_set = sem("rows_in"), sem("con_in"), sem("eps_set")
        ada_in, x_in = [sem(f"ada_in{n}") for n in range(WS)], [sem(f"x_in{n}") for n in range(XS)]
        rows_turned, cols_ready, silu_ready = sem("rows_turned"), sem("cols_ready"), sem("silu_ready")
        ada_used, mod_row, mod_turned, mod_col = sem("ada_used"), sem("mod_row"), sem("mod_turned"), sem("mod_col")
        squares, root, rstd, normed, turned, turned_out = (sem(n) for n in ("squares", "root", "rstd", "normed", "turned", "turned_out"))
        full, hi, lo = sem("full"), sem("hi"), [sem("lo_dve"), sem("lo_pool")]
        POOL_K = (2, 5)
        block = s.enter_context(nc.Block())

        @block.sync
        def _(sp):
            rows = [(S["c"], 0, 8), (S["c_ctx"], 8, 8), (S["g_pre_mix"], 16, 8), (S["g_pre_ffn"], 24, 8), (S["b_ada"], 32, 48)]
            for src, r, n in rows:
                sp.dma_start(prow[r:r + n, :], src.rearrange("(r p) -> r p", p=P)).then_inc(rows_in, 16)
            sp.dma_start(con[:, :], S["consts"]).then_inc(con_in, 16)
            for t in range(TT):
                if t < KT:
                    if t >= WS:
                        sp.wait_ge(ada_used, t - WS + 1)
                    sp.dma_start(wada[:, t % WS, :], S["w_ada"][t * P:(t + 1) * P, 0:2 * D]).then_inc(ada_in[t % WS], 16)
                if t >= XS:
                    sp.wait_ge(turned, t - XS + 1)
                sp.dma_start(xin[:, t % XS, :], S["xall"][t * P:(t + 1) * P, :]).then_inc(x_in[t % XS], 16)
            load_chunk(sp, S, 0, 0)
            load_chunk(sp, S, 0, 1)

        @block.scalar
        def _(act):
            act.wait_ge(cols_ready, 1)
            act.activation(scol[:, :], pcol[:, 0:16], ACT.Silu).then_inc(silu_ready, 1)
            act.wait_ge(eps_set, 1)

            def evacuate(t):
                act.wait_ge(turned, t + 1)
                act.activation(xnT[:, :, t * P:(t + 1) * P], psX[:, 2 * (t % 2):2 * (t % 2) + 2, :].rearrange("p b (k j) -> p (b k) j", j=P),
                               ACT.Copy).then_inc(turned_out, 1)
            for t in range(TT):
                act.wait_ge(squares, t + 1)
                act.activation(rst[:, t:t + 1], ssq[:, t:t + 1], ACT.Sqrt, scale=1.0 / D, bias=epsb[:, :]).then_inc(root, 1)
                if t:
                    evacuate(t - 1)
            evacuate(TT - 1)
            for k in range(KT):
                act.wait_ge(full, k + 1)
                act.activation(hTh[:, k, :], xnT[:, k, :], ACT.Copy).then_inc(hi, 1)

        @block.gpsimd
        def _(pool):
            for k in POOL_K:
                pool.wait_ge(hi, k + 1)
                pool.tensor_tensor(hTl[:, k, :], xnT[:, k, :], hTh[:, k, :].bitcast(F32), ALU.subtract).then_inc(lo[1], 1)

        @block.tensor
        def _(pe):
            pe.wait_ge(rows_in, 80)
            pe.wait_ge(con_in, 16)
            pe.transpose(psA[:, 0, 0:80], prow[:, :], con[0:80, C_ID:C_ID + 80]).then_inc(rows_turned, 1)
            pe.wait_ge(silu_ready, 1)
            lhs = scol[:, :].rearrange("p (w k) -> p k w", w=2)
            for t in range(TT):
                if t < KT:
                    pe.wait_ge(ada_in[t % WS], 16 * (t // WS + 1))
                    for n in range(4):
                        mm = pe.matmul(psA[0:2, n, :], lhs[:, t, :], wada[:, t % WS, n * 512:(n + 1) * 512],
                                       start=(t == 0), stop=(t == KT - 1))
                    mm.then_inc(ada_used, 1)
                pe.wait_ge(normed, t + 1)
                if t >= 2:
                    pe.wait_ge(turned_out, t - 1)
                for k in range(KT):
                    mm = pe.transpose(psX[:, 2 * (t % 2) + k // 4, (k % 4) * P:(k % 4 + 1) * P], xin[:, t % XS, k * P:(k + 1) * P],
                                      con[:, C_ID:C_ID + P])
                mm.then_inc(turned, 1)
                if t == KT:
                    pe.wait_ge(mod_row, 1)
                    for n in range(16):
                        mm = pe.transpose(psA[:, 0, 2 * n:2 * n + 2], modrow[:, n * P:(n + 1) * P], con[0:2, C_ID:C_ID + 2])
                    mm.then_inc(mod_turned, 1)

        @block.vector
        def _(dve):
            dve.memset(epsb[:, :], EPS).then_inc(eps_set, 1)
            dve.wait_ge(rows_turned, 1)
            dve.tensor_copy(pcol[:, :], psA[:, 0, 0:80]).then_inc(cols_ready, 1)

            def square(t):
                dve.wait_ge(x_in[t % XS], 16 * (t // XS + 1))
                if t:
                    dve.wait_ge(squares, t)
                dve.tensor_tensor_reduce(out=junk[:, :], in0=xin[:, t % XS, :], in1=xin[:, t % XS, :], scale=1.0, scalar=0.0,
                                         op0=ALU.mult, op1=ALU.add, accum_out=ssq[:, t:t + 1]).then_inc(squares, 1)

            square(0)
            for t in range(TT):
                if t < TT - 1:
                    square(t + 1)
                dve.wait_ge(root, t + 1)
                dve.reciprocal(rst[:, t:t + 1], rst[:, t:t + 1]).then_inc(rstd, 1)
                dve.wait_ge(rstd, t + 1)
                dve.tensor_scalar(xin[:, t % XS, :], xin[:, t % XS, :], rst[:, t:t + 1], None, ALU.mult).then_inc(normed, 1)
                if t == KT - 1:
                    dve.wait_ge(ada_used, KT)
                    dve.tensor_copy(modrow[:, :], psA[0:2, :, :].rearrange("p b n -> p (b n)")).then_inc(mod_row, 1)
            dve.wait_ge(mod_turned, 1)
            dve.tensor_tensor(B1[:, :, :], psA[:, 0, 0:32].rearrange("p (n w) -> p n w", w=2),
                              pcol[:, 32:48].unsqueeze(2).broadcast_to([P, 16, 2]), ALU.add).then_inc(mod_col, 1)
            dve.wait_ge(mod_col, 1)
            dve.scalar_tensor_tensor(A1[:, :, :], B1[:, 8:16, :], 1.0,
                                     pcol[:, 16:24].unsqueeze(2).broadcast_to([P, 8, 2]), ALU.add, ALU.mult).then_inc(mod_col, 1)
            dve.wait_ge(mod_col, 2)
            dve.wait_ge(turned_out, TT)

            def low(k):
                if k not in POOL_K:
                    dve.wait_ge(hi, k + 1)
                    dve.tensor_tensor(hTl[:, k, :], xnT[:, k, :], hTh[:, k, :].bitcast(F32), ALU.subtract).then_inc(lo[0], 1)
            for k in range(KT):
                dve.tensor_scalar(xnT[:, k, 0:SEQ], xnT[:, k, 0:SEQ], A1[:, k, 0:1], B1[:, k, 0:1], ALU.mult, ALU.add)
                dve.tensor_scalar(xnT[:, k, SEQ:TOK], xnT[:, k, SEQ:TOK], A1[:, k, 1:2], B1[:, k, 1:2], ALU.mult, ALU.add).then_inc(full, 1)
                if k >= 2:
                    low(k - 2)
            low(KT - 2)
            low(KT - 1)


def load_chunk(sp, S, ci, half):
    for n, first in enumerate(CHUNKS[ci]):
        sp.dma_start(S["raw"][:, half, :, n * 256:(n + 1) * 256],
                     S["w_in"].rearrange("(k p) n -> p k n", p=P)[:, 4 * half:4 * half + 4, first:first + 256]
                     ).then_inc(S["raw_in"][half], 16)


def project_block(nc, S):
    sb, con, pcol, scol = (S[n] for n in ("sb", "con", "pcol", "scol"))
    hTh, hTl, A2, B2, G1, G2, proj = (S[n] for n in ("hTh", "hTl", "A2", "B2", "G1", "G2", "proj"))
    with ExitStack() as s:
        def sem(name):
            return s.enter_context(nc.semaphore("p_" + name))
        wh = sb(s, "wh", [P, 2, KT, 512], F32R)
        wl = sb(s, "wl", [P, 2, KT, 512], F32R)
        raw, raw_in = S["raw"], S["raw_in"]
        acc = sb(s, "acc", [P, 4 * D])
        ada = sb(s, "ada", [P, 2, 2 * D])
        stage = G2[:, :].rearrange("p (s n) -> p s n", s=2)
        psW = s.enter_context(nc.psum_tensor("psW", [P, 2, 512], F32))
        psG = s.enter_context(nc.psum_tensor("psG", [P, 4, 512], F32))
        psC = s.enter_context(nc.psum_tensor("psC", [P, 512], F32))
        ada_in = [sem(f"ada_in{n}") for n in range(2)]
        acc_zero, acc_step, rows, gate_sum, cols_done, gates = (sem(n) for n in ("acc_zero", "acc_step", "rows", "gate_sum", "cols_done", "gates"))
        hi, lo = sem("hi"), sem("lo")
        done, copied = Event(nc, s, "p_done"), Event(nc, s, "p_copied")
        stored = [Event(nc, s, f"p_stored{u}", dma=True, credit=1) for u in range(2)]
        block = s.enter_context(nc.Block())
        FIRST = [0, 10, 20, 30, 38]
        END = 46

        def width(ci, t):
            return 512 if not isinstance(ci, int) or ci != 2 else NARROW if t < LT else 2 * RANK

        @block.sync
        def _(sp):
            n_ada = 0

            def ada_piece(n):
                if n >= 2:
                    sp.wait_ge(acc_step, n)
                k, h = n // 2, n % 2
                sp.dma_start(ada[:, n % 2, :], S["w_ada"][k * P:(k + 1) * P, (2 + 2 * h) * D:(4 + 2 * h) * D]).then_inc(ada_in[n % 2], 16)

            for ci in range(1, len(CHUNKS)):
                for half in range(2):
                    sp.wait_ge(lo, 2 * ci + half - 1)
                    load_chunk(sp, S, ci, half)
                    for _ in range(2):
                        ada_piece(n_ada)
                        n_ada += 1
            assert n_ada == 16
            for n, (col, gain) in enumerate(((2 * D, S["g_post_mix"]), (5 * D, S["g_post_ffn"]))):
                sp.wait_ge(acc_step, 16 + n)
                sp.dma_start(ada[:, n, 0:D], S["b_ada"][col:col + D].partition_broadcast(P)).then_inc(rows, 16)
                sp.dma_start(ada[:, n, D:2 * D], gain.partition_broadcast(P)).then_inc(rows, 16)

        @block.scalar
        def _(act):
            copied.open(act)
            for u in range(2):
                stored[u].open(act)

            def high(ci, half, slot, before):
                act.wait_ge(raw_in[half], ci * 32 + 32)
                act.wait_ge(done.sem, done.at(before - 1))
                act.activation(wh[:, bass.ds(slot, 1), 4 * half:4 * half + 4, :].rearrange("p s k n -> p (s k) n"),
                               raw[:, half, :, :], ACT.Copy).then_inc(hi, 1)

            def chunk(ci, g0, used, tiles, slot, col, nxt=True):
                for t in range(tiles):
                    n = width(ci, t)
                    act.wait_ge(done.sem, done.at(g0 + t))
                    act.wait_ge(stored[t % 2].sem, stored[t % 2].at(used + (t // 2 - 1)))
                    last = ci if isinstance(ci, int) else -1
                    g = slice(0, 256) if last == 2 and n == NARROW else slice(256, 512) if last == 4 else slice(0, 0)
                    if g.stop:
                        act.activation(stage[:, t % 2, g], psW[:, t % 2, g], ACT.Silu)
                    r = slice(0, 256) if g.start else slice(g.stop, n)
                    act.activation(stage[:, t % 2, r], psW[:, t % 2, r], ACT.Copy).then_inc(copied.sem, 1)
                    act.wait_ge(copied.sem, copied.at(g0 + t))
                    c0 = ZZ if n == 2 * RANK else col
                    act.dma_start(proj[t * P:(t + 1) * P, bass.ds(c0, n)], stage[:, t % 2, 0:n]).then_inc(stored[t % 2].sem, 16)
                    if nxt and t in (1, 4):
                        high(ci + 1, t // 4, slot, g0)

            high(0, 0, 0, 0)
            high(0, 1, 0, 0)
            with act.Fori(0, 2) as i:
                slot = act.snap(i * -1 + 1)
                chunk(i, i * 10, i * 5, TT, slot, act.snap(i * 512))
            chunk(2, FIRST[2], FIRST[2] // 2, TT, 1, GG2)
            chunk(3, FIRST[3], FIRST[3] // 2, LT, 0, QQ)
            chunk(4, FIRST[4], FIRST[4] // 2, LT, 0, GQ, False)
            for u in range(2):
                act.wait_ge(stored[u].sem, stored[u].at(END // 2 - 1))

        @block.vector
        def _(dve):
            dve.memset(acc[:, :], 0.0).then_inc(acc_step, 1)
            steps = [0]

            def low(ci, half):
                dve.wait_ge(hi, 2 * ci + half + 1)
                dve.tensor_tensor(wl[:, ci % 2, 4 * half:4 * half + 4, :], raw[:, half, :, :],
                                  wh[:, ci % 2, 4 * half:4 * half + 4, :].bitcast(F32), ALU.subtract).then_inc(lo, 1)

            def ada_step():
                n = steps[0]
                k, h = n // 2, n % 2
                dve.wait_ge(ada_in[n % 2], 16 * (n // 2 + 1))
                dve.wait_ge(acc_step, n + 1)
                a = acc[:, h * 2 * D:(h + 1) * 2 * D]
                dve.scalar_tensor_tensor(a, ada[:, n % 2, :], scol[:, k:k + 1], a, ALU.mult, ALU.add).then_inc(acc_step, 1)
                steps[0] += 1

            low(0, 0)
            low(0, 1)
            for ci in range(1, 5):
                for half in range(2):
                    low(ci, half)
                    ada_step()
                    ada_step()
            dve.wait_ge(gate_sum, 1)
            dve.wait_ge(rows, 64)
            for u in range(2):
                dve.wait_ge(stored[u].sem, stored[u].at(END // 2 - 1))
            for n, G in enumerate((G1, G2)):
                dve.tensor_tensor(G[:, :], psG[:, 2 * n:2 * n + 2, :].rearrange("p b n -> p (b n)"), ada[:, n, 0:D], ALU.add).then_inc(gates, 1)
            dve.tensor_tensor(B2[:, :], psC[:, 0:16], pcol[:, 32 + 24:32 + 40], ALU.add).then_inc(gates, 1)
            dve.wait_ge(gates, 3)
            for n, G in enumerate((G1, G2)):
                dve.tensor_tensor(G[:, :], G[:, :], ada[:, n, D:2 * D], ALU.mult)
            dve.scalar_tensor_tensor(A2[:, :], B2[:, 8:16], 1.0, pcol[:, 24:32], ALU.add, ALU.mult)

        @block.tensor
        def _(pe):
            done.open(pe)

            def tile(ci_sem, g, t, w, col, n):
                if t == 0:
                    pe.wait_ge(lo, ci_sem)
                pe.wait_ge(copied.sem, copied.at(g - 2))
                m = 0
                for k in range(KT):
                    for a, b in ((hTh, wh), (hTl, wh), (hTh, wl)):
                        mm = pe.matmul(psW[:, t % 2, 0:n], a[:, k, t * P:(t + 1) * P], b[:, bass.ds(w, 1), k, col:col + n].rearrange("p s n -> p (s n)"),
                                       start=(m == 0), stop=(m == 3 * KT - 1))
                        m += 1
                mm.then_inc(done.sem, 1)

            with pe.Fori(0, 2) as i:
                for t in range(TT):
                    tile(i * 2 + 2, i * 10 + t, t, i, 0, 512)
            for t in range(TT):
                n = NARROW if t < LT else 2 * RANK
                tile(6, FIRST[2] + t, t, 0, 512 - n, n)
            with pe.Fori(0, 2) as i:
                slot = pe.snap(i * -1 + 1)
                for t in range(LT):
                    tile(i * 2 + 8, i * 8 + FIRST[3] + t, t, slot, 0, 512)
            pe.wait_ge(acc_step, 17)
            one = con[:, C_ONE:C_ONE + P]
            for n in range(4):
                col = (0 if n < 2 else 3 * D) + (n % 2) * 512
                pe.matmul(psG[:, n, :], one, acc[:, col:col + 512], start=True, stop=True)
            for n in range(16):
                mm = pe.matmul(psC[:, n:n + 1], acc[:, D + n * P:D + (n + 1) * P], con[:, C_ONE:C_ONE + 1], start=True, stop=True)
            mm.then_inc(gate_sum, 1)


def rope(pool, rotated, t, x, cos, sin, rot, rot2, heads):
    def table(a):
        return a[:, bass.ds(t, 1), :]
    pool.tensor_tensor(rot[:, :, :], x, table(cos).broadcast_to([P, heads, HEAD]), ALU.mult).then_inc(rotated.sem, 1)
    halves = x.rearrange("p h (a b d) -> p h a b d", a=2, b=2)
    out = rot2[:, :, :].rearrange("p h (a b d) -> p h a b d", a=2, b=2)
    signed = table(sin).rearrange("p s (a b d) -> p s a b d", a=2, b=2)
    for b in range(2):
        pool.tensor_tensor(out[:, :, :, b, :], halves[:, :, :, 1 - b, :],
                           signed[:, :, :, b, :].broadcast_to([P, heads, 2, HEAD // 4]), ALU.mult).then_inc(rotated.sem, 1)
    pool.wait_ge(rotated.sem, rotated.at(t, 3))
    pool.tensor_tensor(rot[:, :, :], rot[:, :, :], rot2[:, :, :], ALU.add).then_inc(rotated.sem, 1)


def keys_block(nc, S):
    sb, con, proj = S["sb"], S["con"], S["proj"]
    cos, sin, keyT, val, la, state, fin = (S[n] for n in ("cos", "sin", "keyT", "val", "la", "state", "fin"))
    with ExitStack() as s:
        def sem(name):
            return s.enter_context(nc.semaphore("k_" + name))

        def ev(name, per=1, dma=False):
            return Event(nc, s, "k_" + name, per, dma)
        wg = sb(s, "wg", [33, 512])
        row = sb(s, "krow", [P, 2, D])
        z = sb(s, "z", [P, 2, 2 * RANK])
        zT = sb(s, "zT", [33, 2, P])
        rot = sb(s, "rot", [P, KVH, HEAD])
        rot2 = sb(s, "rot2", [P, KVH, HEAD])
        kdup = sb(s, "kdup", [P, 2, KVH, 2, HEAD], F32R)
        mag = sb(s, "mag", [P, 512])
        lat = sb(s, "lat", [P, 2, 512])
        grow = sb(s, "grow", [P, 2, 512])
        kd = sb(s, "kd", [P, 2, 2, 256])
        dec = sb(s, "dec", [P, 4, TOK // CHUNK])
        prev = sb(s, "prev", [P, 2, 4, HEAD])
        ps = s.enter_context(nc.psum_tensor("kps", [P, 8, 512], F32))
        psZ, psL, psK, psU, psN, psD = (ps[:, n, :] for n in range(6))
        psS = ps[:, 6:8, 0:256]
        consts_in, wg_zero, wg_in, ones_set = sem("consts_in"), sem("wg_zero"), sem("wg_in"), sem("ones_set")
        row_in = [ev(f"row_in{u}", dma=True) for u in range(2)]
        z_in = [ev(f"z_in{u}", dma=True) for u in range(2)]
        rotated, k_split = ev("rotated", 4), ev("k_split", 4)
        k_turned, k_out = ev("k_turned"), ev("k_out")
        z_turned, z_out, logits = ev("z_turned"), ev("z_out"), ev("logits")
        softplus, decays = ev("softplus", 3), ev("decays")
        kept = ev("kept", 2)
        sums, grown, scaled = ev("sums"), ev("grown", 2), ev("scaled")
        added, moved = ev("added"), ev("moved")
        ctx_sum, ctx_exp, ctx_k, ctx_state, ctx_out, scan = (sem(n) for n in ("ctx_sum", "ctx_exp", "ctx_k", "ctx_state", "ctx_out", "scan"))
        block = s.enter_context(nc.Block())

        @block.sync
        def _(sp):
            sp.dma_start(cos[:, :, :], S["cosd"].rearrange("p (t d) -> p t d", d=HEAD)).then_inc(consts_in, 16)
            sp.dma_start(sin[:, :, :], S["sind"].rearrange("p (t d) -> p t d", d=HEAD)).then_inc(consts_in, 16)
            sp.wait_ge(wg_zero, 1)
            for d, (w, b) in enumerate((("w_gate_fwd", "b_gate_fwd"), ("w_gate_bwd", "b_gate_bwd"))):
                sp.dma_start(wg[d * RANK:(d + 1) * RANK, d * 256:(d + 1) * 256], S[w]).then_inc(wg_in, 16)
                sp.dma_start(wg[32:33, d * 256:(d + 1) * 256], S[b].rearrange("(a n) -> a n", a=1)).then_inc(wg_in, 16)
            with sp.Fori(0, TT // 2) as i:
                for u in range(2):
                    t = sp.snap(i * 2 + u)
                    sp.wait_ge(added.sem, added.at(t - 2))
                    sp.wait_ge(kept.sem, kept.at(t - 2))
                    sp.wait_ge(scaled.sem, scaled.at(t - 2))
                    sp.wait_ge(rotated.sem, rotated.at(t - 2))
                    sp.wait_ge(z_turned.sem, z_turned.at(t - 2))
                    sp.dma_start(row[:, u, :], proj[bass.ds(t * P, P), 0:D]).then_inc(row_in[u].sem, 16)
                    sp.dma_start(z[:, u, :], proj[bass.ds(t * P, P), ZZ:ZZ + 2 * RANK]).then_inc(z_in[u].sem, 16)

        @block.gpsimd
        def _(pool):
            rotated.open(pool)
            kept.open(pool)
            pool.wait_ge(consts_in, 32)
            with pool.Fori(0, TT // 2) as i:
                for u in range(2):
                    t = i * 2 + u
                    k = row[:, u, KK:KK + P].rearrange("p (h d) -> p h d", h=KVH)
                    pool.wait_ge(row_in[u].sem, row_in[u].at(i))
                    pool.wait_ge(k_split.sem, k_split.at(t - 1))
                    rope(pool, rotated, t, k, cos, sin, rot, rot2, KVH)
                    pool.tensor_copy(val[:, bass.ds(t + 1, 1), :].rearrange("p s d -> p (s d)"), row[:, u, VV:VV + P]).then_inc(kept.sem, 1)
                    pool.wait_ge(decays.sem, decays.at(t))
                    pool.tensor_copy(la[:, bass.ds(t, 1), :].rearrange("p s d -> p (s d)"), lat[:, u, :]).then_inc(kept.sem, 1)

        @block.scalar
        def _(act):
            for e in (softplus, grown, added):
                e.open(act)
            with act.Fori(0, TT // 2) as i:
                for u in range(2):
                    t = i * 2 + u
                    act.wait_ge(logits.sem, logits.at(t))
                    act.wait_ge(decays.sem, decays.at(t - 1))
                    act.activation(mag[:, :], psL, ACT.Abs).then_inc(softplus.sem, 1)
                    act.wait_ge(softplus.sem, softplus.at(t, 1))
                    act.activation(mag[:, :], mag[:, :], ACT.Exp, scale=-1.0).then_inc(softplus.sem, 1)
                    act.wait_ge(softplus.sem, softplus.at(t, 2))
                    act.activation(mag[:, :], mag[:, :], ACT.Ln, bias=1.0).then_inc(softplus.sem, 1)
                    act.wait_ge(sums.sem, sums.at(t))
                    act.wait_ge(scaled.sem, scaled.at(t - 2))
                    act.activation(grow[:, u, :], psU, ACT.Exp).then_inc(grown.sem, 1)
                    act.wait_ge(moved.sem, moved.at(t))
                    act.activation(dec[:, :, bass.ds(t * 2, 2)], psD[:, 0:8].rearrange("p (q c) -> p q c", q=4), ACT.Exp).then_inc(grown.sem, 1)
                    act.activation(state[:, :, bass.ds(t * 2, 2), :].rearrange("p q c d -> p c q d"),
                                   psS.rearrange("p c (q d) -> p c q d", q=4), ACT.Copy).then_inc(added.sem, 1)
            act.wait_ge(ctx_sum, 1)
            act.wait_ge(scaled.sem, scaled.at(TT - 1))
            act.activation(grow[:, 0, :], psU, ACT.Exp).then_inc(ctx_exp, 1)
            act.activation(grow[:, 1, :], psN, ACT.Exp).then_inc(ctx_exp, 1)
            act.wait_ge(ctx_state, 1)
            act.activation(fin[:, :, :], psS[:, 0, :].rearrange("p (q d) -> p q d", q=4), ACT.Copy).then_inc(ctx_out, 1)

        @block.vector
        def _(dve):
            for e in (k_split, k_out, z_out, decays, scaled):
                e.open(dve)
            dve.memset(wg[:, :], 0.0).then_inc(wg_zero, 1)
            dve.memset(zT[32:33, :, :], 1.0).then_inc(ones_set, 1)
            dve.memset(val[:, 0, :], 0.0).then_inc(ones_set, 1)
            dve.memset(keyT[:, :, :, 0:P].bitcast(F32), 0.0).then_inc(ones_set, 1)
            with dve.Fori(0, TT // 2) as i:
                for u in range(2):
                    t = i * 2 + u
                    dve.wait_ge(z_turned.sem, z_turned.at(t))
                    dve.wait_ge(logits.sem, logits.at(t - 2))
                    dve.tensor_copy(zT[0:32, u, :], psZ[0:32, 0:P]).then_inc(z_out.sem, 1)
                    dve.wait_ge(rotated.sem, rotated.at(t))
                    dve.wait_ge(k_turned.sem, k_turned.at(t - 1))
                    for c in range(2):
                        dve.tensor_copy(kdup[:, 0, :, c, :], rot[:, :, :]).then_inc(k_split.sem, 1)
                    dve.wait_ge(k_split.sem, k_split.at(t, 2))
                    for c in range(2):
                        dve.tensor_tensor(kdup[:, 1, :, c, :], rot[:, :, :], kdup[:, 0, :, c, :].bitcast(F32), ALU.subtract).then_inc(k_split.sem, 1)
                    dve.wait_ge(softplus.sem, softplus.at(t))
                    dve.wait_ge(kept.sem, kept.at(t - 2))
                    dve.wait_ge(moved.sem, moved.at(t - 2))
                    dve.scalar_tensor_tensor(lat[:, u, :], psL, 0.0, mag[:, :], ALU.min, ALU.subtract).then_inc(decays.sem, 1)
                    dve.wait_ge(k_turned.sem, k_turned.at(t))
                    dve.tensor_copy(keyT[:, :, :, bass.ds(t * P + P, P)],
                                    psK.rearrange("p (s h j) -> p s h j", s=2, h=KVH)).then_inc(k_out.sem, 1)
                    dve.wait_ge(grown.sem, grown.at(t, 1))
                    dve.wait_ge(moved.sem, moved.at(t - 2))
                    dve.tensor_tensor(kd[:, u, :, :], grow[:, u, :].rearrange("p (d n) -> p d n", d=2),
                                      row[:, u, GK:GK + 256].unsqueeze(1).broadcast_to([P, 2, 256]), ALU.mult).then_inc(scaled.sem, 1)
            dve.wait_ge(ctx_exp, 2)
            dve.wait_ge(moved.sem, moved.at(TT - 1))
            for u in range(2):
                dve.tensor_tensor(kd[:, u, :, :], grow[:, u, :].rearrange("p (d n) -> p d n", d=2),
                                  row[:, u, GK:GK + 256].unsqueeze(1).broadcast_to([P, 2, 256]), ALU.mult).then_inc(ctx_k, 1)
            dve.wait_ge(ctx_out, 1)
            dve.tensor_copy(prev[:, 0, :, :], fin[:, :, :]).then_inc(scan, 1)
            dve.wait_ge(added.sem, added.at(TT - 1))
            dve.wait_ge(grown.sem, grown.at(TT - 1))
            dve.wait_ge(scan, 1)
            with dve.Fori(0, NCH // 2) as i:
                for u in range(2):
                    n = i * 2 + u
                    for q in range(4):
                        c = n if q < 2 else n * -1 + (NCH - 1)
                        dve.scalar_tensor_tensor(prev[:, 1 - u, q, :], prev[:, u, q, :], dec[:, q, bass.ds(c, 1)],
                                                 state[:, q, bass.ds(c, 1), :].rearrange("p s d -> p (s d)"), ALU.mult, ALU.add)\
                           .then_inc(scan, 1)
                    dve.wait_ge(scan, n * 8 + 5)
                    for q in range(4):
                        c = n if q < 2 else n * -1 + (NCH - 1)
                        dve.tensor_scalar(state[:, q, bass.ds(c, 1), :].rearrange("p s d -> p (s d)"), prev[:, u, q, :], 1.0, None, ALU.mult).then_inc(scan, 1)
                    dve.wait_ge(scan, n * 8 + 9)

        @block.tensor
        def _(pe):
            for e in (k_turned, z_turned, logits, sums, moved):
                e.open(pe)
            ident = con[:, C_ID:C_ID + P]
            pe.wait_ge(wg_in, 64)
            pe.wait_ge(ones_set, 3)
            with pe.Fori(0, TT // 2) as i:
                for u in range(2):
                    t = i * 2 + u
                    pe.wait_ge(z_in[u].sem, z_in[u].at(i))
                    pe.wait_ge(z_out.sem, z_out.at(t - 1))
                    pe.transpose(psZ[0:32, 0:P], z[:, u, :], ident).then_inc(z_turned.sem, 1)
                    pe.wait_ge(z_out.sem, z_out.at(t))
                    pe.wait_ge(decays.sem, decays.at(t - 1))
                    pe.matmul(psL, zT[:, u, :], wg[:, :], start=True, stop=True).then_inc(logits.sem, 1)
                    pe.wait_ge(k_split.sem, k_split.at(t))
                    pe.wait_ge(k_out.sem, k_out.at(t - 1))
                    for m in range(2):
                        for h in range(KVH):
                            mm = pe.transpose(psK[:, (m * KVH + h) * P:(m * KVH + h + 1) * P],
                                              kdup[:, m, h, :, :].rearrange("p c d -> p (c d)").bitcast(F32), ident)
                    mm.then_inc(k_turned.sem, 1)
                    pe.wait_ge(decays.sem, decays.at(t))
                    pe.wait_ge(grown.sem, grown.at(t - 1))
                    pe.matmul(psU[:, 0:256], con[:, C_SUF_F:C_SUF_F + P], lat[:, u, 0:256], start=True, stop=True)
                    mm = pe.matmul(psU[:, 256:512], con[:, C_SUF_B:C_SUF_B + P], lat[:, u, 256:512], start=True, stop=True)
                    mm.then_inc(sums.sem, 1)
                    pe.wait_ge(scaled.sem, scaled.at(t))
                    pe.wait_ge(added.sem, added.at(t - 1))
                    for q in range(4):
                        pe.matmul(psD[:, 2 * q:2 * q + 2], lat[:, u, q * P:(q + 1) * P], con[:, C_IND:C_IND + 2], start=True, stop=True)
                    for d in range(2):
                        for g in range(2):
                            for ch in range(2):
                                for h in range(4):
                                    n = d * 2 + g
                                    rows = slice(ch * CHUNK, (ch + 1) * CHUNK)
                                    mm = pe.matmul(psS[h * DK:(h + 1) * DK, ch, n * HEAD:(n + 1) * HEAD],
                                                   kd[rows, u, d, (g * 4 + h) * DK:(g * 4 + h + 1) * DK],
                                                   row[rows, u, GV + (g * 4 + h) * HEAD:GV + (g * 4 + h + 1) * HEAD],
                                                   start=True, stop=True, tile_position=(ch * CHUNK, h * DK))
                    mm.then_inc(moved.sem, 1)
            pe.wait_ge(grown.sem, grown.at(TT - 1))
            early, late, every = con[:, C_CTX_B:C_CTX_B + P], con[:, C_CTX_F:C_CTX_F + P], con[:, C_ALL:C_ALL + P]
            pe.matmul(psU[:, 0:256], late, lat[:, 0, 0:256], start=True, stop=False)
            pe.matmul(psU[:, 0:256], every, lat[:, 1, 0:256], start=False, stop=True)
            pe.matmul(psU[:, 256:512], early, lat[:, 0, 256:512], start=True, stop=True)
            pe.matmul(psN[:, 0:256], late, lat[:, 1, 0:256], start=True, stop=True)
            pe.matmul(psN[:, 256:512], early, lat[:, 1, 256:512], start=True, stop=False)
            pe.matmul(psN[:, 256:512], every, lat[:, 0, 256:512], start=False, stop=True).then_inc(ctx_sum, 1)
            pe.wait_ge(ctx_k, 2)
            pe.wait_ge(added.sem, added.at(TT - 1))
            for d in range(2):
                for g in range(2):
                    for h in range(4):
                        n = d * 2 + g
                        for u in range(2):
                            mm = pe.matmul(psS[h * DK:(h + 1) * DK, 0, n * HEAD:(n + 1) * HEAD],
                                           kd[:, u, d, (g * 4 + h) * DK:(g * 4 + h + 1) * DK],
                                           row[:, u, GV + (g * 4 + h) * HEAD:GV + (g * 4 + h + 1) * HEAD],
                                           start=(u == 0), stop=(u == 1), tile_position=(0, h * DK))
            mm.then_inc(ctx_state, 1)


def mix_block(nc, S):
    sb, con, proj = S["sb"], S["con"], S["proj"]
    cos, sin, keyT, val, la, state = (S[n] for n in ("cos", "sin", "keyT", "val", "la", "state"))
    mixd = S["mixd"]
    with ExitStack() as s:
        def sem(name):
            return s.enter_context(nc.semaphore("x_" + name))

        def ev(name, per=1, dma=False, credit=None):
            return Event(nc, s, "x_" + name, per, dma, credit)
        KEYS = 3 * P + CTX
        prev_mask = sb(s, "prev_mask", [P, LT, P], BF16)
        next_mask = sb(s, "next_mask", [P, LT, P], BF16)
        identb = sb(s, "identb", [P, P], BF16)
        nsink = sb(s, "nsink", [P, AH])
        gain = sb(s, "gain", [P, HEAD])
        row = sb(s, "xrow", [P, 2, COLS])
        rot = sb(s, "qrot", [P, AH, HEAD])
        rot2 = sb(s, "qrot2", [P, AH, HEAD])
        qs = sb(s, "qs", [P, AH, 2, HEAD], F32R)
        qT = sb(s, "qT", [P, 2, AH * P], F32R)
        prob = sb(s, "prob", [P, 2, KEYS])
        probT = sb(s, "probT", [P, 2, KEYS])
        mx = sb(s, "mx", [P, AH])
        negm = sb(s, "negm", [P, AH])
        den = sb(s, "den", [P, AH])
        snk = sb(s, "snk", [P, AH])
        mix = sb(s, "mix", [P, 2, D])
        expb = sb(s, "expb", [P, 2, 512])
        qd = sb(s, "qd", [P, 512])
        ki = sb(s, "ki", [P, 512])
        qkT = sb(s, "qkT", [P, 8, P])
        qspread = sb(s, "qspread", [P, 4, 4, P])
        amask = sb(s, "amask", [P, 2, P])
        am = sb(s, "am", [P, 4, 4, P])
        st = sb(s, "st", [P, 4, 2, 4, HEAD])
        gg = sb(s, "gg", [P, 512])
        sq = sb(s, "sq", [P, 512])
        ssq = sb(s, "gssq", [P, GH])
        rs = sb(s, "grs", [P, GH])
        ps = s.enter_context(nc.psum_tensor("xps", [P, 8, 512], F32))
        flat = ps[:, :, :].rearrange("p b n -> p (b n)")
        psP = flat[:, 4 * 512:6 * 512]
        psO = flat[:, 6 * 512:7 * 512]
        psM = flat[:, 7 * 512:8 * 512]
        setup_in, setup = sem("setup_in"), sem("setup")
        row_in = [ev(f"row_in{u}", dma=True) for u in range(2)]
        rotated, q_hi, q_lo = ev("rotated", 4), ev("q_hi"), ev("q_lo")
        turned, evac = ev("turned", 9), ev("evac", 9)
        scores, shifted, exps, pv = ev("scores", 8), ev("shifted", 16), ev("exps", 8), ev("pv", 8)
        sink_exp, attn = ev("sink_exp"), ev("attn", 4)
        prefix, expd, q_dec, k_inv = ev("prefix"), ev("expd"), ev("q_dec"), ev("k_inv")
        gq_turned, gq_spread, gq_kept, gk_turned, gk_kept = (ev(n) for n in ("gq_turned", "gq_spread", "gq_kept", "gk_turned", "gk_kept"))
        inner, masked, gla, states, gained = ev("inner", 4), ev("masked", 4), ev("gla"), ev("states"), ev("gained")
        taken, meansq, rstd, mixed = ev("taken"), ev("meansq"), ev("rstd", 2), ev("mixed", 2)
        stored = [ev(f"stored{u}", dma=True, credit=1) for u in range(2)]
        block = s.enter_context(nc.Block())

        def score_tile(h):
            return flat[:, (h % 2) * 1024 + P:(h % 2) * 1024 + P + KEYS]

        def tiles(eng, body):
            body(0, 0, 0, first=True)
            with eng.Fori(0, LT // 2 - 1) as i:
                for v in range(2):
                    body(i * 2 + (v + 1), 1 - v, i + v)
            body(LT - 1, 1, LT // 2 - 1, last=True)

        @block.sync
        def _(sp):
            sp.dma_start(nsink[:, :], S["attn_sink"].partition_broadcast(P)).then_inc(setup_in, 16)
            sp.dma_start(gain[:, :], S["g_gla"].partition_broadcast(P)).then_inc(setup_in, 16)
            for u in range(2):
                stored[u].open(sp)

            def load(t, u):
                sp.wait_ge(gla.sem, gla.at(t - 2))
                sp.wait_ge(gained.sem, gained.at(t - 2))
                sp.wait_ge(k_inv.sem, k_inv.at(t - 2))
                sp.wait_ge(rotated.sem, rotated.at(t - 2))
                sp.dma_start(row[:, u, :], proj[bass.ds(t * P, P), :]).then_inc(row_in[u].sem, 16)

            def store(t, u):
                sp.wait_ge(mixed.sem, mixed.at(t))
                sp.wait_ge(attn.sem, attn.at(t))
                sp.dma_start(mixd[bass.ds(t * P, P), :], mix[:, u, :]).then_inc(stored[u].sem, 16)

            def body(t, u, n, first=False, last=False):
                t = t if first or last else sp.snap(t)
                if not last:
                    load(t + 1 if first else sp.snap(t + 1), 1 - u)
                if not first:
                    store(t - 1 if last else sp.snap(t - 1), 1 - u)

            load(0, 0)
            tiles(sp, body)
            store(LT - 1, 1)
            for u in range(2):
                sp.wait_ge(stored[u].sem, stored[u].at(LT // 2 - 1))

        @block.gpsimd
        def _(pool):
            for e in (rotated, k_inv, states, gained):
                e.open(pool)

            def turn_queries(t, u, n):
                pool.wait_ge(row_in[u].sem, row_in[u].at(n))
                pool.wait_ge(q_hi.sem, q_hi.at(t - 1))
                pool.wait_ge(q_lo.sem, q_lo.at(t - 1))
                rope(pool, rotated, t, row[:, u, QQ:QQ + 512].rearrange("p (h d) -> p h d", h=AH), cos, sin, rot, rot2, AH)

            def body(t, u, n, first=False, last=False):
                pool.wait_ge(gla.sem, gla.at(t - 1))
                for q in range(4):
                    a = pool.tensor_tensor(st[:, q, :, :, :], state[:, q, bass.ds(t * 2, 2), :].unsqueeze(2).broadcast_to([P, 2, 4, HEAD]),
                                           con[:, C_HEAD:C_COLS].unsqueeze(1).unsqueeze(3).broadcast_to([P, 2, 4, HEAD]), ALU.mult)
                a.then_inc(states.sem, 1)
                pool.wait_ge(expd.sem, expd.at(t))
                pool.wait_ge(gk_turned.sem, gk_turned.at(t - 1))
                pool.tensor_tensor(ki[:, :].rearrange("p (d n) -> p d n", d=2), expb[:, 1, :].rearrange("p (d n) -> p d n", d=2),
                                   row[:, u, GK:GK + 256].unsqueeze(1).broadcast_to([P, 2, 256]), ALU.mult).then_inc(k_inv.sem, 1)
                pool.wait_ge(mixed.sem, mixed.at(t - 1))
                for m, col in enumerate((GG1, GG2)):
                    a = pool.tensor_tensor(gg[:, m * 256:(m + 1) * 256].rearrange("p (h d) -> p h d", d=HEAD),
                                           row[:, u, col:col + 256].rearrange("p (h d) -> p h d", d=HEAD),
                                           gain[:, :].unsqueeze(1).broadcast_to([P, 4, HEAD]), ALU.mult)
                a.then_inc(gained.sem, 1)
                if not last:
                    turn_queries(t + 1, 1 - u, n + u)

            turn_queries(0, 0, 0)
            pool.wait_ge(setup, 8)
            tiles(pool, body)

        @block.scalar
        def _(act):
            for e in (q_hi, exps, sink_exp, expd, gq_spread, taken, rstd):
                e.open(act)

            def high(t):
                act.wait_ge(rotated.sem, rotated.at(t))
                act.wait_ge(turned.sem, turned.at(t - 1, 1))
                act.activation(qs[:, :, 0, :], rot[:, :, :], ACT.Copy).then_inc(q_hi.sem, 1)

            def take(t, u, n):
                act.wait_ge(gla.sem, gla.at(t))
                act.wait_ge(stored[u].sem, stored[u].at(n - 1))
                act.wait_ge(meansq.sem, meansq.at(t - 1))
                act.activation(mix[:, u, 512:1024], psM, ACT.Copy)
                act.activation(sq[:, :], psM, ACT.Square).then_inc(taken.sem, 1)

            def root(t):
                act.wait_ge(meansq.sem, meansq.at(t))
                act.wait_ge(mixed.sem, mixed.at(t - 1, 1))
                act.activation(rs[:, :], ssq[:, :], ACT.Ln, scale=1.0 / HEAD, bias=S["epsb"][:, :]).then_inc(rstd.sem, 1)
                act.wait_ge(rstd.sem, rstd.at(t, 1))
                act.activation(rs[:, :], rs[:, :], ACT.Exp, scale=-0.5).then_inc(rstd.sem, 1)

            def body(t, u, n, first=False, last=False):
                if not first:
                    take(t - 1, 1 - u, n + u - 1)
                for h in range(AH):
                    act.wait_ge(shifted.sem, shifted.at(t, 2 * h + 2))
                    act.wait_ge(turned.sem, turned.at(t, h) if h >= 2 else turned.at(t - 1, 8 + h))
                    if h == 0:
                        act.wait_ge(attn.sem, attn.at(t - 1))
                    act.activation(prob[:, h % 2, :], score_tile(h), ACT.Exp, scale=0.125, bias=negm[:, h:h + 1],
                                   accum_out=den[:, h:h + 1]).then_inc(exps.sem, 1)
                    if h == 1:
                        act.wait_ge(prefix.sem, prefix.at(t))
                        act.wait_ge(q_dec.sem, q_dec.at(t - 1))
                        act.wait_ge(k_inv.sem, k_inv.at(t - 1))
                        act.activation(expb[:, 0, :], psM, ACT.Exp)
                        act.activation(expb[:, 1, :], psM, ACT.Exp, scale=-1.0).then_inc(expd.sem, 1)
                    if h == 2 and not first:
                        root(t - 1)
                    if h == 3:
                        act.wait_ge(gq_kept.sem, gq_kept.at(t))
                        act.wait_ge(inner.sem, inner.at(t - 1))
                        for k in range(4):
                            a = act.activation(qspread[:, :, k, :], qkT[:, 0:4, :], ACT.Copy,
                                               scale=con[:, C_HEAD + k:C_HEAD + k + 1])
                        a.then_inc(gq_spread.sem, 1)
                    if h == 5 and not last:
                        high(t + 1)
                act.wait_ge(attn.sem, attn.at(t, 1))
                act.activation(snk[:, :], snk[:, :], ACT.Exp).then_inc(sink_exp.sem, 1)

            high(0)
            tiles(act, body)
            take(LT - 1, 1, LT // 2 - 1)
            root(LT - 1)

        @block.vector
        def _(dve):
            for e in (q_lo, evac, shifted, attn, q_dec, gq_kept, gk_kept, masked, meansq, mixed):
                e.open(dve)
            dve.wait_ge(setup_in, 32)
            dve.tensor_scalar(nsink[:, :], nsink[:, :], -1.0, None, ALU.mult).then_inc(setup, 1)
            dve.memset(prev_mask[:, 0:1, :], NEG).then_inc(setup, 1)
            dve.memset(next_mask[:, LT - 1:LT, :], NEG).then_inc(setup, 1)
            dve.tensor_copy(prev_mask[:, 1:LT, :], con[:, C_PREV:C_PREV + P].unsqueeze(1).broadcast_to([P, LT - 1, P])).then_inc(setup, 1)
            dve.tensor_copy(next_mask[:, 0:LT - 1, :], con[:, C_NEXT:C_NEXT + P].unsqueeze(1).broadcast_to([P, LT - 1, P])).then_inc(setup, 1)
            dve.tensor_copy(identb[:, :], con[:, C_ID:C_ID + P]).then_inc(setup, 1)
            dve.tensor_scalar(amask[:, 0, :], con[:, C_PREF_F:C_PREF_F + P], TAU, None, ALU.mult).then_inc(setup, 1)
            dve.tensor_scalar(amask[:, 1, :], con[:, C_PREF_B:C_PREF_B + P], TAU, None, ALU.mult).then_inc(setup, 1)
            dve.wait_ge(setup, 8)

            def low(t):
                dve.wait_ge(q_hi.sem, q_hi.at(t))
                dve.tensor_tensor(qs[:, :, 1, :], rot[:, :, :], qs[:, :, 0, :].bitcast(F32), ALU.subtract).then_inc(q_lo.sem, 1)

            def queries(t, u):
                dve.wait_ge(turned.sem, turned.at(t, 1))
                dve.wait_ge(scores.sem, scores.at(t - 2))
                dve.tensor_copy(qT[:, u, :], psP).then_inc(evac.sem, 1)

            def maximum(t, h):
                dve.wait_ge(scores.sem, scores.at(t, h + 1))
                if h == 0:
                    dve.wait_ge(exps.sem, exps.at(t - 1))
                dve.reduce_max(mx[:, h:h + 1], score_tile(h), AX.X).then_inc(shifted.sem, 1)
                dve.wait_ge(shifted.sem, shifted.at(t, 2 * h + 1))
                dve.tensor_scalar(negm[:, h:h + 1], mx[:, h:h + 1], -0.125, nsink[:, h:h + 1], ALU.mult, ALU.min).then_inc(shifted.sem, 1)

            def transposed(t, h):
                dve.wait_ge(turned.sem, turned.at(t, h + 2))
                dve.wait_ge(pv.sem, pv.at(t, h - 1) if h >= 2 else pv.at(t - 1, 7 + h))
                dve.tensor_copy(probT[:, h % 2, :], psP[:, 0:KEYS]).then_inc(evac.sem, 1)

            def mask(t, q):
                dve.wait_ge(inner.sem, inner.at(t, q + 1))
                if q == 0:
                    dve.wait_ge(gla.sem, gla.at(t - 1))
                dve.tensor_tensor(am[:, q, :, :], psM.rearrange("p (h j) -> p h j", j=P),
                                  amask[:, q // 2, :].unsqueeze(1).broadcast_to([P, 4, P]), ALU.mult).then_inc(masked.sem, 1)

            def by_head(a):
                return a.rearrange("p (h d) -> p h d", d=HEAD)

            def sum_squares(t):
                dve.wait_ge(taken.sem, taken.at(t))
                dve.wait_ge(rstd.sem, rstd.at(t - 1))
                dve.reduce_sum(ssq[:, :], by_head(sq[:, :]), AX.X).then_inc(meansq.sem, 1)

            def norm(t, u):
                dve.wait_ge(rstd.sem, rstd.at(t))
                dve.tensor_tensor(by_head(mix[:, u, 512:1024]), by_head(mix[:, u, 512:1024]),
                                  rs[:, :].unsqueeze(2).broadcast_to([P, GH, HEAD]), ALU.mult).then_inc(mixed.sem, 1)

            def gate(t, u):
                dve.wait_ge(mixed.sem, mixed.at(t, 1))
                dve.wait_ge(gained.sem, gained.at(t))
                dve.tensor_tensor(mix[:, u, 512:1024], mix[:, u, 512:1024], gg[:, :], ALU.mult).then_inc(mixed.sem, 1)

            def body(t, u, n, first=False, last=False):
                for h in range(AH + 1):
                    if h < AH:
                        maximum(t, h)
                    else:
                        dve.wait_ge(shifted.sem, shifted.at(t))
                        dve.tensor_tensor(snk[:, :], negm[:, :], nsink[:, :], ALU.subtract).then_inc(attn.sem, 1)
                    if h:
                        transposed(t, h - 1)
                    if h == 1 and not first:
                        sum_squares(t - 1)
                    if h == 2:
                        dve.wait_ge(expd.sem, expd.at(t))
                        dve.wait_ge(gq_turned.sem, gq_turned.at(t - 1))
                        dve.scalar_tensor_tensor(qd[:, :].rearrange("p (d n) -> p d n", d=2),
                                                 row[:, u, GQ:GQ + 256].unsqueeze(1).broadcast_to([P, 2, 256]), DK ** -0.5,
                                                 expb[:, 0, :].rearrange("p (d n) -> p d n", d=2), ALU.mult, ALU.mult).then_inc(q_dec.sem, 1)
                    if h == 3:
                        dve.wait_ge(gq_turned.sem, gq_turned.at(t))
                        dve.wait_ge(gla.sem, gla.at(t - 1))
                        dve.tensor_copy(qkT[:, 0:4, :], psM.rearrange("p (b j) -> p b j", j=P)).then_inc(gq_kept.sem, 1)
                        if not first:
                            norm(t - 1, 1 - u)
                    if h == 4:
                        dve.wait_ge(gk_turned.sem, gk_turned.at(t))
                        dve.tensor_copy(qkT[:, 4:8, :], psM.rearrange("p (b j) -> p b j", j=P)).then_inc(gk_kept.sem, 1)
                        if not first:
                            gate(t - 1, 1 - u)
                    if h == 6 and not last:
                        low(t + 1)
                    if h >= 5:
                        mask(t, h - 5)
                if not last:
                    queries(t + 1, 1 - u)
                dve.wait_ge(sink_exp.sem, sink_exp.at(t))
                dve.tensor_tensor(den[:, :], den[:, :], snk[:, :], ALU.add).then_inc(attn.sem, 1)
                dve.wait_ge(attn.sem, attn.at(t, 2))
                dve.reciprocal(den[:, :], den[:, :]).then_inc(attn.sem, 1)
                dve.wait_ge(attn.sem, attn.at(t, 3))
                dve.wait_ge(pv.sem, pv.at(t))
                dve.wait_ge(stored[u].sem, stored[u].at(n - 1))
                dve.tensor_tensor(by_head(mix[:, u, 0:512]), by_head(psO),
                                  den[:, :].unsqueeze(2).broadcast_to([P, AH, HEAD]), ALU.mult).then_inc(attn.sem, 1)

            low(0)
            queries(0, 0)
            tiles(dve, body)
            sum_squares(LT - 1)
            norm(LT - 1, 1)
            gate(LT - 1, 1)

        @block.tensor
        def _(pe):
            for e in (turned, scores, pv, prefix, gq_turned, gk_turned, inner, gla):
                e.open(pe)
            ident = con[:, C_ID:C_ID + P]
            pe.wait_ge(setup, 8)

            def queries(t):
                pe.wait_ge(q_lo.sem, q_lo.at(t))
                pe.wait_ge(evac.sem, evac.at(t - 1))
                for h in range(AH):
                    mm = pe.transpose(psP[:, h * P:(h + 1) * P], qs[:, h, :, :].rearrange("p m d -> p (m d)").bitcast(F32), ident)
                mm.then_inc(turned.sem, 1)

            def score(t, u, h):
                if h == 0:
                    pe.wait_ge(evac.sem, evac.at(t, 1))
                pe.wait_ge(exps.sem, exps.at(t, h - 1) if h >= 2 else exps.at(t - 1, 7 + h))
                sc, q, kv = score_tile(h), qT[:, u, h * P:(h + 1) * P], h // 4
                pe.matmul(sc[:, 0:3 * P], q, keyT[:, 0, kv, bass.ds(t * P, 3 * P)], start=True, stop=False)
                pe.matmul(sc[:, 0:P], identb[:, :], prev_mask[:, bass.ds(t, 1), :].rearrange("p s j -> p (s j)"), start=False, stop=False)
                pe.matmul(sc[:, 2 * P:3 * P], identb[:, :], next_mask[:, bass.ds(t, 1), :].rearrange("p s j -> p (s j)"), start=False, stop=False)
                pe.matmul(sc[:, 0:3 * P], q, keyT[:, 1, kv, bass.ds(t * P, 3 * P)], start=False, stop=True)
                for m in range(2):
                    mm = pe.matmul(sc[:, 3 * P:KEYS], q, keyT[:, m, kv, (LT + 1) * P:(TT + 1) * P], start=(m == 0), stop=(m == 1))
                mm.then_inc(scores.sem, 1)

            def turn(t, h):
                pe.wait_ge(exps.sem, exps.at(t, h + 1))
                pe.wait_ge(evac.sem, evac.at(t, h + 1))
                for b in range(KEYS // P):
                    mm = pe.transpose(psP[:, b * P:(b + 1) * P], prob[:, h % 2, b * P:(b + 1) * P], ident)
                mm.then_inc(turned.sem, 1)

            def weigh(t, h):
                pe.wait_ge(evac.sem, evac.at(t, h + 2))
                if h == 0:
                    pe.wait_ge(attn.sem, attn.at(t - 1))
                kv = (h // 4) * HEAD
                for b in range(KEYS // P):
                    v = val[:, bass.ds(t + b, 1), kv:kv + HEAD].rearrange("p s d -> p (s d)") if b < 3 else val[:, LT + 1 + b - 3, kv:kv + HEAD]
                    mm = pe.matmul(psO[:, h * HEAD:(h + 1) * HEAD], probT[:, h % 2, b * P:(b + 1) * P], v,
                                   start=(b == 0), stop=(b == KEYS // P - 1))
                mm.then_inc(pv.sem, 1)

            def prefix_sums(t):
                pe.wait_ge(taken.sem, taken.at(t - 1))
                for d, m in enumerate((C_PREF_F, C_PREF_B)):
                    mm = pe.matmul(psM[:, d * 256:(d + 1) * 256], con[:, m:m + P],
                                   la[:, bass.ds(t, 1), d * 256:(d + 1) * 256].rearrange("p s n -> p (s n)"), start=True, stop=True)
                mm.then_inc(prefix.sem, 1)

            def turn_gla(t, a, event):
                for b in range(4):
                    mm = pe.transpose(psM[:, b * P:(b + 1) * P], a[:, b * P:(b + 1) * P], ident)
                mm.then_inc(event.sem, 1)

            def inner_products(t, q):
                if q == 0:
                    pe.wait_ge(gq_spread.sem, gq_spread.at(t))
                    pe.wait_ge(gk_kept.sem, gk_kept.at(t))
                else:
                    pe.wait_ge(masked.sem, masked.at(t, q))
                pe.matmul(psM, qkT[:, 4 + q, :], qspread[:, q, :, :].rearrange("p h j -> p (h j)"), start=True, stop=True).then_inc(inner.sem, 1)

            def gla_output(t, u):
                pe.wait_ge(masked.sem, masked.at(t))
                pe.wait_ge(states.sem, states.at(t))
                for g in range(2):
                    for d in range(2):
                        for ch in range(2):
                            j = slice(ch * CHUNK, (ch + 1) * CHUNK)
                            pe.matmul(psM[j, g * 256:(g + 1) * 256], qkT[:, d * 2 + g, j],
                                      st[:, d * 2 + g, ch, :, :].rearrange("p h d -> p (h d)"),
                                      start=(g == 0 and d == 0), stop=False, skip_group_check=True)
                for h in range(GH):
                    for d in range(2):
                        mm = pe.matmul(psM[:, h * HEAD:(h + 1) * HEAD], am[:, 2 * d + h // 4, h % 4, :],
                                       row[:, u, GV + h * HEAD:GV + (h + 1) * HEAD], start=False, stop=(h == GH - 1 and d == 1),
                                       skip_group_check=True)
                mm.then_inc(gla.sem, 1)

            def body(t, u, n, first=False, last=False):
                for h in range(AH + 1):
                    if h < AH:
                        score(t, u, h)
                    if h >= 1:
                        turn(t, h - 1)
                    if h >= 2:
                        weigh(t, h - 2)
                    if h == 1:
                        prefix_sums(t)
                    if h == 3:
                        pe.wait_ge(q_dec.sem, q_dec.at(t))
                        pe.wait_ge(expd.sem, expd.at(t))
                        turn_gla(t, qd, gq_turned)
                    if h == 4:
                        pe.wait_ge(k_inv.sem, k_inv.at(t))
                        pe.wait_ge(gq_kept.sem, gq_kept.at(t))
                        turn_gla(t, ki, gk_turned)
                    if h >= 5:
                        inner_products(t, h - 5)
                if not last:
                    queries(t + 1)
                weigh(t, AH - 1)
                gla_output(t, u)

            queries(0)
            tiles(pe, body)


def output_block(nc, S):
    sb, con, A2, B2, G1, epsb = (S[n] for n in ("sb", "con", "A2", "B2", "G1", "epsb"))
    h2h, h2l, mixd, x2d = (S[n] for n in ("h2h", "h2l", "mixd", "x2d"))
    with ExitStack() as s:
        def sem(name):
            return s.enter_context(nc.semaphore("o_" + name))

        def ev(name, per=1, dma=False, credit=None):
            return Event(nc, s, "o_" + name, per, dma, credit)
        woh = sb(s, "woh", [P, KT, D], F32R)
        wol = sb(s, "wol", [P, KT, D], F32R)
        raw = sb(s, "oraw", [P, 2, D])
        mix = sb(s, "omix", [P, 2, D])
        x = sb(s, "ox", [P, 2, D])
        mh = sb(s, "omh", [P, 2, KT, P], F32R)
        ml = sb(s, "oml", [P, 2, KT, P], F32R)
        junk = sb(s, "ojunk", [P, D])
        work = sb(s, "owork", [P, 2, D])
        stats = sb(s, "ostats", [P, 2, 4])
        h2 = sb(s, "oh2", [P, KT, P])
        ps = s.enter_context(nc.psum_tensor("ops", [P, 8, 512], F32))
        flat = ps[:, :, :].rearrange("p b n -> p (b n)")
        psT, psY, psH = flat[:, 0:1024], [flat[:, 1024:2048], flat[:, 2048:3072]], flat[:, 3072:4096]
        raw_in, hi, lo = [sem(f"raw_in{n}") for n in range(2)], sem("hi"), sem("lo")
        mix_in, x_in = ([ev(f"{n}{u}", dma=True) for u in range(2)] for n in ("mix_in", "x_in"))
        mix_turned, mix_hi, mix_lo, product = ev("mix_turned"), ev("mix_hi"), ev("mix_lo"), ev("product")
        squares, roots, inverse = ev("squares", 2), ev("roots", 2), ev("inverse", 2)
        branch, residual, normed = ev("branch"), ev("residual"), ev("normed")
        turned, modulated, h_hi, h_lo = ev("turned"), ev("modulated"), ev("h_hi"), ev("h_lo")
        stored = [ev(f"stored{u}", dma=True, credit=1) for u in range(2)]
        block = s.enter_context(nc.Block())

        def pipelined(eng, ahead, now, behind):
            ahead(0, 0, 0)
            ahead(1, 1, 0)
            now(0, 0, 0)
            with eng.Fori(0, LT // 2 - 1) as i:
                for u in range(2):
                    t = i * 2 + (u + 1)
                    ahead(t + 1, u, i + 1)
                    now(t, 1 - u, i + u)
                    behind(t - 1, u, i)
            now(LT - 1, 1, LT // 2 - 1)
            behind(LT - 2, 0, LT // 2 - 1)
            behind(LT - 1, 1, LT // 2 - 1)

        def nothing(t, u, n):
            pass

        @block.sync
        def _(sp):
            for k in range(KT):
                if k >= 2:
                    sp.wait_ge(lo, k - 1)
                sp.dma_start(raw[:, k % 2, :], S["w_out"][k * P:(k + 1) * P, :]).then_inc(raw_in[k % 2], 16)

            def load_mix(t, u, n):
                sp.wait_ge(mix_turned.sem, mix_turned.at(t - 2))
                sp.dma_start(mix[:, u, :], mixd[bass.ds(t * P, P), :]).then_inc(mix_in[u].sem, 16)

            def load_x(t, u, n):
                sp.wait_ge(turned.sem, turned.at(t - 2))
                sp.wait_ge(stored[u].sem, stored[u].at(n - 1))
                sp.dma_start(x[:, u, :], S["xall"][bass.ds(t * P, P), :]).then_inc(x_in[u].sem, 16)
            pipelined(sp, load_mix, load_x, nothing)

        @block.gpsimd
        def _(pool):
            residual.open(pool)
            h_lo.open(pool)

            def add(t, u, n):
                pool.wait_ge(branch.sem, branch.at(t))
                pool.wait_ge(x_in[u].sem, x_in[u].at(n))
                pool.tensor_tensor(x[:, u, :], x[:, u, :], work[:, u, :], ALU.add).then_inc(residual.sem, 1)

            def low(t, u, n):
                pool.wait_ge(h_hi.sem, h_hi.at(t))
                pool.tensor_tensor(h2l[:, :, bass.ds(t * P, P)], h2[:, :, :], h2h[:, :, bass.ds(t * P, P)].bitcast(F32),
                                   ALU.subtract).then_inc(h_lo.sem, 1)
            pipelined(pool, nothing, add, low)

        @block.scalar
        def _(act):
            for e in (mix_hi, squares, roots, modulated, h_hi, *stored):
                e.open(act)
            for k in range(KT):
                act.wait_ge(raw_in[k % 2], 16 * (k // 2 + 1))
                act.activation(woh[:, k, :], raw[:, k % 2, :], ACT.Copy).then_inc(hi, 1)

            def stat(n, t, u, src):
                act.activation(junk[:, :], src, ACT.Square, accum_out=stats[:, u, 2 * n:2 * n + 1]).then_inc(squares.sem, 1)
                act.wait_ge(squares.sem, squares.at(t, n + 1))
                act.activation(stats[:, u, 2 * n + 1:2 * n + 2], stats[:, u, 2 * n:2 * n + 1], ACT.Sqrt, scale=1.0 / D,
                               bias=epsb[:, :]).then_inc(roots.sem, 1)

            def high(t, u, n):
                act.wait_ge(mix_turned.sem, mix_turned.at(t))
                act.wait_ge(product.sem, product.at(t - 2))
                act.activation(mh[:, u, :, :], psT.rearrange("p (k j) -> p k j", j=P), ACT.Copy).then_inc(mix_hi.sem, 1)

            def sums(t, u, n):
                act.wait_ge(product.sem, product.at(t))
                act.wait_ge(squares.sem, squares.at(t - 1))
                act.wait_ge(branch.sem, branch.at(t - 2))
                stat(0, t, u, psY[u])
                act.wait_ge(residual.sem, residual.at(t))
                act.dma_start(x2d[bass.ds(t * P, P), :], x[:, u, :]).then_inc(stored[u].sem, 16)
                act.wait_ge(squares.sem, squares.at(t, 1))
                stat(1, t, u, x[:, u, :])

            def modulate(t, u, n):
                act.wait_ge(turned.sem, turned.at(t))
                act.wait_ge(h_lo.sem, h_lo.at(t - 1))
                for k in range(KT):
                    a = act.activation(h2[:, k, :], psH[:, k * P:(k + 1) * P], ACT.Identity, scale=A2[:, k:k + 1], bias=B2[:, k:k + 1])
                a.then_inc(modulated.sem, 1)
                act.wait_ge(modulated.sem, modulated.at(t))
                act.activation(h2h[:, :, bass.ds(t * P, P)], h2[:, :, :], ACT.Copy).then_inc(h_hi.sem, 1)
            pipelined(act, high, sums, modulate)
            for u in range(2):
                act.wait_ge(stored[u].sem, stored[u].at(LT // 2 - 1))

        @block.vector
        def _(dve):
            for e in (mix_lo, inverse, branch, normed):
                e.open(dve)
            for k in range(KT):
                dve.wait_ge(hi, k + 1)
                dve.tensor_tensor(wol[:, k, :], raw[:, k % 2, :], woh[:, k, :].bitcast(F32), ALU.subtract).then_inc(lo, 1)

            def low(t, u, n):
                dve.wait_ge(mix_hi.sem, mix_hi.at(t))
                dve.tensor_tensor(ml[:, u, :, :], psT.rearrange("p (k j) -> p k j", j=P), mh[:, u, :, :].bitcast(F32), ALU.subtract).then_inc(mix_lo.sem, 1)

            def norm(t, u, n):
                dve.wait_ge(roots.sem, roots.at(t, 1))
                dve.reciprocal(stats[:, u, 1:2], stats[:, u, 1:2]).then_inc(inverse.sem, 1)
                dve.wait_ge(inverse.sem, inverse.at(t, 1))
                dve.wait_ge(turned.sem, turned.at(t - 2))
                dve.scalar_tensor_tensor(work[:, u, :], psY[u], stats[:, u, 1:2], G1[:, :], ALU.mult, ALU.mult).then_inc(branch.sem, 1)
                dve.wait_ge(roots.sem, roots.at(t, 2))
                dve.reciprocal(stats[:, u, 3:4], stats[:, u, 3:4]).then_inc(inverse.sem, 1)
                dve.wait_ge(inverse.sem, inverse.at(t, 2))
                dve.wait_ge(branch.sem, branch.at(t))
                dve.tensor_scalar(work[:, u, :], x[:, u, :], stats[:, u, 3:4], None, ALU.mult).then_inc(normed.sem, 1)
            pipelined(dve, low, norm, nothing)

        @block.tensor
        def _(pe):
            for e in (mix_turned, product, turned):
                e.open(pe)
            ident = con[:, C_ID:C_ID + P]

            def turn_mix(t, u, n):
                pe.wait_ge(mix_in[u].sem, mix_in[u].at(n))
                pe.wait_ge(mix_lo.sem, mix_lo.at(t - 1))
                for k in range(KT):
                    mm = pe.transpose(psT[:, k * P:(k + 1) * P], mix[:, u, k * P:(k + 1) * P], ident)
                mm.then_inc(mix_turned.sem, 1)

            def project(t, u, n):
                pe.wait_ge(mix_lo.sem, mix_lo.at(t))
                pe.wait_ge(branch.sem, branch.at(t - 2))
                for n in range(2):
                    m = 0
                    for k in range(KT):
                        for a, b in ((mh, woh), (ml, woh), (mh, wol)):
                            mm = pe.matmul(psY[u][:, n * 512:(n + 1) * 512], a[:, u, k, :], b[:, k, n * 512:(n + 1) * 512],
                                           start=(m == 0), stop=(m == 3 * KT - 1))
                            m += 1
                mm.then_inc(product.sem, 1)

            def turn_h(t, u, n):
                pe.wait_ge(normed.sem, normed.at(t))
                pe.wait_ge(modulated.sem, modulated.at(t - 1))
                for k in range(KT):
                    mm = pe.transpose(psH[:, k * P:(k + 1) * P], work[:, u, k * P:(k + 1) * P], ident)
                mm.then_inc(turned.sem, 1)

            pe.wait_ge(lo, KT)
            pipelined(pe, turn_mix, project, turn_h)


def ffn_block(nc, S):
    sb, G2, epsb, h2h, h2l, x2d = (S[n] for n in ("sb", "G2", "epsb", "h2h", "h2l", "x2d"))
    with ExitStack() as s:
        def sem(name):
            return s.enter_context(nc.semaphore("f_" + name))

        def ev(name, per=1, dma=False):
            return Event(nc, s, "f_" + name, per, dma)
        HALF = SEQ // 2
        wih = sb(s, "wih", [P, 2, KT, 2, P], F32R)
        wil = sb(s, "wil", [P, 2, KT, 2, P], F32R)
        raw = sb(s, "fraw", [P, KT, 2, 2 * P])
        wdh = sb(s, "wdh", [P, 2, D], F32R)
        wdl = sb(s, "wdl", [P, 2, D], F32R)
        draw = sb(s, "fdraw", [P, D])
        ah = sb(s, "ah", [P, 2, SEQ], F32R)
        al = sb(s, "al", [P, 2, SEQ], F32R)
        x_back = raw[:, :, :, :].rearrange("p k m n -> p (k m n)").rearrange("p (t n) -> p t n", n=D)
        act_t = sb(s, "act_t", [P, SEQ])
        down = sb(s, "down", [P, LT, D])
        stats = sb(s, "fstats", [P, LT])
        ps = s.enter_context(nc.psum_tensor("fps", [P, 8, 512], F32))
        flat = ps[:, :, :].rearrange("p b n -> p (b n)")
        psG, psU = flat[:, 0:1024], flat[:, 1024:2048]
        psD = [flat[:, 2048:3072], flat[:, 3072:4096]]
        raw_in, draw_in = ev("raw_in", 2, dma=True), ev("draw_in", dma=True)
        in_hi, in_lo, down_hi, down_lo = ev("in_hi"), ev("in_lo"), ev("down_hi"), ev("down_lo")
        product, silu, act_full, act_hi, act_lo = (ev(n, 2) for n in ("product", "silu", "act_full", "act_hi", "act_lo"))
        share, summed = ev("share", LT), ev("summed", LT)
        x_in = [sem(f"x_in{n}") for n in range(4)]
        zeroed, f_sq, f_root, f_inv, f_res, f_out = (sem(n) for n in (
            "zeroed", "f_sq", "f_root", "f_inv", "f_res", "f_out"))
        block = s.enter_context(nc.Block())
        w_in = S["w_ffn_in"].rearrange("(k p) (two n) -> p k two n", p=P, two=2)
        PAIRS = HT // 2

        def cols(n):
            return slice(n * HALF, (n + 1) * HALF)

        @block.sync
        def _(sp):
            with sp.Fori(0, PAIRS) as i:
                sp.wait_ge(in_lo.sem, in_lo.at(i * 2 - 1))
                for m in range(2):
                    sp.dma_start(raw[:, :, m, :], w_in[:, :, m, bass.ds(i * 2 * P, 2 * P)]).then_inc(raw_in.sem, 16)
                for u in range(2):
                    j = i * 2 + u
                    sp.wait_ge(down_lo.sem, down_lo.at(j - 1))
                    sp.dma_start(draw[:, :], S["w_ffn_out"][bass.ds(j * P, P), :]).then_inc(draw_in.sem, 16)
            sp.wait_ge(in_lo.sem, in_lo.at(HT - 1))
            for t in range(LT):
                if t >= 4:
                    sp.wait_ge(f_res, t - 3)
                sp.dma_start(x_back[:, t % 4, :], x2d[t * P:(t + 1) * P, :]).then_inc(x_in[t % 4], 16)
            for t in range(LT):
                sp.wait_ge(f_res, t + 1)
                sp.dma_start(S["out"][t * P:(t + 1) * P, :], down[:, t, :]).then_inc(f_out, 16)
            sp.wait_ge(f_out, 16 * LT)

        @block.gpsimd
        def _(pool):
            pool.memset(down[:, :, :], 0.0).then_inc(zeroed, 1)

        @block.scalar
        def _(act):
            for e in (in_hi, down_hi, silu, act_hi):
                e.open(act)

            def split_in(j, slot, pair):
                act.wait_ge(raw_in.sem, raw_in.at(pair))
                act.wait_ge(product.sem, product.at(j - 2))
                act.activation(wih[:, slot, :, :, :], raw[:, :, :, slot * P:(slot + 1) * P], ACT.Copy).then_inc(in_hi.sem, 1)

            def split_down(j, slot, pair):
                act.wait_ge(draw_in.sem, draw_in.at(j))
                act.wait_ge(share.sem, share.at(pair - 1))
                act.activation(wdh[:, slot, :], draw[:, :], ACT.Copy).then_inc(down_hi.sem, 1)

            def gate(j, slot, n):
                act.wait_ge(product.sem, product.at(j, n + 1))
                act.wait_ge(act_lo.sem, act_lo.at(j - 1, n + 1))
                act.activation(act_t[:, cols(n)], psG[:, cols(n)], ACT.Silu).then_inc(silu.sem, 1)

            def high(j, slot, n):
                act.wait_ge(act_full.sem, act_full.at(j, n + 1))
                act.activation(ah[:, slot, cols(n)], act_t[:, cols(n)], ACT.Copy).then_inc(act_hi.sem, 1)

            def body(p, last=False):
                for u in range(2):
                    j = p * 2 + u
                    split_down(j, u, p)
                    gate(j, u, 0)
                    high(j, u, 0)
                    gate(j, u, 1)
                    high(j, u, 1)
                    if not last:
                        split_in(j + 2, u, p + 1)

            split_in(0, 0, 0)
            split_in(1, 1, 0)
            with act.Fori(0, PAIRS - 1) as i:
                body(i)
            body(PAIRS - 1, last=True)
            act.wait_ge(act_lo.sem, act_lo.at(HT - 1))
            for t in range(LT):
                act.wait_ge(summed.sem, summed.at(PAIRS - 1, t + 1))
                if t:
                    act.wait_ge(f_sq, t)
                act.activation(act_t[:, :], down[:, t, :], ACT.Square, accum_out=stats[:, t:t + 1]).then_inc(f_sq, 1)
                act.wait_ge(f_sq, t + 1)
                act.activation(stats[:, t:t + 1], stats[:, t:t + 1], ACT.Sqrt, scale=1.0 / D, bias=epsb[:, :]).then_inc(f_root, 1)

        @block.vector
        def _(dve):
            for e in (in_lo, down_lo, act_full, act_lo, summed):
                e.open(dve)

            def split_in(j, slot):
                dve.wait_ge(in_hi.sem, in_hi.at(j))
                dve.tensor_tensor(wil[:, slot, :, :, :], raw[:, :, :, slot * P:(slot + 1) * P], wih[:, slot, :, :, :].bitcast(F32),
                                  ALU.subtract).then_inc(in_lo.sem, 1)

            def add(p, t):
                dve.wait_ge(share.sem, share.at(p, t + 1))
                dve.wait_ge(summed.sem, summed.at(p - 1, t + 1))
                dve.tensor_tensor(down[:, t, :], down[:, t, :], psD[t % 2], ALU.add).then_inc(summed.sem, 1)

            def activate(j, slot, n):
                dve.wait_ge(silu.sem, silu.at(j, n + 1))
                dve.tensor_tensor(act_t[:, cols(n)], act_t[:, cols(n)], psU[:, cols(n)], ALU.mult).then_inc(act_full.sem, 1)
                dve.wait_ge(act_hi.sem, act_hi.at(j, n + 1))
                dve.tensor_tensor(al[:, slot, cols(n)], act_t[:, cols(n)], ah[:, slot, cols(n)].bitcast(F32), ALU.subtract).then_inc(act_lo.sem, 1)

            def body(p, last=False):
                for u in range(2):
                    j = p * 2 + u
                    dve.wait_ge(down_hi.sem, down_hi.at(j))
                    dve.tensor_tensor(wdl[:, u, :], draw[:, :], wdh[:, u, :].bitcast(F32), ALU.subtract).then_inc(down_lo.sem, 1)
                    for n in range(2):
                        activate(j, u, n)
                    if not last and u == 0:
                        split_in(j + 2, u)
                for t in range(LT):
                    add(p, t)
                    if not last and t == 1:
                        split_in(p * 2 + 3, 1)

            def finish(t):
                dve.wait_ge(f_root, t + 1)
                dve.reciprocal(stats[:, t:t + 1], stats[:, t:t + 1]).then_inc(f_inv, 1)
                dve.wait_ge(f_inv, 2 * t + 1)
                dve.scalar_tensor_tensor(down[:, t, :], down[:, t, :], stats[:, t:t + 1], G2[:, :], ALU.mult, ALU.mult).then_inc(f_inv, 1)
                dve.wait_ge(f_inv, 2 * t + 2)
                dve.wait_ge(x_in[t % 4], 16 * (t // 4 + 1))
                dve.tensor_tensor(down[:, t, :], down[:, t, :], x_back[:, t % 4, :], ALU.add).then_inc(f_res, 1)

            dve.wait_ge(zeroed, 1)
            split_in(0, 0)
            split_in(1, 1)
            with dve.Fori(0, PAIRS - 1) as i:
                body(i)
            for u in range(2):
                j = HT - 2 + u
                dve.wait_ge(down_hi.sem, down_hi.at(j))
                dve.tensor_tensor(wdl[:, u, :], draw[:, :], wdh[:, u, :].bitcast(F32), ALU.subtract).then_inc(down_lo.sem, 1)
                for n in range(2):
                    activate(j, u, n)
            for t in range(LT):
                add(PAIRS - 1, t)
                if t:
                    finish(t - 1)
            finish(LT - 1)

        @block.tensor
        def _(pe):
            product.open(pe)
            share.open(pe)

            def gate_up(j, slot):
                pe.wait_ge(in_lo.sem, in_lo.at(j))
                for n in range(2):
                    pe.wait_ge(act_full.sem, act_full.at(j - 1, n + 1))
                    for m, bank in enumerate((psG, psU)):
                        c = 0
                        for k in range(KT):
                            for w, h in ((wih, h2h), (wih, h2l), (wil, h2h)):
                                mm = pe.matmul(bank[:, cols(n)], w[:, slot, k, m, :], h[:, k, cols(n)],
                                               start=(c == 0), stop=(c == 3 * KT - 1))
                                c += 1
                    mm.then_inc(product.sem, 1)

            def down_share(p):
                pe.wait_ge(down_lo.sem, down_lo.at(p * 2 + 1))
                for t in range(LT):
                    if t % 4 == 0:
                        pe.wait_ge(act_lo.sem, act_lo.at(p * 2 + 1, t // 4 + 1))
                    pe.wait_ge(summed.sem, summed.at(p, t - 1) if t >= 2 else summed.at(p - 1, LT - 1 + t))
                    for n in range(2):
                        c = 0
                        for u in range(2):
                            for a, w in ((ah, wdh), (al, wdh), (ah, wdl)):
                                mm = pe.matmul(psD[t % 2][:, n * 512:(n + 1) * 512], a[:, u, t * P:(t + 1) * P],
                                               w[:, u, n * 512:(n + 1) * 512], start=(c == 0), stop=(c == 5))
                                c += 1
                    mm.then_inc(share.sem, 1)

            with pe.Fori(0, PAIRS) as i:
                gate_up(i * 2, 0)
                gate_up(i * 2 + 1, 1)
                down_share(i)


def kernel(**inputs):
    import concourse.bacc as bacc
    from concourse.bass_utils import run_bass_kernel_spmd

    a = {n: np.ascontiguousarray(v) for n, v in inputs.items()}
    consts, cosd, sind = constants()
    arrays = {
        "xall": np.concatenate([a["x"][0], a["ctx"][0]], axis=0), "c": a["c"][0], "c_ctx": a["c_ctx"],
        "w_ada": a["w_ada"][0], "b_ada": a["b_ada"][0], "g_pre_mix": a["g_pre_mix"][0], "g_post_mix": a["g_post_mix"][0],
        "g_pre_ffn": a["g_pre_ffn"][0], "g_post_ffn": a["g_post_ffn"][0], "w_in": a["w_in"][0], "attn_sink": a["attn_sink"][0],
        "w_gate_fwd": a["w_gate_fwd"][0], "b_gate_fwd": a["b_gate_fwd"][0], "w_gate_bwd": a["w_gate_bwd"][0],
        "b_gate_bwd": a["b_gate_bwd"][0], "g_gla": a["g_gla_norm"][0], "w_out": a["w_out"][0],
        "w_ffn_in": a["w_ffn_in"][0], "w_ffn_out": a["w_ffn_out"][0], "consts": consts, "cosd": cosd, "sind": sind,
    }
    nc = bacc.Bacc("TRN2", target_bir_lowering=False, num_devices=1)
    args = {n: nc.dram_tensor(f"in_{n}", v.shape, F32, kind="ExternalInput").ap() for n, v in arrays.items()}
    args["out"] = nc.dram_tensor("out_0", (SEQ, D), F32, kind="ExternalOutput").ap()
    for n, shape in (("proj", (TOK, COLS)), ("mixd", (SEQ, D)), ("x2d", (SEQ, D))):
        args[n] = nc.dram_tensor(f"scratch_{n}", shape, F32, kind=SCRATCH).ap()
    build(nc, **args)
    r = run_bass_kernel_spmd(nc, [{f"in_{n}": v for n, v in arrays.items()}], core_ids=[0])
    return r.results[0]["out_0"].reshape(1, SEQ, D)
```

```python
from contextlib import ExitStack

import numpy as np

import concourse.bass as bass
from concourse import mybir

ALU = mybir.AluOpType
ACT = mybir.ActivationFunctionType
F32 = mybir.dt.float32
F32R = mybir.dt.float32r
BF16 = mybir.dt.bfloat16
AX = mybir.AxisListType

P = 128
D = 1024
KT = D // P
SEQ = 1024
CTX = 256
TOK = SEQ + CTX
LT = SEQ // P
TT = TOK // P
HEAD = 64
AH, KVH = 8, 2
GH, DK = 8, 32
CHUNK = 64
NCH = SEQ // CHUNK
RANK = 16
TAU = 16.0
GRID_W = 64
ROPE_BASE = 10000.0
HID = 2816
HT = HID // P
EPS = 1e-6
NEG = -1e30
SCRATCH = "Internal"

KK, VV, GK, GV, GG2, ZZ, QQ, GQ, GG1 = 0, 128, 256, 512, 1024, 1280, 1312, 1824, 2080
COLS = 2336
W_Q, W_K, W_GQ, W_GK, W_GV, W_GG, W_Z = 0, 512, 768, 1024, 1280, 1792, 2304
CHUNKS = [[W_K, W_GK], [W_GV, W_GV + 256], [COLS - 512, COLS - 256], [W_Q, W_Q + 256], [W_GQ, W_GG]]
NARROW = COLS - (W_GG + 256)

C_ID, C_ONE, C_PREF_F, C_PREF_B, C_SUF_F, C_SUF_B, C_CTX_F, C_CTX_B, C_ALL, C_PREV, C_NEXT, C_IND = [P * n for n in range(12)]
C_HEAD = C_IND + 2
C_COLS = C_HEAD + 4


def constants():
    j, i = np.arange(P)[:, None], np.arange(P)[None, :]
    same = (j // CHUNK) == (i // CHUNK)
    c = np.zeros((P, C_COLS), np.float32)
    inv = 1.0 / TAU
    c[:, C_ID:C_ID + P] = j == i
    c[:, C_ONE:C_ONE + P] = 1.0
    c[:, C_PREF_F:C_PREF_F + P] = ((j <= i) & same) * inv
    c[:, C_PREF_B:C_PREF_B + P] = ((j >= i) & same) * inv
    c[:, C_SUF_F:C_SUF_F + P] = ((j > i) & same) * inv
    c[:, C_SUF_B:C_SUF_B + P] = ((j < i) & same) * inv
    c[:, C_CTX_F:C_CTX_F + P] = (j > i) * inv
    c[:, C_CTX_B:C_CTX_B + P] = (j < i) * inv
    c[:, C_ALL:C_ALL + P] = inv
    c[:, C_PREV:C_PREV + P] = np.where(i >= j, 0.0, NEG)
    c[:, C_NEXT:C_NEXT + P] = np.where(i <= j, 0.0, NEG)
    c[:, C_IND] = (np.arange(P) < CHUNK) * inv
    c[:, C_IND + 1] = (np.arange(P) >= CHUNK) * inv
    c[:, C_HEAD:C_COLS] = (np.arange(P) // DK)[:, None] == np.arange(4)
    tok = np.arange(SEQ)
    half = HEAD // 2
    freq = (np.float32(ROPE_BASE) ** (-np.arange(0, half, 2, dtype=np.float32) / np.float32(half))).astype(np.float32)
    ar = (tok // GRID_W).astype(np.float32)[:, None] * freq
    ac = (tok % GRID_W).astype(np.float32)[:, None] * freq
    cos = np.ones((TOK, HEAD), np.float32)
    sin = np.zeros((TOK, HEAD), np.float32)
    cos[:SEQ] = np.cos(np.concatenate([ar, ar, ac, ac], 1))
    sin[:SEQ] = np.sin(np.concatenate([-ar, ar, -ac, ac], 1))
    tile = lambda a: np.ascontiguousarray(a.reshape(TT, P, HEAD).transpose(1, 0, 2).reshape(P, TT * HEAD))
    return c, tile(cos), tile(sin)


class Event:

    def __init__(self, nc, ctx, name, per=1, dma=False, credit=None):
        self.sem = ctx.enter_context(nc.semaphore(name))
        self.per = per * (16 if dma else 1)
        self.one = 16 if dma else 1
        self.credit = credit if credit is not None else 0 if dma else 2

    def open(self, eng):
        eng.sem_inc(self.sem, self.credit * self.per)

    def at(self, t, k=None):
        return (t + self.credit) * self.per + (self.per if k is None else k * self.one)


def build(nc, xall, c, c_ctx, w_ada, b_ada, g_pre_mix, g_post_mix, g_pre_ffn, g_post_ffn, w_in, attn_sink,
          w_gate_fwd, b_gate_fwd, w_gate_bwd, b_gate_bwd, g_gla, w_out, w_ffn_in, w_ffn_out, consts, cosd, sind, out,
          proj, mixd, x2d):
    top = ExitStack()
    with top:
        persist(nc, top, locals())


def persist(nc, top, A):
    def sb(stack, name, shape, dt=F32):
        return stack.enter_context(nc.sbuf_tensor(name, shape, dt))

    S = dict(A)
    S["sb"] = sb
    S["con"] = sb(top, "con", [P, C_COLS])
    S["pcol"] = sb(top, "pcol", [P, 80])
    S["A1"] = sb(top, "A1", [P, KT, 2])
    S["B1"] = sb(top, "B1", [P, 16, 2])
    S["A2"] = sb(top, "A2", [P, KT])
    S["B2"] = sb(top, "B2", [P, 16])
    S["G1"] = sb(top, "G1", [P, D])
    S["G2"] = sb(top, "G2", [P, D])
    S["epsb"] = sb(top, "epsb", [P, 1])
    S["scol"] = sb(top, "scol", [P, 16])
    with ExitStack() as s:
        S["hTh"] = sb(s, "hTh", [P, KT, TOK], F32R)
        S["hTl"] = sb(s, "hTl", [P, KT, TOK], F32R)
        S["raw"] = sb(s, "raw", [P, 2, 4, 512])
        S["raw_in"] = [s.enter_context(nc.semaphore(f"p_raw_in{n}")) for n in range(2)]
        modulate_block(nc, S)
        project_block(nc, S)
    S["wraw"] = sb(top, "wraw", [P, 4 * D])
    S["wout_in"] = top.enter_context(nc.semaphore("wout_in"))
    S["mix_stored"] = [Event(nc, top, f"mix_stored{u}", dma=True, credit=1) for u in range(2)]
    S["ffn_in"] = Event(nc, top, "ffn_in", 2, dma=True)
    with ExitStack() as s:
        S["cos"] = sb(s, "cos", [P, TT, HEAD])
        S["sin"] = sb(s, "sin", [P, TT, HEAD])
        S["keyT"] = sb(s, "keyT", [P, 2, KVH, (TT + 1) * P], F32R)
        S["val"] = sb(s, "val", [P, TT + 1, P])
        S["la"] = sb(s, "la", [P, TT, 512])
        S["state"] = sb(s, "state", [P, 4, NCH + 1, HEAD])
        S["dec"] = sb(s, "dec", [P, 4, NCH])
        S["row"] = sb(s, "xrow", [P, 2, COLS])
        S["rot"] = sb(s, "qrot", [P, AH, HEAD])
        S["rot2"] = sb(s, "qrot2", [P, AH, HEAD])
        S["prev_mask"] = sb(s, "prev_mask", [P, LT, P], BF16)
        S["next_mask"] = sb(s, "next_mask", [P, LT, P], BF16)
        S["identb"] = sb(s, "identb", [P, P], BF16)
        S["amask"] = sb(s, "amask", [P, 2, P])
        S["nsink"] = sb(s, "nsink", [P, AH])
        S["gain"] = sb(s, "gain", [P, HEAD])
        S["mix_row_in"] = [Event(nc, s, f"x_row_in{u}", dma=True) for u in range(2)]
        S["q_rotated"] = Event(nc, s, "x_rotated", 4)
        keys_block(nc, S)
        mix_block(nc, S)
    with ExitStack() as s:
        S["h2h"] = sb(s, "h2h", [P, KT, SEQ], F32R)
        S["h2l"] = sb(s, "h2l", [P, KT, SEQ], F32R)
        output_block(nc, S)
        ffn_block(nc, S)


def modulate_block(nc, S):
    sb, con, pcol, A1, B1, scol, epsb = (S[n] for n in ("sb", "con", "pcol", "A1", "B1", "scol", "epsb"))
    hTh, hTl, raw = S["hTh"], S["hTl"], S["raw"]
    with ExitStack() as s:
        def sem(name):
            return s.enter_context(nc.semaphore("m_" + name))
        WS, XS = 3, 4
        prow = sb(s, "prow", [80, P])
        wada = sb(s, "wada", [P, WS, 2 * D])
        xin = sb(s, "xin", [P, XS, D])
        junk = sb(s, "junk", [P, D])
        ssq = sb(s, "ssq", [P, TT])
        rst = sb(s, "rst", [P, TT])
        xnT = sb(s, "xnT", [P, KT, TOK])
        modrow = sb(s, "modrow", [2, 2 * D])
        psA = s.enter_context(nc.psum_tensor("psA", [P, 4, 512], F32))
        psX = s.enter_context(nc.psum_tensor("psX", [P, 4, 512], F32))
        rows_in, con_in, eps_set = sem("rows_in"), sem("con_in"), sem("eps_set")
        ada_in, x_in = [sem(f"ada_in{n}") for n in range(WS)], [sem(f"x_in{n}") for n in range(XS)]
        rows_turned, cols_ready, silu_ready = sem("rows_turned"), sem("cols_ready"), sem("silu_ready")
        ada_used, mod_row, mod_turned, mod_col = sem("ada_used"), sem("mod_row"), sem("mod_turned"), sem("mod_col")
        squares, root, rstd, normed, turned, turned_out = (sem(n) for n in ("squares", "root", "rstd", "normed", "turned", "turned_out"))
        full, hi, lo = sem("full"), sem("hi"), [sem("lo_dve"), sem("lo_pool")]
        full_ctx = sem("full_ctx")
        POOL_K = (0, 3, 6)
        ORDER = [("ada", 0), ("x", 0), ("x", 1), ("ada", 1), ("x", 2), ("ada", 2), ("x", 3), ("x", 4), ("ada", 3), ("x", 5), ("ada", 4),
                 ("x", 6), ("ada", 5), ("x", 7), ("x", 8), ("ada", 6), ("x", 9), ("ada", 7)]
        assert len(ORDER) == TT + KT
        block = s.enter_context(nc.Block())

        @block.sync
        def _(sp):
            rows = [(S["c"], 0, 8), (S["c_ctx"], 8, 8), (S["g_pre_mix"], 16, 8), (S["g_pre_ffn"], 24, 8), (S["b_ada"], 32, 48)]
            for src, r, n in rows:
                sp.dma_start(prow[r:r + n, :], src.rearrange("(r p) -> r p", p=P)).then_inc(rows_in, 16)
            sp.dma_start(con[:, :], S["consts"]).then_inc(con_in, 16)
            for what, t in ORDER:
                if what == "ada":
                    if t >= WS:
                        sp.wait_ge(ada_used, t - WS + 1)
                    sp.dma_start(wada[:, t % WS, :], S["w_ada"][t * P:(t + 1) * P, 0:2 * D]).then_inc(ada_in[t % WS], 16)
                else:
                    if t >= XS:
                        sp.wait_ge(turned, t - XS + 1)
                    sp.dma_start(xin[:, t % XS, :], S["xall"][t * P:(t + 1) * P, :]).then_inc(x_in[t % XS], 16)
            load_chunk(sp, S, 0, 0)
            load_chunk(sp, S, 0, 1)

        @block.scalar
        def _(act):
            act.wait_ge(cols_ready, 1)
            act.activation(scol[:, :], pcol[:, 0:16], ACT.Silu).then_inc(silu_ready, 1)
            act.wait_ge(eps_set, 1)

            def evacuate(t):
                act.wait_ge(turned, t + 1)
                act.activation(xnT[:, :, t * P:(t + 1) * P], psX[:, 2 * (t % 2):2 * (t % 2) + 2, :].rearrange("p b (k j) -> p (b k) j", j=P),
                               ACT.Copy).then_inc(turned_out, 1)
            for t in range(TT):
                act.wait_ge(squares, t + 1)
                act.activation(rst[:, t:t + 1], ssq[:, t:t + 1], ACT.Sqrt, scale=1.0 / D, bias=epsb[:, :]).then_inc(root, 1)
                if t:
                    evacuate(t - 1)
            evacuate(TT - 1)
            act.wait_ge(ada_used, KT)
            act.activation(modrow[:, D:2 * D], psA[0:2, 2:4, :].rearrange("p b n -> p (b n)"), ACT.Copy).then_inc(mod_row, 1)
            act.wait_ge(turned_out, TT)
            act.wait_ge(mod_col, 2)
            for k in range(KT):
                for c in ((0, 1) if k == 0 else (k + 1,)):
                    if c < KT:
                        act.activation(xnT[:, c, SEQ:TOK], xnT[:, c, SEQ:TOK], ACT.Identity, scale=A1[:, c, 1:2], bias=B1[:, c, 1:2]).then_inc(full_ctx, 1)
                act.wait_ge(full, k + 1)
                act.wait_ge(full_ctx, k + 1)
                act.activation(hTh[:, k, :], xnT[:, k, :], ACT.Copy).then_inc(hi, 1)

        @block.gpsimd
        def _(pool):
            for k in POOL_K:
                pool.wait_ge(hi, k + 1)
                pool.tensor_tensor(hTl[:, k, :], xnT[:, k, :], hTh[:, k, :].bitcast(F32), ALU.subtract).then_inc(lo[1], 1)

        @block.tensor
        def _(pe):
            pe.wait_ge(rows_in, 80)
            pe.wait_ge(con_in, 16)
            pe.transpose(psA[:, 0, 0:80], prow[:, :], con[0:80, C_ID:C_ID + 80]).then_inc(rows_turned, 1)
            pe.wait_ge(silu_ready, 1)
            lhs = scol[:, :].rearrange("p (w k) -> p k w", w=2)
            for what, t in ORDER:
                if what == "ada":
                    pe.wait_ge(ada_in[t % WS], 16 * (t // WS + 1))
                    for n in range(4):
                        mm = pe.matmul(psA[0:2, n, :], lhs[:, t, :], wada[:, t % WS, n * 512:(n + 1) * 512],
                                       start=(t == 0), stop=(t == KT - 1))
                    mm.then_inc(ada_used, 1)
                else:
                    pe.wait_ge(normed, t + 1)
                    if t >= 2:
                        pe.wait_ge(turned_out, t - 1)
                    for k in range(KT):
                        mm = pe.transpose(psX[:, 2 * (t % 2) + k // 4, (k % 4) * P:(k % 4 + 1) * P], xin[:, t % XS, k * P:(k + 1) * P],
                                          con[:, C_ID:C_ID + P])
                    mm.then_inc(turned, 1)
            pe.wait_ge(mod_row, 2)
            for n in range(16):
                mm = pe.transpose(psA[:, 0, 2 * n:2 * n + 2], modrow[:, n * P:(n + 1) * P], con[0:2, C_ID:C_ID + 2])
            mm.then_inc(mod_turned, 1)

        @block.vector
        def _(dve):
            dve.memset(epsb[:, :], EPS).then_inc(eps_set, 1)
            dve.wait_ge(rows_turned, 1)
            dve.tensor_copy(pcol[:, :], psA[:, 0, 0:80]).then_inc(cols_ready, 1)

            def square(t):
                dve.wait_ge(x_in[t % XS], 16 * (t // XS + 1))
                if t:
                    dve.wait_ge(squares, t)
                dve.tensor_tensor_reduce(out=junk[:, :], in0=xin[:, t % XS, :], in1=xin[:, t % XS, :], scale=1.0, scalar=0.0,
                                         op0=ALU.mult, op1=ALU.add, accum_out=ssq[:, t:t + 1]).then_inc(squares, 1)

            square(0)
            for t in range(TT):
                if t < TT - 1:
                    square(t + 1)
                dve.wait_ge(root, t + 1)
                dve.reciprocal(rst[:, t:t + 1], rst[:, t:t + 1]).then_inc(rstd, 1)
                dve.wait_ge(rstd, t + 1)
                dve.tensor_scalar(xin[:, t % XS, :], xin[:, t % XS, :], rst[:, t:t + 1], None, ALU.mult).then_inc(normed, 1)
            dve.wait_ge(ada_used, KT)
            dve.tensor_copy(modrow[:, 0:D], psA[0:2, 0:2, :].rearrange("p b n -> p (b n)")).then_inc(mod_row, 1)
            dve.wait_ge(mod_turned, 1)
            dve.tensor_tensor(B1[:, :, :], psA[:, 0, 0:32].rearrange("p (n w) -> p n w", w=2),
                              pcol[:, 32:48].unsqueeze(2).broadcast_to([P, 16, 2]), ALU.add).then_inc(mod_col, 1)
            dve.wait_ge(mod_col, 1)
            dve.scalar_tensor_tensor(A1[:, :, :], B1[:, 8:16, :], 1.0,
                                     pcol[:, 16:24].unsqueeze(2).broadcast_to([P, 8, 2]), ALU.add, ALU.mult).then_inc(mod_col, 1)
            dve.wait_ge(mod_col, 2)
            dve.wait_ge(turned_out, TT)

            def low(k):
                if k not in POOL_K:
                    dve.wait_ge(hi, k + 1)
                    dve.tensor_tensor(hTl[:, k, :], xnT[:, k, :], hTh[:, k, :].bitcast(F32), ALU.subtract).then_inc(lo[0], 1)
            for k in range(KT):
                dve.tensor_scalar(xnT[:, k, 0:SEQ], xnT[:, k, 0:SEQ], A1[:, k, 0:1], B1[:, k, 0:1], ALU.mult, ALU.add).then_inc(full, 1)
                if k >= 2:
                    low(k - 2)
            low(KT - 2)
            low(KT - 1)


def load_chunk(sp, S, ci, half):
    for n, first in enumerate(CHUNKS[ci]):
        sp.dma_start(S["raw"][:, half, :, n * 256:(n + 1) * 256],
                     S["w_in"].rearrange("(k p) n -> p k n", p=P)[:, 4 * half:4 * half + 4, first:first + 256]
                     ).then_inc(S["raw_in"][half], 16)


def project_block(nc, S):
    sb, con, pcol, scol = (S[n] for n in ("sb", "con", "pcol", "scol"))
    hTh, hTl, A2, B2, G1, G2, proj = (S[n] for n in ("hTh", "hTl", "A2", "B2", "G1", "G2", "proj"))
    with ExitStack() as s:
        def sem(name):
            return s.enter_context(nc.semaphore("p_" + name))
        wh = sb(s, "wh", [P, 2, KT, 512], F32R)
        wl = sb(s, "wl", [P, 2, KT, 512], F32R)
        raw, raw_in = S["raw"], S["raw_in"]
        acc = sb(s, "acc", [P, 4 * D])
        ada = sb(s, "ada", [P, 2, 2 * D])
        stage = G2[:, :].rearrange("p (s n) -> p s n", s=2)
        psW = s.enter_context(nc.psum_tensor("psW", [P, 2, 512], F32))
        psG = s.enter_context(nc.psum_tensor("psG", [P, 4, 512], F32))
        psC = s.enter_context(nc.psum_tensor("psC", [P, 512], F32))
        ada_in = [sem(f"ada_in{n}") for n in range(2)]
        acc_step, rows, gate_sum, gates = (sem(n) for n in ("acc_step", "rows", "gate_sum", "gates"))
        hi, lo = sem("hi"), sem("lo")
        done, copied = Event(nc, s, "p_done"), Event(nc, s, "p_copied")
        stored = [Event(nc, s, f"p_stored{u}", dma=True, credit=1) for u in range(2)]
        block = s.enter_context(nc.Block())
        FIRST = [0, 10, 20, 30, 38]
        END = 46

        def width(ci, t):
            return 512 if not isinstance(ci, int) or ci != 2 else NARROW if t < LT else 2 * RANK

        @block.sync
        def _(sp):
            n_ada = 0

            def ada_piece(n):
                if n >= 2:
                    sp.wait_ge(acc_step, n)
                k, h = n // 2, n % 2
                sp.dma_start(ada[:, n % 2, :], S["w_ada"][k * P:(k + 1) * P, (2 + 2 * h) * D:(4 + 2 * h) * D]).then_inc(ada_in[n % 2], 16)

            for ci in range(1, len(CHUNKS)):
                for half in range(2):
                    sp.wait_ge(lo, 2 * ci + half - 1)
                    load_chunk(sp, S, ci, half)
                    for _ in range(2):
                        ada_piece(n_ada)
                        n_ada += 1
            assert n_ada == 16
            for n, (col, gain) in enumerate(((2 * D, S["g_post_mix"]), (5 * D, S["g_post_ffn"]))):
                sp.wait_ge(acc_step, 16 + n)
                sp.dma_start(ada[:, n, 0:D], S["b_ada"][col:col + D].partition_broadcast(P)).then_inc(rows, 16)
                sp.dma_start(ada[:, n, D:2 * D], gain.partition_broadcast(P)).then_inc(rows, 16)

        @block.gpsimd
        def _(pool):
            pool.memset(acc[:, :], 0.0).then_inc(acc_step, 1)

        @block.scalar
        def _(act):
            copied.open(act)
            for u in range(2):
                stored[u].open(act)

            def high(ci, half, slot, before):
                act.wait_ge(raw_in[half], ci * 32 + 32)
                act.wait_ge(done.sem, done.at(before - 1))
                act.activation(wh[:, bass.ds(slot, 1), 4 * half:4 * half + 4, :].rearrange("p s k n -> p (s k) n"),
                               raw[:, half, :, :], ACT.Copy).then_inc(hi, 1)

            def chunk(ci, g0, used, tiles, slot, col, nxt=True):
                for t in range(tiles):
                    n = width(ci, t)
                    act.wait_ge(done.sem, done.at(g0 + t))
                    act.wait_ge(stored[t % 2].sem, stored[t % 2].at(used + (t // 2 - 1)))
                    last = ci if isinstance(ci, int) else -1
                    g = slice(0, 256) if last == 2 and n == NARROW else slice(256, 512) if last == 4 else slice(0, 0)
                    if g.stop:
                        act.activation(stage[:, t % 2, g], psW[:, t % 2, g], ACT.Silu)
                    r = slice(0, 256) if g.start else slice(g.stop, n)
                    act.activation(stage[:, t % 2, r], psW[:, t % 2, r], ACT.Copy).then_inc(copied.sem, 1)
                    act.wait_ge(copied.sem, copied.at(g0 + t))
                    c0 = ZZ if n == 2 * RANK else col
                    act.dma_start(proj[t * P:(t + 1) * P, bass.ds(c0, n)], stage[:, t % 2, 0:n]).then_inc(stored[t % 2].sem, 16)
                    if nxt and t in (1, 4):
                        high(ci + 1, t // 4, slot, g0)

            high(0, 0, 0, 0)
            high(0, 1, 0, 0)
            with act.Fori(0, 2) as i:
                slot = act.snap(i * -1 + 1)
                chunk(i, i * 10, i * 5, TT, slot, act.snap(i * 512))
            chunk(2, FIRST[2], FIRST[2] // 2, TT, 1, GG2)
            chunk(3, FIRST[3], FIRST[3] // 2, LT, 0, QQ)
            chunk(4, FIRST[4], FIRST[4] // 2, LT, 0, GQ, False)
            for u in range(2):
                act.wait_ge(stored[u].sem, stored[u].at(END // 2 - 1))

        @block.vector
        def _(dve):
            steps = [0]

            def low(ci, half):
                dve.wait_ge(hi, 2 * ci + half + 1)
                dve.tensor_tensor(wl[:, ci % 2, 4 * half:4 * half + 4, :], raw[:, half, :, :],
                                  wh[:, ci % 2, 4 * half:4 * half + 4, :].bitcast(F32), ALU.subtract).then_inc(lo, 1)

            def ada_step():
                n = steps[0]
                k, h = n // 2, n % 2
                dve.wait_ge(ada_in[n % 2], 16 * (n // 2 + 1))
                dve.wait_ge(acc_step, n + 1)
                a = acc[:, h * 2 * D:(h + 1) * 2 * D]
                dve.scalar_tensor_tensor(a, ada[:, n % 2, :], scol[:, k:k + 1], a, ALU.mult, ALU.add).then_inc(acc_step, 1)
                steps[0] += 1

            low(0, 0)
            low(0, 1)
            for ci in range(1, 5):
                for half in range(2):
                    low(ci, half)
                    ada_step()
                    ada_step()
            dve.wait_ge(rows, 64)
            dve.wait_ge(acc_step, 17)
            for n in range(2):
                a = acc[:, n * 3 * D:n * 3 * D + D]
                dve.tensor_tensor(a, a, ada[:, n, D:2 * D], ALU.mult).then_inc(acc_step, 1)
                dve.tensor_tensor(ada[:, n, 0:D], ada[:, n, 0:D], ada[:, n, D:2 * D], ALU.mult).then_inc(gates, 1)
            dve.wait_ge(gate_sum, 1)
            dve.wait_ge(gates, 2)
            dve.tensor_tensor(G1[:, :], psG[:, 0:2, :].rearrange("p b n -> p (b n)"), ada[:, 0, 0:D], ALU.add)
            dve.tensor_tensor(B2[:, :], psC[:, 0:16], pcol[:, 32 + 24:32 + 40], ALU.add).then_inc(gates, 1)
            dve.wait_ge(gates, 3)
            dve.scalar_tensor_tensor(A2[:, :], B2[:, 8:16], 1.0, pcol[:, 24:32], ALU.add, ALU.mult)
            for u in range(2):
                dve.wait_ge(stored[u].sem, stored[u].at(END // 2 - 1))
            dve.tensor_tensor(G2[:, :], psG[:, 2:4, :].rearrange("p b n -> p (b n)"), ada[:, 1, 0:D], ALU.add)

        @block.tensor
        def _(pe):
            done.open(pe)

            def tile(ci_sem, g, t, w, col, n):
                if t == 0:
                    pe.wait_ge(lo, ci_sem - 1)
                pe.wait_ge(copied.sem, copied.at(g - 2))
                m = 0
                for k in range(KT):
                    if t == 0 and k == KT // 2:
                        pe.wait_ge(lo, ci_sem)
                    for a, b in ((hTh, wh), (hTl, wh), (hTh, wl)):
                        mm = pe.matmul(psW[:, t % 2, 0:n], a[:, k, t * P:(t + 1) * P], b[:, bass.ds(w, 1), k, col:col + n].rearrange("p s n -> p (s n)"),
                                       start=(m == 0), stop=(m == 3 * KT - 1))
                        m += 1
                mm.then_inc(done.sem, 1)

            with pe.Fori(0, 2) as i:
                for t in range(TT):
                    tile(i * 2 + 2, i * 10 + t, t, i, 0, 512)
            for t in range(TT):
                n = NARROW if t < LT else 2 * RANK
                tile(6, FIRST[2] + t, t, 0, 512 - n, n)
            with pe.Fori(0, 2) as i:
                slot = pe.snap(i * -1 + 1)
                for t in range(LT):
                    tile(i * 2 + 8, i * 8 + FIRST[3] + t, t, slot, 0, 512)
            pe.wait_ge(acc_step, 19)
            one = con[:, C_ONE:C_ONE + P]
            for n in range(4):
                col = (0 if n < 2 else 3 * D) + (n % 2) * 512
                pe.matmul(psG[:, n, :], one, acc[:, col:col + 512], start=True, stop=True)
            for n in range(16):
                mm = pe.matmul(psC[:, n:n + 1], acc[:, D + n * P:D + (n + 1) * P], con[:, C_ONE:C_ONE + 1], start=True, stop=True)
            mm.then_inc(gate_sum, 1)


def rope(pool, rotated, t, x, cos, sin, rot, rot2, heads):
    def table(a):
        return a[:, bass.ds(t, 1), :]
    pool.tensor_tensor(rot[:, :, :], x, table(cos).broadcast_to([P, heads, HEAD]), ALU.mult).then_inc(rotated.sem, 1)
    halves = x.rearrange("p h (a b d) -> p h a b d", a=2, b=2)
    out = rot2[:, :, :].rearrange("p h (a b d) -> p h a b d", a=2, b=2)
    signed = table(sin).rearrange("p s (a b d) -> p s a b d", a=2, b=2)
    for b in range(2):
        pool.tensor_tensor(out[:, :, :, b, :], halves[:, :, :, 1 - b, :],
                           signed[:, :, :, b, :].broadcast_to([P, heads, 2, HEAD // 4]), ALU.mult).then_inc(rotated.sem, 1)
    pool.wait_ge(rotated.sem, rotated.at(t, 3))
    pool.tensor_tensor(rot[:, :, :], rot[:, :, :], rot2[:, :, :], ALU.add).then_inc(rotated.sem, 1)


def keys_block(nc, S):
    sb, con, proj = S["sb"], S["con"], S["proj"]
    cos, sin, keyT, val, la, state, dec = (S[n] for n in ("cos", "sin", "keyT", "val", "la", "state", "dec"))
    with ExitStack() as s:
        def sem(name):
            return s.enter_context(nc.semaphore("k_" + name))

        def ev(name, per=1, dma=False):
            return Event(nc, s, "k_" + name, per, dma)
        ZR, ZK = 2 * RANK, 6 * RANK + 2
        wraw = sb(s, "wgraw", [ZK, 512])
        wg = sb(s, "wg", [ZK, 512], F32R)
        z3 = sb(s, "z3", [P, 2, 3, ZR], F32R)
        kv = sb(s, "kv", [P, 2, 256])
        gk = sb(s, "gk", [P, 2, 256])
        gv = sb(s, "gv", [P, 2, 512])
        z = sb(s, "z", [P, 2, 2 * RANK])
        zT = sb(s, "zT", [ZK, 2, P], F32R)
        rot = sb(s, "rot", [P, KVH, HEAD])
        rot2 = sb(s, "rot2", [P, KVH, HEAD])
        kdup = sb(s, "kdup", [P, 2, KVH, 2, HEAD], F32R)
        mag = sb(s, "mag", [P, 512])
        lat = sb(s, "lat", [P, 2, 512])
        grow = sb(s, "grow", [P, 2, 512])
        kd = sb(s, "kd", [P, 2, 2, 256])
        ps = s.enter_context(nc.psum_tensor("kps", [P, 8, 512], F32))
        psZ, psK, psU, psD = (ps[:, n, :] for n in range(4))
        psL = [ps[:, 4, :], ps[:, 5, :]]
        psS = ps[:, 6:8, 0:256]
        z_split = ev("z_split", 2)
        consts_in, wg_in, zeros_set = sem("consts_in"), sem("wg_in"), sem("zeros_set")
        kv_in, gk_in, gv_in, z_in = ([ev(f"{n}_in{u}", dma=True) for u in range(2)] for n in ("kv", "gk", "gv", "z"))
        rotated, k_split = ev("rotated", 4), ev("k_split", 4)
        k_turned, k_out = ev("k_turned"), ev("k_out")
        z_turned, z_out, logits = ev("z_turned"), ev("z_out"), ev("logits")
        softplus, decays, val_kept, la_kept = ev("softplus", 3), ev("decays"), ev("val_kept"), ev("la_kept")
        sums, grown, scaled = ev("sums"), ev("grown"), ev("scaled")
        whole, whole_exp, moved, added = ev("whole"), ev("whole_exp"), ev("moved"), ev("added")
        ctx_products, ctx_exp, ctx_k = (sem(n) for n in ("ctx_products", "ctx_exp", "ctx_k"))
        block = s.enter_context(nc.Block())

        def increment(q, ch):
            return ch + (q < 2)

        def load_gates(eng, d):
            eng.wait_ge(zeros_set, 1)
            w, b = (("w_gate_fwd", "b_gate_fwd"), ("w_gate_bwd", "b_gate_bwd"))[d]
            eng.dma_start(wraw[d * RANK:(d + 1) * RANK, d * 256:(d + 1) * 256], S[w]).then_inc(wg_in, 16)
            eng.dma_start(wraw[3 * ZR:ZK, d * 256:(d + 1) * 256], S[b].partition_broadcast(2)).then_inc(wg_in, 16)

        def tiles(eng, body):
            body(0, 0, 0, first=True)
            with eng.Fori(0, LT // 2 - 1) as i:
                for v in range(2):
                    body(i * 2 + (v + 1), 1 - v, i + v)
            body(LT - 1, 1, LT // 2 - 1)

        @block.sync
        def _(sp):
            def early(t, u, rows):
                sp.wait_ge(z_turned.sem, z_turned.at(t - 2))
                sp.wait_ge(rotated.sem, rotated.at(t - 2))
                sp.wait_ge(val_kept.sem, val_kept.at(t - 2))
                sp.dma_start(z[:, u, :], proj[rows, ZZ:ZZ + 2 * RANK]).then_inc(z_in[u].sem, 16)
                sp.dma_start(kv[:, u, :], proj[rows, KK:KK + 256]).then_inc(kv_in[u].sem, 16)
                sp.wait_ge(scaled.sem, scaled.at(t - 2))
                sp.dma_start(gk[:, u, :], proj[rows, GK:GK + 256]).then_inc(gk_in[u].sem, 16)

            def late(t, u, rows):
                sp.wait_ge(moved.sem, moved.at(t - 2))
                sp.dma_start(gv[:, u, :], proj[rows, GV:GV + 512]).then_inc(gv_in[u].sem, 16)

            load_gates(sp, 0)
            early(0, 0, slice(0, P))
            with sp.Fori(0, LT // 2) as i:
                for v in range(2):
                    t = sp.snap(i * 2 + (v + 1))
                    early(t, 1 - v, bass.ds(sp.snap(t * P), P))
                    late(sp.snap(t - 1), v, bass.ds(sp.snap(t * P - P), P))
            early(TT - 1, 1, slice((TT - 1) * P, TOK))
            for t in (LT, TT - 1):
                sp.wait_ge(moved.sem, moved.at(t - 2))
                sp.dma_start(gv[:, t % 2, :], proj[t * P:(t + 1) * P, GV:GV + 512]).then_inc(gv_in[t % 2].sem, 16)
            sp.dma_start(S["nsink"][:, :], S["attn_sink"].partition_broadcast(P)).then_inc(wg_in, 16)
            sp.dma_start(S["gain"][:, :], S["g_gla"].partition_broadcast(P)).then_inc(wg_in, 16)
            sp.dma_start(S["row"][:, 0, :], proj[0:P, :]).then_inc(S["mix_row_in"][0].sem, 16)
            sp.dma_start(S["wraw"][:, :].rearrange("p (k n) -> p k n", n=D), S["w_out"].rearrange("(k p) n -> p k n", p=P)[:, 0:4, :]).then_inc(S["wout_in"], 16)

        @block.gpsimd
        def _(pool):
            for e in (rotated, val_kept, la_kept):
                e.open(pool)

            def keys(t, u, n):
                pool.wait_ge(kv_in[u].sem, kv_in[u].at(n))
                pool.wait_ge(k_split.sem, k_split.at(t - 1))
                rope(pool, rotated, t, kv[:, u, 0:P].rearrange("p (h d) -> p h d", h=KVH), cos, sin, rot, rot2, KVH)
                pool.tensor_copy(val[:, bass.ds(t + 1, 1), :].rearrange("p s d -> p (s d)"), kv[:, u, VV:VV + P]).then_inc(val_kept.sem, 1)

            def keep(t, u):
                pool.wait_ge(decays.sem, decays.at(t))
                pool.tensor_copy(la[:, bass.ds(t, 1), :].rearrange("p s d -> p (s d)"), lat[:, u, :]).then_inc(la_kept.sem, 1)

            prev_mask, next_mask, identb, amask = (S[n] for n in ("prev_mask", "next_mask", "identb", "amask"))
            pool.memset(prev_mask[:, 0:1, :], NEG)
            pool.memset(next_mask[:, LT - 1:LT, :], NEG)
            pool.tensor_copy(prev_mask[:, 1:LT, :], con[:, C_PREV:C_PREV + P].unsqueeze(1).broadcast_to([P, LT - 1, P]))
            pool.tensor_copy(next_mask[:, 0:LT - 1, :], con[:, C_NEXT:C_NEXT + P].unsqueeze(1).broadcast_to([P, LT - 1, P]))
            pool.tensor_copy(identb[:, :], con[:, C_ID:C_ID + P])
            pool.tensor_scalar(amask[:, 0, :], con[:, C_PREF_F:C_PREF_F + P], TAU, None, ALU.mult)
            pool.tensor_scalar(amask[:, 1, :], con[:, C_PREF_B:C_PREF_B + P], TAU, None, ALU.mult)
            pool.wait_ge(consts_in, 32)
            keys(0, 0, 0)
            with pool.Fori(0, LT // 2) as i:
                for u in range(2):
                    t = i * 2 + u
                    keys(t + 1, 1 - u, i + u)
                    keep(t, u)
            keys(TT - 1, 1, TT // 2 - 1)
            S["q_rotated"].open(pool)
            pool.wait_ge(S["mix_row_in"][0].sem, S["mix_row_in"][0].at(0))
            rope(pool, S["q_rotated"], 0, S["row"][:, 0, QQ:QQ + 512].rearrange("p (h d) -> p h d", h=AH), cos, sin, S["rot"], S["rot2"], AH)

        @block.scalar
        def _(act):
            for e in (softplus, grown, whole_exp, added):
                e.open(act)
            load_gates(act, 1)
            act.dma_start(cos[:, :, :], S["cosd"].rearrange("p (t d) -> p t d", d=HEAD)).then_inc(consts_in, 16)
            act.dma_start(sin[:, :, :], S["sind"].rearrange("p (t d) -> p t d", d=HEAD)).then_inc(consts_in, 16)

            def soft(t, u):
                act.wait_ge(logits.sem, logits.at(t))
                act.wait_ge(decays.sem, decays.at(t - 1))
                act.activation(mag[:, :], psL[u], ACT.Abs).then_inc(softplus.sem, 1)
                act.wait_ge(softplus.sem, softplus.at(t, 1))
                act.activation(mag[:, :], mag[:, :], ACT.Exp, scale=-1.0).then_inc(softplus.sem, 1)
                act.wait_ge(softplus.sem, softplus.at(t, 2))
                act.activation(mag[:, :], mag[:, :], ACT.Ln, bias=1.0).then_inc(softplus.sem, 1)

            def keep_increments(t):
                act.wait_ge(moved.sem, moved.at(t))
                for d in range(2):
                    a = act.activation(state[:, 2 * d:2 * d + 2, bass.ds(t * 2 + increment(2 * d, 0), 2), :].rearrange("p q c d -> p c q d"),
                                       psS[:, :, d * 128:(d + 1) * 128].rearrange("p c (q d) -> p c q d", q=2), ACT.Copy)
                a.then_inc(added.sem, 1)

            def body(t, u, n, first=False):
                act.wait_ge(sums.sem, sums.at(t))
                act.wait_ge(scaled.sem, scaled.at(t - 2))
                act.activation(grow[:, u, :], psU, ACT.Exp).then_inc(grown.sem, 1)
                soft(t + 1, 1 - u)
                act.wait_ge(whole.sem, whole.at(t))
                act.activation(dec[:, :, bass.ds(t * 2, 2)], psD[:, 0:8].rearrange("p (q c) -> p q c", q=4), ACT.Exp).then_inc(whole_exp.sem, 1)
                if not first:
                    keep_increments(t - 1)

            soft(0, 0)
            tiles(act, body)
            soft(TT - 1, 1)
            keep_increments(LT - 1)
            act.wait_ge(ctx_products, 1)
            act.wait_ge(scaled.sem, scaled.at(LT - 1))
            act.activation(grow[:, 0, :], psU, ACT.Exp).then_inc(ctx_exp, 1)
            act.activation(grow[:, 1, :], psL[0], ACT.Exp).then_inc(ctx_exp, 1)
            act.wait_ge(ctx_products, 2)
            for d in range(2):
                act.activation(state[:, 2 * d:2 * d + 2, d * NCH, :], psS[:, 0, d * 128:(d + 1) * 128].rearrange("p (q d) -> p q d", q=2), ACT.Copy)

        @block.vector
        def _(dve):
            for e in (k_split, z_split, k_out, z_out, decays, scaled):
                e.open(dve)
            dve.memset(wraw[:, :], 0.0).then_inc(zeros_set, 1)
            dve.memset(zT[3 * ZR:ZK, :, :].bitcast(F32), 1.0).then_inc(zeros_set, 1)
            dve.memset(val[:, 0, :], 0.0).then_inc(zeros_set, 1)
            dve.memset(keyT[:, :, :, 0:P].bitcast(F32), 0.0).then_inc(zeros_set, 1)

            def split_z(t, u, n):
                dve.wait_ge(z_in[u].sem, z_in[u].at(n))
                dve.wait_ge(z_turned.sem, z_turned.at(t - 2))
                dve.tensor_copy(z3[:, u, 0:3:2, :], z[:, u, :].unsqueeze(1).broadcast_to([P, 2, ZR])).then_inc(z_split.sem, 1)
                dve.wait_ge(z_split.sem, z_split.at(t, 1))
                dve.tensor_tensor(z3[:, u, 1, :], z[:, u, :], z3[:, u, 0, :].bitcast(F32), ALU.subtract).then_inc(z_split.sem, 1)

            def split_gates():
                dve.wait_ge(wg_in, 64)
                dve.tensor_copy(wg[0:ZR, :], wraw[0:ZR, :]).then_inc(zeros_set, 1)
                dve.tensor_copy(wg[3 * ZR:ZK, :], wraw[3 * ZR:ZK, :]).then_inc(zeros_set, 1)
                dve.wait_ge(zeros_set, 6)
                dve.tensor_copy(wg[ZR:2 * ZR, :], wg[0:ZR, :].bitcast(F32)).then_inc(zeros_set, 1)
                dve.tensor_tensor(wg[2 * ZR:3 * ZR, :], wraw[0:ZR, :], wg[0:ZR, :].bitcast(F32), ALU.subtract).then_inc(zeros_set, 1)
                dve.tensor_tensor(wg[3 * ZR:ZK, :], wraw[3 * ZR:ZK, :], wg[3 * ZR:ZK, :].bitcast(F32), ALU.subtract).then_inc(zeros_set, 1)
                dve.wait_ge(zeros_set, 9)
                dve.tensor_copy(wg[3 * ZR:3 * ZR + 1, :], wraw[3 * ZR:3 * ZR + 1, :]).then_inc(zeros_set, 1)

            def z_columns(t, u):
                dve.wait_ge(z_turned.sem, z_turned.at(t))
                dve.wait_ge(logits.sem, logits.at(t - 2))
                dve.tensor_copy(zT[0:3 * ZR, u, :], psZ[0:3 * ZR, 0:P]).then_inc(z_out.sem, 1)

            def split(t):
                dve.wait_ge(rotated.sem, rotated.at(t))
                dve.wait_ge(k_turned.sem, k_turned.at(t - 1))
                for c in range(2):
                    dve.tensor_copy(kdup[:, 0, :, c, :], rot[:, :, :]).then_inc(k_split.sem, 1)
                dve.wait_ge(k_split.sem, k_split.at(t, 2))
                for c in range(2):
                    dve.tensor_tensor(kdup[:, 1, :, c, :], rot[:, :, :], kdup[:, 0, :, c, :].bitcast(F32), ALU.subtract).then_inc(k_split.sem, 1)

            def key_columns(t):
                dve.wait_ge(k_turned.sem, k_turned.at(t))
                dve.tensor_copy(keyT[:, :, :, bass.ds(t * P + P, P)], psK.rearrange("p (s h j) -> p s h j", s=2, h=KVH)).then_inc(k_out.sem, 1)

            def log_decays(t, u):
                dve.wait_ge(softplus.sem, softplus.at(t))
                dve.wait_ge(la_kept.sem, la_kept.at(t - 2))
                dve.wait_ge(whole.sem, whole.at(t - 2))
                dve.scalar_tensor_tensor(lat[:, u, :], psL[u], 0.0, mag[:, :], ALU.min, ALU.subtract).then_inc(decays.sem, 1)

            def scale(t, u):
                return dve.tensor_tensor(kd[:, u, :, :], grow[:, u, :].rearrange("p (d n) -> p d n", d=2),
                                         gk[:, u, :].unsqueeze(1).broadcast_to([P, 2, 256]), ALU.mult)

            split_gates()
            split_z(0, 0, 0)
            split_z(1, 1, 0)
            z_columns(0, 0)
            split(0)
            z_columns(1, 1)
            key_columns(0)
            log_decays(0, 0)
            with dve.Fori(0, LT // 2) as i:
                for u in range(2):
                    t = i * 2 + u
                    split(t + 1)
                    dve.wait_ge(grown.sem, grown.at(t))
                    dve.wait_ge(moved.sem, moved.at(t - 2))
                    dve.wait_ge(gk_in[u].sem, gk_in[u].at(i))
                    scale(t, u).then_inc(scaled.sem, 1)
                    split_z(t + 2, u, i + 1)
                    log_decays(t + 1, 1 - u)
                    z_columns(t + 2, u)
                    key_columns(t + 1)
            split(TT - 1)
            key_columns(TT - 1)
            log_decays(TT - 1, 1)
            dve.wait_ge(wg_in, 96)
            dve.tensor_scalar(S["nsink"][:, :], S["nsink"][:, :], -1.0, None, ALU.mult)
            dve.wait_ge(ctx_exp, 2)
            dve.wait_ge(moved.sem, moved.at(LT - 1))
            for u in range(2):
                dve.wait_ge(gk_in[u].sem, gk_in[u].at(TT // 2 - 1))
                scale(LT + u, u).then_inc(ctx_k, 1)

        @block.tensor
        def _(pe):
            for e in (k_turned, z_turned, logits, sums, whole, moved):
                e.open(pe)
            ident = con[:, C_ID:C_ID + P]

            def turn_z(t, u):
                pe.wait_ge(z_split.sem, z_split.at(t))
                pe.wait_ge(z_out.sem, z_out.at(t - 1))
                pe.transpose(psZ[0:3 * ZR, 0:P], z3[:, u, :, :].rearrange("p c r -> p (c r)").bitcast(F32), ident).then_inc(z_turned.sem, 1)

            def gate_logits(t, u):
                pe.wait_ge(z_out.sem, z_out.at(t))
                pe.wait_ge(decays.sem, decays.at(t - 2))
                pe.matmul(psL[u], zT[:, u, :], wg[:, :], start=True, stop=True).then_inc(logits.sem, 1)

            def turn_keys(t):
                pe.wait_ge(k_split.sem, k_split.at(t))
                pe.wait_ge(k_out.sem, k_out.at(t - 1))
                for m in range(2):
                    for h in range(KVH):
                        mm = pe.transpose(psK[:, (m * KVH + h) * P:(m * KVH + h + 1) * P],
                                          kdup[:, m, h, :, :].rearrange("p c d -> p (c d)").bitcast(F32), ident)
                mm.then_inc(k_turned.sem, 1)

            pe.wait_ge(zeros_set, 10)
            turn_z(0, 0)
            gate_logits(0, 0)
            turn_z(1, 1)
            turn_keys(0)
            def await_increments(t, u, n):
                pe.wait_ge(gv_in[u].sem, gv_in[u].at(n))
                pe.wait_ge(added.sem, added.at(t - 1))
                pe.wait_ge(scaled.sem, scaled.at(t))

            def increments(t, u):
                for d in range(2):
                    for g in range(2):
                        for ch in range(2):
                            for h in range(4):
                                q = d * 2 + g
                                rows = slice(ch * CHUNK, (ch + 1) * CHUNK)
                                mm = pe.matmul(psS[h * DK:(h + 1) * DK, ch, q * HEAD:(q + 1) * HEAD],
                                               kd[rows, u, d, (g * 4 + h) * DK:(g * 4 + h + 1) * DK],
                                               gv[rows, u, (g * 4 + h) * HEAD:(g * 4 + h + 1) * HEAD],
                                               start=True, stop=True, tile_position=(ch * CHUNK, h * DK))
                mm.then_inc(moved.sem, 1)

            def body(t, u, n, first=False):
                pe.wait_ge(decays.sem, decays.at(t))
                pe.wait_ge(grown.sem, grown.at(t - 1))
                pe.matmul(psU[:, 0:256], con[:, C_SUF_F:C_SUF_F + P], lat[:, u, 0:256], start=True, stop=True)
                mm = pe.matmul(psU[:, 256:512], con[:, C_SUF_B:C_SUF_B + P], lat[:, u, 256:512], start=True, stop=True)
                mm.then_inc(sums.sem, 1)
                gate_logits(t + 1, 1 - u)
                pe.wait_ge(whole_exp.sem, whole_exp.at(t - 1))
                for q in range(4):
                    mm = pe.matmul(psD[:, 2 * q:2 * q + 2], lat[:, u, q * P:(q + 1) * P], con[:, C_IND:C_IND + 2], start=True, stop=True)
                mm.then_inc(whole.sem, 1)
                turn_z(t + 2, u)
                if not first:
                    await_increments(t - 1, 1 - u, n + u - 1)
                turn_keys(t + 1)
                if not first:
                    increments(t - 1, 1 - u)

            tiles(pe, body)
            gate_logits(TT - 1, 1)
            turn_keys(TT - 1)
            await_increments(LT - 1, 1, LT // 2 - 1)
            increments(LT - 1, 1)
            pe.wait_ge(decays.sem, decays.at(TT - 1))
            pe.wait_ge(grown.sem, grown.at(LT - 1))
            early, late, every = con[:, C_CTX_B:C_CTX_B + P], con[:, C_CTX_F:C_CTX_F + P], con[:, C_ALL:C_ALL + P]
            pe.matmul(psU[:, 0:256], late, lat[:, 0, 0:256], start=True, stop=False)
            pe.matmul(psU[:, 0:256], every, lat[:, 1, 0:256], start=False, stop=True)
            pe.matmul(psU[:, 256:512], early, lat[:, 0, 256:512], start=True, stop=True)
            pe.matmul(psL[0][:, 0:256], late, lat[:, 1, 0:256], start=True, stop=True)
            pe.matmul(psL[0][:, 256:512], early, lat[:, 1, 256:512], start=True, stop=False)
            pe.matmul(psL[0][:, 256:512], every, lat[:, 0, 256:512], start=False, stop=True).then_inc(ctx_products, 1)
            pe.wait_ge(ctx_k, 2)
            pe.wait_ge(added.sem, added.at(LT - 1))
            for u in range(2):
                pe.wait_ge(gv_in[u].sem, gv_in[u].at(TT // 2 - 1))
            for d in range(2):
                for g in range(2):
                    for h in range(4):
                        n = d * 2 + g
                        for u in range(2):
                            mm = pe.matmul(psS[h * DK:(h + 1) * DK, 0, n * HEAD:(n + 1) * HEAD],
                                           kd[:, u, d, (g * 4 + h) * DK:(g * 4 + h + 1) * DK],
                                           gv[:, u, (g * 4 + h) * HEAD:(g * 4 + h + 1) * HEAD],
                                           start=(u == 0), stop=(u == 1), tile_position=(0, h * DK))
            mm.then_inc(ctx_products, 1)


def mix_block(nc, S):
    sb, con, proj = S["sb"], S["con"], S["proj"]
    cos, sin, keyT, val, la, state, dec = (S[n] for n in ("cos", "sin", "keyT", "val", "la", "state", "dec"))
    mixd = S["mixd"]
    with ExitStack() as s:
        def sem(name):
            return s.enter_context(nc.semaphore("x_" + name))

        def ev(name, per=1, dma=False, credit=None):
            return Event(nc, s, "x_" + name, per, dma, credit)
        KEYS = 3 * P + CTX
        row, rot, rot2, prev_mask, next_mask, identb, amask, nsink, gain = (
            S[n] for n in ("row", "rot", "rot2", "prev_mask", "next_mask", "identb", "amask", "nsink", "gain"))
        qs = sb(s, "qs", [P, AH, 2, HEAD], F32R)
        qT = sb(s, "qT", [P, 2, AH * P], F32R)
        prob = sb(s, "prob", [P, 2, KEYS])
        probT = sb(s, "probT", [P, 2, KEYS])
        mx = sb(s, "mx", [P, AH])
        negm = sb(s, "negm", [P, AH])
        den = sb(s, "den", [P, AH])
        snk = sb(s, "snk", [P, AH])
        mix = sb(s, "mix", [P, 2, D])
        expb = sb(s, "expb", [P, 2, 512])
        qd = sb(s, "qd", [P, 512])
        ki = sb(s, "ki", [P, 512])
        qkT = sb(s, "qkT", [P, 8, P])
        qspread = sb(s, "qspread", [P, 4, 4, P])
        am = sb(s, "am", [P, 4, 4, P])
        decayed = sb(s, "decayed", [P, 2, HEAD])
        st = sb(s, "st", [P, 4, 2, 4, HEAD])
        gg = sb(s, "gg", [P, 512])
        sq = sb(s, "sq", [P, 512])
        ssq = sb(s, "gssq", [P, GH])
        rs = sb(s, "grs", [P, GH])
        ps = s.enter_context(nc.psum_tensor("xps", [P, 8, 512], F32))
        flat = ps[:, :, :].rearrange("p b n -> p (b n)")
        psP = flat[:, 4 * 512:6 * 512]
        psO = flat[:, 6 * 512:7 * 512]
        psM = flat[:, 7 * 512:8 * 512]
        scan_fwd, scan_bwd = sem("scan_fwd"), sem("scan_bwd")
        row_in, rotated, q_hi, q_lo = S["mix_row_in"], S["q_rotated"], ev("q_hi"), ev("q_lo")
        turned, evac = ev("turned", 9), ev("evac", 9)
        scores, shifted, exps, pv = ev("scores", 8), ev("shifted", 16), ev("exps", 8), ev("pv", 8)
        sink_exp, attn = ev("sink_exp"), ev("attn", 4)
        prefix, expd, q_dec, k_inv = ev("prefix"), ev("expd"), ev("q_dec"), ev("k_inv")
        gq_turned, gq_kept, gk_turned, gk_kept = (ev(n) for n in ("gq_turned", "gq_kept", "gk_turned", "gk_kept"))
        gq_spread = ev("gq_spread", 2)
        inner, masked, gla, states, gained = ev("inner", 4), ev("masked", 4), ev("gla"), ev("states"), ev("gained")
        taken, meansq, rstd, mixed = ev("taken"), ev("meansq"), ev("rstd", 2), ev("mixed", 2)
        stored = S["mix_stored"]
        block = s.enter_context(nc.Block())

        def score_tile(h):
            return flat[:, (h % 2) * 1024 + P:(h % 2) * 1024 + P + KEYS]

        def tiles(eng, body):
            body(0, 0, 0, first=True)
            with eng.Fori(0, LT // 2 - 1) as i:
                for v in range(2):
                    body(i * 2 + (v + 1), 1 - v, i + v)
            body(LT - 1, 1, LT // 2 - 1, last=True)

        @block.sync
        def _(sp):
            for u in range(2):
                stored[u].open(sp)

            def load(t, u):
                sp.wait_ge(gla.sem, gla.at(t - 2))
                sp.wait_ge(gained.sem, gained.at(t - 2))
                sp.wait_ge(k_inv.sem, k_inv.at(t - 2))
                sp.wait_ge(rotated.sem, rotated.at(t - 2))
                sp.dma_start(row[:, u, :], proj[bass.ds(t * P, P), :]).then_inc(row_in[u].sem, 16)

            def store(t, u):
                sp.wait_ge(mixed.sem, mixed.at(t))
                sp.wait_ge(attn.sem, attn.at(t))
                sp.dma_start(mixd[bass.ds(t * P, P), :], mix[:, u, :]).then_inc(stored[u].sem, 16)

            def body(t, u, n, first=False, last=False):
                t = t if first or last else sp.snap(t)
                if not last:
                    load(t + 1 if first else sp.snap(t + 1), 1 - u)
                if not first:
                    store(t - 1 if last else sp.snap(t - 1), 1 - u)

            tiles(sp, body)
            store(LT - 1, 1)
            sp.wait_ge(stored[0].sem, stored[0].at(LT // 2 - 1))
            sp.wait_ge(stored[1].sem, stored[1].at(LT // 2 - 2))

        @block.gpsimd
        def _(pool):
            for e in (k_inv, states, gained):
                e.open(pool)

            def scan_forward():
                with pool.Fori(0, NCH - 1) as c:
                    pool.wait_ge(scan_fwd, c * 2 + 2)
                    pool.tensor_tensor(decayed[:, :, :], state[:, 0:2, bass.ds(c, 1), :].rearrange("p q s d -> p q (s d)"),
                                       dec[:, 0:2, bass.ds(c, 1)].broadcast_to([P, 2, HEAD]), ALU.mult).then_inc(scan_fwd, 1)
                    new = state[:, 0:2, bass.ds(c + 1, 1), :].rearrange("p q s d -> p q (s d)")
                    pool.wait_ge(scan_fwd, c * 2 + 3)
                    pool.tensor_tensor(new, new, decayed[:, :, :], ALU.add).then_inc(scan_fwd, 1)

            def turn_queries(t, u, n):
                pool.wait_ge(row_in[u].sem, row_in[u].at(n))
                pool.wait_ge(q_hi.sem, q_hi.at(t - 1))
                pool.wait_ge(q_lo.sem, q_lo.at(t - 1))
                rope(pool, rotated, t, row[:, u, QQ:QQ + 512].rearrange("p (h d) -> p h d", h=AH), cos, sin, rot, rot2, AH)

            def body(t, u, n, first=False, last=False):
                pool.wait_ge(expd.sem, expd.at(t))
                pool.wait_ge(gk_turned.sem, gk_turned.at(t - 1))
                pool.tensor_tensor(ki[:, :].rearrange("p (d n) -> p d n", d=2), expb[:, 1, :].rearrange("p (d n) -> p d n", d=2),
                                   row[:, u, GK:GK + 256].unsqueeze(1).broadcast_to([P, 2, 256]), ALU.mult).then_inc(k_inv.sem, 1)
                if not last:
                    turn_queries(t + 1, 1 - u, n + u)
                if first:
                    pool.wait_ge(scan_fwd, 2 * NCH)
                    pool.wait_ge(scan_bwd, 2 * (NCH - 1))
                pool.wait_ge(gla.sem, gla.at(t - 1))
                for q in range(4):
                    a = pool.tensor_tensor(st[:, q, :, :, :], state[:, q, bass.ds(t * 2 + q // 2, 2), :].unsqueeze(2).broadcast_to([P, 2, 4, HEAD]),
                                           con[:, C_HEAD:C_COLS].unsqueeze(1).unsqueeze(3).broadcast_to([P, 2, 4, HEAD]), ALU.mult)
                a.then_inc(states.sem, 1)
                pool.wait_ge(mixed.sem, mixed.at(t - 1))
                for m, col in enumerate((GG1, GG2)):
                    a = pool.tensor_tensor(gg[:, m * 256:(m + 1) * 256].rearrange("p (h d) -> p h d", d=HEAD),
                                           row[:, u, col:col + 256].rearrange("p (h d) -> p h d", d=HEAD),
                                           gain[:, :].unsqueeze(1).broadcast_to([P, 4, HEAD]), ALU.mult)
                a.then_inc(gained.sem, 1)

            pool.sem_inc(scan_fwd, 2)
            scan_forward()
            tiles(pool, body)

        @block.scalar
        def _(act):
            for e in (q_hi, exps, sink_exp, expd, gq_spread, taken, rstd):
                e.open(act)

            def high(t):
                act.wait_ge(rotated.sem, rotated.at(t))
                act.wait_ge(turned.sem, turned.at(t - 1, 1))
                act.activation(qs[:, :, 0, :], rot[:, :, :], ACT.Copy).then_inc(q_hi.sem, 1)

            def take(t, u, n):
                act.wait_ge(gla.sem, gla.at(t))
                act.wait_ge(stored[u].sem, stored[u].at(n - 1))
                act.wait_ge(meansq.sem, meansq.at(t - 1))
                act.activation(mix[:, u, 512:1024], psM, ACT.Copy)
                act.activation(sq[:, :], psM, ACT.Square).then_inc(taken.sem, 1)

            def root(t):
                act.wait_ge(meansq.sem, meansq.at(t))
                act.wait_ge(mixed.sem, mixed.at(t - 1, 1))
                act.activation(rs[:, :], ssq[:, :], ACT.Ln, scale=1.0 / HEAD, bias=S["epsb"][:, :]).then_inc(rstd.sem, 1)
                act.wait_ge(rstd.sem, rstd.at(t, 1))
                act.activation(rs[:, :], rs[:, :], ACT.Exp, scale=-0.5).then_inc(rstd.sem, 1)

            def body(t, u, n, first=False, last=False):
                for h in range(AH):
                    act.wait_ge(shifted.sem, shifted.at(t, 2 * h + 2))
                    act.wait_ge(turned.sem, turned.at(t, h) if h >= 2 else turned.at(t - 1, 8 + h))
                    if h == 0:
                        act.wait_ge(attn.sem, attn.at(t - 1))
                    act.activation(prob[:, h % 2, :], score_tile(h), ACT.Exp, scale=0.125, bias=negm[:, h:h + 1],
                                   accum_out=den[:, h:h + 1]).then_inc(exps.sem, 1)
                    if h == 0 and not first:
                        take(t - 1, 1 - u, n + u - 1)
                    if h == 1:
                        act.wait_ge(prefix.sem, prefix.at(t))
                        act.wait_ge(q_dec.sem, q_dec.at(t - 1))
                        act.wait_ge(k_inv.sem, k_inv.at(t - 1))
                        act.activation(expb[:, 0, :], psM, ACT.Exp)
                        act.activation(expb[:, 1, :], psM, ACT.Exp, scale=-1.0).then_inc(expd.sem, 1)
                    if h in (3, 4):
                        act.wait_ge(gq_kept.sem, gq_kept.at(t))
                        act.wait_ge(inner.sem, inner.at(t - 1))
                        for k in range(2 * h - 6, 2 * h - 4):
                            a = act.activation(qspread[:, :, k, :], qkT[:, 0:4, :], ACT.Copy,
                                               scale=con[:, C_HEAD + k:C_HEAD + k + 1])
                        a.then_inc(gq_spread.sem, 1)
                    if h == 4 and not last:
                        high(t + 1)
                    if h == 5 and not first:
                        root(t - 1)
                act.wait_ge(attn.sem, attn.at(t, 1))
                act.activation(snk[:, :], snk[:, :], ACT.Exp).then_inc(sink_exp.sem, 1)

            high(0)
            tiles(act, body)
            take(LT - 1, 1, LT // 2 - 1)
            root(LT - 1)

        @block.vector
        def _(dve):
            for e in (q_lo, evac, shifted, attn, q_dec, gq_kept, gk_kept, masked, meansq, mixed):
                e.open(dve)

            def low(t):
                dve.wait_ge(q_hi.sem, q_hi.at(t))
                dve.tensor_tensor(qs[:, :, 1, :], rot[:, :, :], qs[:, :, 0, :].bitcast(F32), ALU.subtract).then_inc(q_lo.sem, 1)

            def queries(t, u):
                dve.wait_ge(turned.sem, turned.at(t, 1))
                dve.wait_ge(scores.sem, scores.at(t - 2))
                dve.tensor_copy(qT[:, u, :], psP).then_inc(evac.sem, 1)

            def maximum(t, h):
                dve.wait_ge(scores.sem, scores.at(t, h + 1))
                if h == 0:
                    dve.wait_ge(exps.sem, exps.at(t - 1))
                dve.reduce_max(mx[:, h:h + 1], score_tile(h), AX.X).then_inc(shifted.sem, 1)
                dve.wait_ge(shifted.sem, shifted.at(t, 2 * h + 1))
                dve.tensor_scalar(negm[:, h:h + 1], mx[:, h:h + 1], -0.125, nsink[:, h:h + 1], ALU.mult, ALU.min).then_inc(shifted.sem, 1)

            def transposed(t, h):
                dve.wait_ge(turned.sem, turned.at(t, h + 2))
                dve.wait_ge(pv.sem, pv.at(t, h - 1) if h >= 2 else pv.at(t - 1, 7 + h))
                dve.tensor_copy(probT[:, h % 2, :], psP[:, 0:KEYS]).then_inc(evac.sem, 1)

            def mask(t, q):
                dve.wait_ge(inner.sem, inner.at(t, q + 1))
                if q == 0:
                    dve.wait_ge(gla.sem, gla.at(t - 1))
                dve.tensor_tensor(am[:, q, :, :], psM.rearrange("p (h j) -> p h j", j=P),
                                  amask[:, q // 2, :].unsqueeze(1).broadcast_to([P, 4, P]), ALU.mult).then_inc(masked.sem, 1)

            def by_head(a):
                return a.rearrange("p (h d) -> p h d", d=HEAD)

            def sum_squares(t):
                dve.wait_ge(taken.sem, taken.at(t))
                dve.wait_ge(rstd.sem, rstd.at(t - 1))
                dve.reduce_sum(ssq[:, :], by_head(sq[:, :]), AX.X).then_inc(meansq.sem, 1)

            def norm(t, u):
                dve.wait_ge(rstd.sem, rstd.at(t))
                dve.tensor_tensor(by_head(mix[:, u, 512:1024]), by_head(mix[:, u, 512:1024]),
                                  rs[:, :].unsqueeze(2).broadcast_to([P, GH, HEAD]), ALU.mult).then_inc(mixed.sem, 1)

            def gate(t, u):
                dve.wait_ge(mixed.sem, mixed.at(t, 1))
                dve.wait_ge(gained.sem, gained.at(t))
                dve.tensor_tensor(mix[:, u, 512:1024], mix[:, u, 512:1024], gg[:, :], ALU.mult).then_inc(mixed.sem, 1)

            def scan_backward(n):
                c = NCH - 1 - n
                if n:
                    dve.wait_ge(scan_bwd, 2 * n)
                for q in (2, 3):
                    dve.scalar_tensor_tensor(state[:, q, c, :], state[:, q, c + 1, :], dec[:, q, c:c + 1], state[:, q, c, :],
                                             ALU.mult, ALU.add).then_inc(scan_bwd, 1)

            def body(t, u, n, first=False, last=False):
                for h in range(AH + 1):
                    if h < AH:
                        maximum(t, h)
                    else:
                        dve.wait_ge(shifted.sem, shifted.at(t))
                        dve.tensor_tensor(snk[:, :], negm[:, :], nsink[:, :], ALU.subtract).then_inc(attn.sem, 1)
                    if h:
                        transposed(t, h - 1)
                    if h == 2:
                        dve.wait_ge(expd.sem, expd.at(t))
                        dve.wait_ge(gq_turned.sem, gq_turned.at(t - 1))
                        dve.scalar_tensor_tensor(qd[:, :].rearrange("p (d n) -> p d n", d=2),
                                                 row[:, u, GQ:GQ + 256].unsqueeze(1).broadcast_to([P, 2, 256]), DK ** -0.5,
                                                 expb[:, 0, :].rearrange("p (d n) -> p d n", d=2), ALU.mult, ALU.mult).then_inc(q_dec.sem, 1)
                    if h == 3:
                        dve.wait_ge(gq_turned.sem, gq_turned.at(t))
                        dve.wait_ge(gla.sem, gla.at(t - 1))
                        dve.tensor_copy(qkT[:, 0:4, :], psM.rearrange("p (b j) -> p b j", j=P)).then_inc(gq_kept.sem, 1)
                    if h == 4:
                        dve.wait_ge(gk_turned.sem, gk_turned.at(t))
                        dve.tensor_copy(qkT[:, 4:8, :], psM.rearrange("p (b j) -> p b j", j=P)).then_inc(gk_kept.sem, 1)
                    if h >= 5:
                        mask(t, h - 5)
                    if first and h < 5:
                        for m in range(3):
                            scan_backward(3 * h + m)
                    if h == 1 and not first:
                        sum_squares(t - 1)
                    if h == 7 and not first:
                        norm(t - 1, 1 - u)
                    if h == 8 and not first:
                        gate(t - 1, 1 - u)
                    if h == 6 and not last:
                        low(t + 1)
                if not last:
                    queries(t + 1, 1 - u)
                dve.wait_ge(sink_exp.sem, sink_exp.at(t))
                dve.tensor_tensor(den[:, :], den[:, :], snk[:, :], ALU.add).then_inc(attn.sem, 1)
                dve.wait_ge(attn.sem, attn.at(t, 2))
                dve.reciprocal(den[:, :], den[:, :]).then_inc(attn.sem, 1)
                dve.wait_ge(attn.sem, attn.at(t, 3))
                dve.wait_ge(pv.sem, pv.at(t))
                dve.wait_ge(stored[u].sem, stored[u].at(n - 1))
                dve.tensor_tensor(by_head(mix[:, u, 0:512]), by_head(psO),
                                  den[:, :].unsqueeze(2).broadcast_to([P, AH, HEAD]), ALU.mult).then_inc(attn.sem, 1)

            low(0)
            queries(0, 0)
            tiles(dve, body)
            sum_squares(LT - 1)
            norm(LT - 1, 1)
            gate(LT - 1, 1)

        @block.tensor
        def _(pe):
            for e in (turned, scores, pv, prefix, gq_turned, gk_turned, inner, gla):
                e.open(pe)
            ident = con[:, C_ID:C_ID + P]

            def queries(t):
                pe.wait_ge(q_lo.sem, q_lo.at(t))
                pe.wait_ge(evac.sem, evac.at(t - 1))
                for h in range(AH):
                    mm = pe.transpose(psP[:, h * P:(h + 1) * P], qs[:, h, :, :].rearrange("p m d -> p (m d)").bitcast(F32), ident)
                mm.then_inc(turned.sem, 1)

            def score(t, u, h):
                if h == 0:
                    pe.wait_ge(evac.sem, evac.at(t, 1))
                pe.wait_ge(exps.sem, exps.at(t, h - 1) if h >= 2 else exps.at(t - 1, 7 + h))
                sc, q, kv = score_tile(h), qT[:, u, h * P:(h + 1) * P], h // 4
                pe.matmul(sc[:, 0:3 * P], q, keyT[:, 0, kv, bass.ds(t * P, 3 * P)], start=True, stop=False)
                pe.matmul(sc[:, 0:P], identb[:, :], prev_mask[:, bass.ds(t, 1), :].rearrange("p s j -> p (s j)"), start=False, stop=False)
                pe.matmul(sc[:, 2 * P:3 * P], identb[:, :], next_mask[:, bass.ds(t, 1), :].rearrange("p s j -> p (s j)"), start=False, stop=False)
                pe.matmul(sc[:, 0:3 * P], q, keyT[:, 1, kv, bass.ds(t * P, 3 * P)], start=False, stop=True)
                for m in range(2):
                    mm = pe.matmul(sc[:, 3 * P:KEYS], q, keyT[:, m, kv, (LT + 1) * P:(TT + 1) * P], start=(m == 0), stop=(m == 1))
                mm.then_inc(scores.sem, 1)

            def turn(t, h):
                pe.wait_ge(exps.sem, exps.at(t, h + 1))
                pe.wait_ge(evac.sem, evac.at(t, h + 1))
                for b in range(KEYS // P):
                    mm = pe.transpose(psP[:, b * P:(b + 1) * P], prob[:, h % 2, b * P:(b + 1) * P], ident)
                mm.then_inc(turned.sem, 1)

            def weigh(t, h):
                pe.wait_ge(evac.sem, evac.at(t, h + 2))
                if h == 0:
                    pe.wait_ge(attn.sem, attn.at(t - 1))
                kv = (h // 4) * HEAD
                for b in range(KEYS // P):
                    v = val[:, bass.ds(t + b, 1), kv:kv + HEAD].rearrange("p s d -> p (s d)") if b < 3 else val[:, LT + 1 + b - 3, kv:kv + HEAD]
                    mm = pe.matmul(psO[:, h * HEAD:(h + 1) * HEAD], probT[:, h % 2, b * P:(b + 1) * P], v,
                                   start=(b == 0), stop=(b == KEYS // P - 1))
                mm.then_inc(pv.sem, 1)

            def prefix_sums(t):
                pe.wait_ge(taken.sem, taken.at(t - 1))
                for d, m in enumerate((C_PREF_F, C_PREF_B)):
                    mm = pe.matmul(psM[:, d * 256:(d + 1) * 256], con[:, m:m + P],
                                   la[:, bass.ds(t, 1), d * 256:(d + 1) * 256].rearrange("p s n -> p (s n)"), start=True, stop=True)
                mm.then_inc(prefix.sem, 1)

            def turn_gla(t, a, event):
                for b in range(4):
                    mm = pe.transpose(psM[:, b * P:(b + 1) * P], a[:, b * P:(b + 1) * P], ident)
                mm.then_inc(event.sem, 1)

            def inner_products(t, q):
                if q == 0:
                    pe.wait_ge(gq_spread.sem, gq_spread.at(t))
                    pe.wait_ge(gk_kept.sem, gk_kept.at(t))
                else:
                    pe.wait_ge(masked.sem, masked.at(t, q))
                pe.matmul(psM, qkT[:, 4 + q, :], qspread[:, q, :, :].rearrange("p h j -> p (h j)"), start=True, stop=True).then_inc(inner.sem, 1)

            def from_states(t):
                pe.wait_ge(masked.sem, masked.at(t))
                pe.wait_ge(states.sem, states.at(t))
                for g in range(2):
                    for d in range(2):
                        for ch in range(2):
                            j = slice(ch * CHUNK, (ch + 1) * CHUNK)
                            pe.matmul(psM[j, g * 256:(g + 1) * 256], qkT[:, d * 2 + g, j],
                                      st[:, d * 2 + g, ch, :, :].rearrange("p h d -> p (h d)"),
                                      start=(g == 0 and d == 0), stop=False, skip_group_check=True)

            def within_chunks(t, u, half):
                for h in range(half * 4, half * 4 + 4):
                    for d in range(2):
                        mm = pe.matmul(psM[:, h * HEAD:(h + 1) * HEAD], am[:, 2 * d + h // 4, h % 4, :],
                                       row[:, u, GV + h * HEAD:GV + (h + 1) * HEAD], start=False, stop=(h == GH - 1 and d == 1),
                                       skip_group_check=True)
                if half:
                    mm.then_inc(gla.sem, 1)

            def body(t, u, n, first=False, last=False):
                for h in range(AH + 1):
                    if h < AH:
                        score(t, u, h)
                    if h == 1 and not first:
                        within_chunks(t - 1, 1 - u, 1)
                    if h == 2:
                        prefix_sums(t)
                    if h >= 1:
                        turn(t, h - 1)
                    if h >= 2:
                        weigh(t, h - 2)
                    if h == 3:
                        pe.wait_ge(q_dec.sem, q_dec.at(t))
                        pe.wait_ge(expd.sem, expd.at(t))
                        turn_gla(t, qd, gq_turned)
                    if h == 4:
                        pe.wait_ge(k_inv.sem, k_inv.at(t))
                        pe.wait_ge(gq_kept.sem, gq_kept.at(t))
                        turn_gla(t, ki, gk_turned)
                    if h >= 5:
                        inner_products(t, h - 5)
                if not last:
                    queries(t + 1)
                weigh(t, AH - 1)
                from_states(t)
                within_chunks(t, u, 0)

            queries(0)
            tiles(pe, body)
            within_chunks(LT - 1, 1, 1)


def output_block(nc, S):
    sb, con, A2, B2, G1, epsb = (S[n] for n in ("sb", "con", "A2", "B2", "G1", "epsb"))
    h2h, h2l, mixd, x2d = (S[n] for n in ("h2h", "h2l", "mixd", "x2d"))
    with ExitStack() as s:
        def sem(name):
            return s.enter_context(nc.semaphore("o_" + name))

        def ev(name, per=1, dma=False, credit=None):
            return Event(nc, s, "o_" + name, per, dma, credit)
        woh = sb(s, "woh", [P, KT, D], F32R)
        wol = sb(s, "wol", [P, KT, D], F32R)
        mix = sb(s, "omix", [P, 2, D])
        x = sb(s, "ox", [P, 2, D])
        mh = sb(s, "omh", [P, 2, KT, P], F32R)
        ml = sb(s, "oml", [P, 2, KT, P], F32R)
        junk = sb(s, "ojunk", [P, D])
        work = sb(s, "owork", [P, 2, D])
        stats = sb(s, "ostats", [P, 2, 4])
        h2 = sb(s, "oh2", [P, KT, P])
        raw = [S["wraw"][:, k * D:(k + 1) * D] for k in range(4)] + [work[:, 0, :], work[:, 1, :], junk[:, :], h2[:, :, :].rearrange("p k j -> p (k j)")]
        ps = s.enter_context(nc.psum_tensor("ops", [P, 8, 512], F32))
        flat = ps[:, :, :].rearrange("p b n -> p (b n)")
        psT, psY, psH = flat[:, 0:1024], [flat[:, 1024:2048], flat[:, 2048:3072]], flat[:, 3072:4096]
        rest_in, hi, lo = [sem(f"rest_in{n}") for n in range(2)], sem("hi"), sem("lo")
        mix_in, x_in = ([ev(f"{n}{u}", dma=True) for u in range(2)] for n in ("mix_in", "x_in"))
        mix_turned, mix_hi, mix_lo, product = ev("mix_turned"), ev("mix_hi"), ev("mix_lo"), ev("product")
        squares, roots, inverse = ev("squares", 2), ev("roots", 2), ev("inverse", 2)
        branch, residual, normed = ev("branch"), ev("residual"), ev("normed")
        turned, modulated, h_hi, h_lo = ev("turned"), ev("modulated"), ev("h_hi"), ev("h_lo")
        stored = [ev(f"stored{u}", dma=True, credit=1) for u in range(2)]
        block = s.enter_context(nc.Block())

        def pipelined(eng, ahead, now, behind):
            ahead(0, 0, 0)
            ahead(1, 1, 0)
            now(0, 0, 0)
            with eng.Fori(0, LT // 2 - 1) as i:
                for u in range(2):
                    t = i * 2 + (u + 1)
                    ahead(t + 1, u, i + 1)
                    now(t, 1 - u, i + u)
                    behind(t - 1, u, i)
            now(LT - 1, 1, LT // 2 - 1)
            behind(LT - 2, 0, LT // 2 - 1)
            behind(LT - 1, 1, LT // 2 - 1)

        def nothing(t, u, n):
            pass

        @block.sync
        def _(sp):
            def load_mix(t, u, n):
                sp.wait_ge(mix_turned.sem, mix_turned.at(t - 2))
                sp.dma_start(mix[:, u, :], mixd[bass.ds(t * P, P), :]).then_inc(mix_in[u].sem, 16)

            def load_x(t, u, n):
                if isinstance(t, int) and t == 0:
                    sp.wait_ge(S["mix_stored"][1].sem, S["mix_stored"][1].at(LT // 2 - 1))
                sp.wait_ge(turned.sem, turned.at(t - 2))
                sp.wait_ge(stored[u].sem, stored[u].at(n - 1))
                sp.dma_start(x[:, u, :], S["xall"][bass.ds(t * P, P), :]).then_inc(x_in[u].sem, 16)
            pipelined(sp, load_mix, load_x, nothing)
            sp.wait_ge(lo, 4)
            load_ffn_in(sp, S, 0)

        @block.gpsimd
        def _(pool):
            residual.open(pool)
            h_lo.open(pool)

            def add(t, u, n):
                pool.wait_ge(branch.sem, branch.at(t))
                pool.wait_ge(x_in[u].sem, x_in[u].at(n))
                pool.tensor_tensor(x[:, u, :], x[:, u, :], work[:, u, :], ALU.add).then_inc(residual.sem, 1)

            def low(t, u, n):
                pool.wait_ge(h_hi.sem, h_hi.at(t))
                pool.tensor_tensor(h2l[:, :, bass.ds(t * P, P)], h2[:, :, :], h2h[:, :, bass.ds(t * P, P)].bitcast(F32),
                                   ALU.subtract).then_inc(h_lo.sem, 1)
            def low_but_last(t, u, n):
                if not isinstance(t, int):
                    low(t, u, n)

            def add_but_last(t, u, n):
                if not (isinstance(t, int) and t == LT - 1):
                    add(t, u, n)
            pipelined(pool, nothing, add_but_last, low_but_last)

        @block.scalar
        def _(act):
            for e in (mix_hi, squares, roots, modulated, h_hi, *stored):
                e.open(act)
            for k in range(4, KT):
                act.dma_start(raw[k], S["w_out"][k * P:(k + 1) * P, :]).then_inc(rest_in[(k - 4) // 2], 16)

            def split(k):
                if k == 0:
                    act.wait_ge(S["wout_in"], 16)
                if k in (4, 6):
                    act.wait_ge(rest_in[(k - 4) // 2], 32)
                act.activation(woh[:, k, :], raw[k], ACT.Copy).then_inc(hi, 1)

            def stat(n, t, u, src):
                act.activation(junk[:, :], src, ACT.Square, accum_out=stats[:, u, 2 * n:2 * n + 1]).then_inc(squares.sem, 1)
                act.wait_ge(squares.sem, squares.at(t, n + 1))
                act.activation(stats[:, u, 2 * n + 1:2 * n + 2], stats[:, u, 2 * n:2 * n + 1], ACT.Sqrt, scale=1.0 / D,
                               bias=epsb[:, :]).then_inc(roots.sem, 1)

            def high(t, u, n):
                act.wait_ge(mix_turned.sem, mix_turned.at(t))
                act.wait_ge(product.sem, product.at(t - 2))
                act.activation(mh[:, u, :, :], psT.rearrange("p (k j) -> p k j", j=P), ACT.Copy).then_inc(mix_hi.sem, 1)

            def split_and_high(t, u, n):
                if isinstance(t, int) and t == 0:
                    for k in range(4):
                        split(k)
                high(t, u, n)
                if isinstance(t, int) and t == 0:
                    for k in range(4, KT):
                        split(k)

            def sums(t, u, n):
                act.wait_ge(product.sem, product.at(t))
                act.wait_ge(squares.sem, squares.at(t - 1))
                act.wait_ge(branch.sem, branch.at(t - 2))
                stat(0, t, u, psY[u])
                act.wait_ge(residual.sem, residual.at(t))
                act.dma_start(x2d[bass.ds(t * P, P), :], x[:, u, :]).then_inc(stored[u].sem, 16)
                act.wait_ge(squares.sem, squares.at(t, 1))
                stat(1, t, u, x[:, u, :])

            def modulate(t, u, n):
                act.wait_ge(turned.sem, turned.at(t))
                act.wait_ge(h_lo.sem, h_lo.at(t - 1))
                for k in range(KT):
                    a = act.activation(h2[:, k, :], psH[:, k * P:(k + 1) * P], ACT.Identity, scale=A2[:, k:k + 1], bias=B2[:, k:k + 1])
                a.then_inc(modulated.sem, 1)
                act.wait_ge(modulated.sem, modulated.at(t))
                act.activation(h2h[:, :, bass.ds(t * P, P)], h2[:, :, :], ACT.Copy).then_inc(h_hi.sem, 1)
            pipelined(act, split_and_high, sums, modulate)
            for u in range(2):
                act.wait_ge(stored[u].sem, stored[u].at(LT // 2 - 1))

        @block.vector
        def _(dve):
            for e in (mix_lo, inverse, branch, normed):
                e.open(dve)
            def split(k):
                dve.wait_ge(hi, k + 1)
                dve.tensor_tensor(wol[:, k, :], raw[k], woh[:, k, :].bitcast(F32), ALU.subtract).then_inc(lo, 1)

            def low(t, u, n):
                dve.wait_ge(mix_hi.sem, mix_hi.at(t))
                dve.tensor_tensor(ml[:, u, :, :], psT.rearrange("p (k j) -> p k j", j=P), mh[:, u, :, :].bitcast(F32), ALU.subtract).then_inc(mix_lo.sem, 1)

            def split_and_low(t, u, n):
                if isinstance(t, int) and t == 0:
                    for k in range(4):
                        split(k)
                low(t, u, n)
                if isinstance(t, int) and t == 0:
                    for k in range(4, KT):
                        split(k)

            def norm(t, u, n):
                dve.wait_ge(roots.sem, roots.at(t, 1))
                dve.reciprocal(stats[:, u, 1:2], stats[:, u, 1:2]).then_inc(inverse.sem, 1)
                dve.wait_ge(inverse.sem, inverse.at(t, 1))
                dve.wait_ge(turned.sem, turned.at(t - 2))
                dve.scalar_tensor_tensor(work[:, u, :], psY[u], stats[:, u, 1:2], G1[:, :], ALU.mult, ALU.mult).then_inc(branch.sem, 1)
                if isinstance(t, int) and t == LT - 1:
                    dve.wait_ge(branch.sem, branch.at(t))
                    dve.wait_ge(x_in[u].sem, x_in[u].at(n))
                    dve.tensor_tensor(x[:, u, :], x[:, u, :], work[:, u, :], ALU.add).then_inc(residual.sem, 1)
                dve.wait_ge(roots.sem, roots.at(t, 2))
                dve.reciprocal(stats[:, u, 3:4], stats[:, u, 3:4]).then_inc(inverse.sem, 1)
                dve.wait_ge(inverse.sem, inverse.at(t, 2))
                dve.wait_ge(branch.sem, branch.at(t))
                dve.tensor_scalar(work[:, u, :], x[:, u, :], stats[:, u, 3:4], None, ALU.mult).then_inc(normed.sem, 1)
            def last_low(t, u, n):
                if isinstance(t, int):
                    dve.wait_ge(h_hi.sem, h_hi.at(t))
                    dve.tensor_tensor(h2l[:, :, t * P:(t + 1) * P], h2[:, :, :], h2h[:, :, t * P:(t + 1) * P].bitcast(F32),
                                      ALU.subtract).then_inc(h_lo.sem, 1)
            pipelined(dve, split_and_low, norm, last_low)

        @block.tensor
        def _(pe):
            for e in (mix_turned, product, turned):
                e.open(pe)
            ident = con[:, C_ID:C_ID + P]

            def turn_mix(t, u, n):
                pe.wait_ge(mix_in[u].sem, mix_in[u].at(n))
                pe.wait_ge(mix_lo.sem, mix_lo.at(t - 1))
                for k in range(KT):
                    mm = pe.transpose(psT[:, k * P:(k + 1) * P], mix[:, u, k * P:(k + 1) * P], ident)
                mm.then_inc(mix_turned.sem, 1)

            def project(t, u, n):
                pe.wait_ge(mix_lo.sem, mix_lo.at(t))
                pe.wait_ge(branch.sem, branch.at(t - 2))
                for n in range(2):
                    m = 0
                    for k in range(KT):
                        if isinstance(t, int) and t == 0 and n == 0:
                            pe.wait_ge(lo, k + 1)
                        for a, b in ((mh, woh), (ml, woh), (mh, wol)):
                            mm = pe.matmul(psY[u][:, n * 512:(n + 1) * 512], a[:, u, k, :], b[:, k, n * 512:(n + 1) * 512],
                                           start=(m == 0), stop=(m == 3 * KT - 1))
                            m += 1
                mm.then_inc(product.sem, 1)

            def turn_h(t, u, n):
                pe.wait_ge(normed.sem, normed.at(t))
                pe.wait_ge(modulated.sem, modulated.at(t - 1))
                for k in range(KT):
                    mm = pe.transpose(psH[:, k * P:(k + 1) * P], work[:, u, k * P:(k + 1) * P], ident)
                mm.then_inc(turned.sem, 1)

            pipelined(pe, turn_mix, project, turn_h)


def load_ffn_in(sp, S, pair):
    raw = S["wraw"][:, :].rearrange("p (k m n) -> p k m n", k=KT, m=2)
    w_in = S["w_ffn_in"].rearrange("(k p) (two n) -> p k two n", p=P, two=2)
    for m in range(2):
        sp.dma_start(raw[:, :, m, :], w_in[:, :, m, bass.ds(pair * (2 * P), 2 * P)]).then_inc(S["ffn_in"].sem, 16)


def ffn_block(nc, S):
    sb, G2, epsb, h2h, h2l, x2d = (S[n] for n in ("sb", "G2", "epsb", "h2h", "h2l", "x2d"))
    with ExitStack() as s:
        def sem(name):
            return s.enter_context(nc.semaphore("f_" + name))

        def ev(name, per=1, dma=False):
            return Event(nc, s, "f_" + name, per, dma)
        HALF = SEQ // 2
        wih = sb(s, "wih", [P, 2, KT, 2, P], F32R)
        wil = sb(s, "wil", [P, 2, KT, 2, P], F32R)
        raw = S["wraw"][:, :].rearrange("p (k m n) -> p k m n", k=KT, m=2)
        wdh = sb(s, "wdh", [P, 2, D], F32R)
        wdl = sb(s, "wdl", [P, 2, D], F32R)
        draw = sb(s, "fdraw", [P, D])
        ah = sb(s, "ah", [P, 2, SEQ], F32R)
        al = sb(s, "al", [P, 2, SEQ], F32R)
        x_back = S["wraw"][:, :].rearrange("p (t n) -> p t n", n=D)
        act_t = sb(s, "act_t", [P, SEQ])
        down = sb(s, "down", [P, LT, D])
        stats = sb(s, "fstats", [P, LT])
        ps = s.enter_context(nc.psum_tensor("fps", [P, 8, 512], F32))
        flat = ps[:, :, :].rearrange("p b n -> p (b n)")
        psG, psU = flat[:, 0:1024], flat[:, 1024:2048]
        psD = [flat[:, 2048:3072], flat[:, 3072:4096]]
        raw_in, draw_in = S["ffn_in"], ev("draw_in", dma=True)
        in_hi, in_lo, down_hi, down_lo = ev("in_hi"), ev("in_lo"), ev("down_hi"), ev("down_lo")
        product, silu, act_full, act_hi, act_lo = (ev(n, 2) for n in ("product", "silu", "act_full", "act_hi", "act_lo"))
        share, summed = ev("share", LT), ev("summed", LT)
        x_in = [sem(f"x_in{n}") for n in range(4)]
        zeroed, f_stat, f_inv, f_res, f_out = (sem(n) for n in (
            "zeroed", "f_stat", "f_inv", "f_res", "f_out"))
        block = s.enter_context(nc.Block())
        PAIRS = HT // 2

        def cols(n):
            return slice(n * HALF, (n + 1) * HALF)

        @block.sync
        def _(sp):
            def load_down(p):
                for u in range(2):
                    j = p * 2 + u
                    sp.wait_ge(down_lo.sem, down_lo.at(j - 1))
                    sp.dma_start(draw[:, :], S["w_ffn_out"][bass.ds(j * P, P), :]).then_inc(draw_in.sem, 16)

            load_down(0)
            with sp.Fori(0, PAIRS - 1) as i:
                sp.wait_ge(in_lo.sem, in_lo.at(i * 2 + 1))
                load_ffn_in(sp, S, i + 1)
                load_down(i + 1)
            sp.wait_ge(in_lo.sem, in_lo.at(HT - 1))
            for t in range(LT):
                if t >= 4:
                    sp.wait_ge(f_res, t - 3)
                sp.dma_start(x_back[:, t % 4, :], x2d[t * P:(t + 1) * P, :]).then_inc(x_in[t % 4], 16)
            for t in range(LT):
                sp.wait_ge(f_res, t + 1)
                sp.dma_start(S["out"][t * P:(t + 1) * P, :], down[:, t, :]).then_inc(f_out, 16)
            sp.wait_ge(f_out, 16 * LT)

        @block.gpsimd
        def _(pool):
            pool.memset(down[:, :, :], 0.0).then_inc(zeroed, 1)

        @block.scalar
        def _(act):
            for e in (in_hi, down_hi, silu, act_hi):
                e.open(act)

            def split_in(j, slot, pair):
                act.wait_ge(raw_in.sem, raw_in.at(pair))
                act.wait_ge(product.sem, product.at(j - 2))
                act.activation(wih[:, slot, :, :, :], raw[:, :, :, slot * P:(slot + 1) * P], ACT.Copy).then_inc(in_hi.sem, 1)

            def split_down(j, slot, pair):
                act.wait_ge(draw_in.sem, draw_in.at(j))
                act.wait_ge(share.sem, share.at(pair - 1))
                act.activation(wdh[:, slot, :], draw[:, :], ACT.Copy).then_inc(down_hi.sem, 1)

            def gate(j, slot, n):
                act.wait_ge(product.sem, product.at(j, n + 1))
                act.wait_ge(act_lo.sem, act_lo.at(j - 1, n + 1))
                act.activation(act_t[:, cols(n)], psG[:, cols(n)], ACT.Silu).then_inc(silu.sem, 1)

            def high(j, slot, n):
                act.wait_ge(act_full.sem, act_full.at(j, n + 1))
                act.activation(ah[:, slot, cols(n)], act_t[:, cols(n)], ACT.Copy).then_inc(act_hi.sem, 1)

            def body(p, last=False):
                for u in range(2):
                    j = p * 2 + u
                    split_down(j, u, p)
                    gate(j, u, 0)
                    high(j, u, 0)
                    gate(j, u, 1)
                    high(j, u, 1)
                    if not last:
                        split_in(j + 2, u, p + 1)

            split_in(0, 0, 0)
            split_in(1, 1, 0)
            with act.Fori(0, PAIRS - 1) as i:
                body(i)
            body(PAIRS - 1, last=True)
            act.wait_ge(act_lo.sem, act_lo.at(HT - 1))
            for t in range(LT):
                act.wait_ge(summed.sem, summed.at(PAIRS - 1, t + 1))
                if t:
                    act.wait_ge(f_stat, 2 * t)
                act.activation(act_t[:, :], down[:, t, :], ACT.Square, accum_out=stats[:, t:t + 1]).then_inc(f_stat, 1)
                act.wait_ge(f_stat, 2 * t + 1)
                act.activation(stats[:, t:t + 1], stats[:, t:t + 1], ACT.Sqrt, scale=1.0 / D, bias=epsb[:, :]).then_inc(f_stat, 1)

        @block.vector
        def _(dve):
            for e in (in_lo, down_lo, act_full, act_lo, summed):
                e.open(dve)

            def split_in(j, slot):
                dve.wait_ge(in_hi.sem, in_hi.at(j))
                dve.tensor_tensor(wil[:, slot, :, :, :], raw[:, :, :, slot * P:(slot + 1) * P], wih[:, slot, :, :, :].bitcast(F32),
                                  ALU.subtract).then_inc(in_lo.sem, 1)

            def add(p, t):
                dve.wait_ge(share.sem, share.at(p, t + 1))
                dve.wait_ge(summed.sem, summed.at(p - 1, t + 1))
                dve.tensor_tensor(down[:, t, :], down[:, t, :], psD[t % 2], ALU.add).then_inc(summed.sem, 1)

            def activate(j, slot, n):
                dve.wait_ge(silu.sem, silu.at(j, n + 1))
                dve.tensor_tensor(act_t[:, cols(n)], act_t[:, cols(n)], psU[:, cols(n)], ALU.mult).then_inc(act_full.sem, 1)
                dve.wait_ge(act_hi.sem, act_hi.at(j, n + 1))
                dve.tensor_tensor(al[:, slot, cols(n)], act_t[:, cols(n)], ah[:, slot, cols(n)].bitcast(F32), ALU.subtract).then_inc(act_lo.sem, 1)

            def body(p, last=False):
                for u in range(2):
                    j = p * 2 + u
                    dve.wait_ge(down_hi.sem, down_hi.at(j))
                    dve.tensor_tensor(wdl[:, u, :], draw[:, :], wdh[:, u, :].bitcast(F32), ALU.subtract).then_inc(down_lo.sem, 1)
                    for n in range(2):
                        activate(j, u, n)
                    if not last and u == 0:
                        split_in(j + 2, u)
                for t in range(LT):
                    add(p, t)
                    if not last and t == 1:
                        split_in(p * 2 + 3, 1)

            def finish(t):
                dve.wait_ge(f_stat, 2 * t + 2)
                dve.reciprocal(stats[:, t:t + 1], stats[:, t:t + 1]).then_inc(f_inv, 1)
                dve.wait_ge(f_inv, 2 * t + 1)
                dve.scalar_tensor_tensor(down[:, t, :], down[:, t, :], stats[:, t:t + 1], G2[:, :], ALU.mult, ALU.mult).then_inc(f_inv, 1)
                dve.wait_ge(f_inv, 2 * t + 2)
                dve.wait_ge(x_in[t % 4], 16 * (t // 4 + 1))
                dve.tensor_tensor(down[:, t, :], down[:, t, :], x_back[:, t % 4, :], ALU.add).then_inc(f_res, 1)

            split_in(0, 0)
            split_in(1, 1)
            dve.wait_ge(zeroed, 1)
            with dve.Fori(0, PAIRS - 1) as i:
                body(i)
            for u in range(2):
                j = HT - 2 + u
                dve.wait_ge(down_hi.sem, down_hi.at(j))
                dve.tensor_tensor(wdl[:, u, :], draw[:, :], wdh[:, u, :].bitcast(F32), ALU.subtract).then_inc(down_lo.sem, 1)
                for n in range(2):
                    activate(j, u, n)
            for t in range(LT):
                add(PAIRS - 1, t)
                if t:
                    finish(t - 1)
            finish(LT - 1)

        @block.tensor
        def _(pe):
            product.open(pe)
            share.open(pe)

            def gate_up(j, slot):
                pe.wait_ge(in_lo.sem, in_lo.at(j))
                for n in range(2):
                    pe.wait_ge(act_full.sem, act_full.at(j - 1, n + 1))
                    for m, bank in enumerate((psG, psU)):
                        c = 0
                        for k in range(KT):
                            for w, h in ((wih, h2h), (wih, h2l), (wil, h2h)):
                                mm = pe.matmul(bank[:, cols(n)], w[:, slot, k, m, :], h[:, k, cols(n)],
                                               start=(c == 0), stop=(c == 3 * KT - 1))
                                c += 1
                    mm.then_inc(product.sem, 1)

            def down_share(p):
                pe.wait_ge(down_lo.sem, down_lo.at(p * 2 + 1))
                for t in range(LT):
                    if t % 4 == 0:
                        pe.wait_ge(act_lo.sem, act_lo.at(p * 2 + 1, t // 4 + 1))
                    pe.wait_ge(summed.sem, summed.at(p, t - 1) if t >= 2 else summed.at(p - 1, LT - 1 + t))
                    for n in range(2):
                        c = 0
                        for u in range(2):
                            for a, w in ((ah, wdh), (al, wdh), (ah, wdl)):
                                mm = pe.matmul(psD[t % 2][:, n * 512:(n + 1) * 512], a[:, u, t * P:(t + 1) * P],
                                               w[:, u, n * 512:(n + 1) * 512], start=(c == 0), stop=(c == 5))
                                c += 1
                    mm.then_inc(share.sem, 1)

            with pe.Fori(0, PAIRS) as i:
                gate_up(i * 2, 0)
                gate_up(i * 2 + 1, 1)
                down_share(i)


def kernel(**inputs):
    import concourse.bacc as bacc
    from concourse.bass_utils import run_bass_kernel_spmd

    a = {n: np.ascontiguousarray(v) for n, v in inputs.items()}
    consts, cosd, sind = constants()
    arrays = {
        "xall": np.concatenate([a["x"][0], a["ctx"][0]], axis=0), "c": a["c"][0], "c_ctx": a["c_ctx"],
        "w_ada": a["w_ada"][0], "b_ada": a["b_ada"][0], "g_pre_mix": a["g_pre_mix"][0], "g_post_mix": a["g_post_mix"][0],
        "g_pre_ffn": a["g_pre_ffn"][0], "g_post_ffn": a["g_post_ffn"][0], "w_in": a["w_in"][0], "attn_sink": a["attn_sink"][0],
        "w_gate_fwd": a["w_gate_fwd"][0], "b_gate_fwd": a["b_gate_fwd"][0], "w_gate_bwd": a["w_gate_bwd"][0],
        "b_gate_bwd": a["b_gate_bwd"][0], "g_gla": a["g_gla_norm"][0], "w_out": a["w_out"][0],
        "w_ffn_in": a["w_ffn_in"][0], "w_ffn_out": a["w_ffn_out"][0], "consts": consts, "cosd": cosd, "sind": sind,
    }
    nc = bacc.Bacc("TRN2", target_bir_lowering=False, num_devices=1)
    args = {n: nc.dram_tensor(f"in_{n}", v.shape, F32, kind="ExternalInput").ap() for n, v in arrays.items()}
    args["out"] = nc.dram_tensor("out_0", (SEQ, D), F32, kind="ExternalOutput").ap()
    for n, shape in (("proj", (TOK, COLS)), ("mixd", (SEQ, D)), ("x2d", (SEQ, D))):
        args[n] = nc.dram_tensor(f"scratch_{n}", shape, F32, kind=SCRATCH).ap()
    build(nc, **args)
    r = run_bass_kernel_spmd(nc, [{f"in_{n}": v for n, v in arrays.items()}], core_ids=[0])
    return r.results[0]["out_0"].reshape(1, SEQ, D)
```
